# Optimizing a Trainium2 kernel written in Bass

```python
import jax, jax.numpy as jnp
from jax import lax
import numpy as np

D_MODEL = 2048
BATCH = 1
SEQ = 256
DEPTH = 1

N_META = 16
BLOCK_Q = 128
D_MIX = D_MODEL
D_ATTN = D_MIX // 2
D_CONV = D_MIX - D_ATTN
ATTN_HEAD_DIM = 128
N_ATTN_HEADS = D_ATTN // ATTN_HEAD_DIM
CONV_GROUP_DIM = 128
N_CONV_GROUPS = D_CONV // CONV_GROUP_DIM
GROUP_DIM = 128
N_GROUPS = D_MIX // GROUP_DIM
CONV_WIDTH = 3
D_FF = -(-8 * D_MODEL // (3 * 256)) * 256
D_IN = 3 * D_ATTN + 3 * D_CONV + N_ATTN_HEADS
EPS = 1e-6
NEG = -1e30


def rmsnorm(x, g):
    xf = x.astype(jnp.float32)
    y = xf * lax.rsqrt(jnp.mean(xf * xf, axis=-1, keepdims=True) + EPS)
    return (y * g.astype(jnp.float32)).astype(x.dtype)

def short_conv(u, w):
    L = u.shape[1]
    up = jnp.pad(u, ((0, 0), (CONV_WIDTH - 1, 0), (0, 0)))
    y = w[0] * up[:, 0:L]
    for k in range(1, CONV_WIDTH):
        y = y + w[k] * up[:, k:k + L]
    return y

def forgetting_attention(q, k, v, log_f):
    Bsz, L, H, Dh = q.shape
    n_pad = (-L) % BLOCK_Q
    Lp = L + n_pad
    nb = Lp // BLOCK_Q
    pad4 = ((0, 0), (n_pad, 0), (0, 0), (0, 0))
    qp = jnp.pad(q, pad4).transpose(0, 2, 1, 3)
    kp = jnp.pad(k, pad4).transpose(0, 2, 1, 3)
    vp = jnp.pad(v, pad4).transpose(0, 2, 1, 3)
    lf = jnp.pad(log_f.astype(jnp.float32), ((0, 0), (n_pad, 0), (0, 0)))
    c = jnp.cumsum(lf, axis=1).transpose(0, 2, 1)
    key_pos = jnp.arange(Lp)
    key_valid = key_pos >= n_pad
    scale = ATTN_HEAD_DIM ** -0.5
    qb = qp.reshape(Bsz, H, nb, BLOCK_Q, Dh).transpose(2, 0, 1, 3, 4)
    cqb = c.reshape(Bsz, H, nb, BLOCK_Q).transpose(2, 0, 1, 3)

    def block(args):
        qi, cqi, i = args
        s = jnp.einsum('bhqd,bhkd->bhqk', qi, kp,
                       preferred_element_type=jnp.float32) * scale
        s = s + cqi[..., :, None] - c[:, :, None, :]
        qpos = i * BLOCK_Q + jnp.arange(BLOCK_Q)
        mask = (key_pos[None, :] <= qpos[:, None]) & key_valid[None, :]
        s = jnp.where(mask, s, NEG)
        p = jax.nn.softmax(s, axis=-1)
        return jnp.einsum('bhqk,bhkd->bhqd', p.astype(vp.dtype), vp)

    out = lax.map(block, (qb, cqb, jnp.arange(nb)))
    out = out.transpose(1, 0, 3, 2, 4).reshape(Bsz, Lp, H, Dh)
    return out[:, n_pad:]

def hybrid_mixer(h, w_in, b_f, conv_w, out_gain, w_out):
    Bsz, L, _ = h.shape
    z = h @ w_in
    o = 0
    q = z[..., o:o + D_ATTN]; o += D_ATTN
    k = z[..., o:o + D_ATTN]; o += D_ATTN
    v = z[..., o:o + D_ATTN]; o += D_ATTN
    gate_b = z[..., o:o + D_CONV]; o += D_CONV
    gate_c = z[..., o:o + D_CONV]; o += D_CONV
    hc = z[..., o:o + D_CONV]; o += D_CONV
    f_logit = z[..., o:o + N_ATTN_HEADS]
    shp = (Bsz, L, N_ATTN_HEADS, ATTN_HEAD_DIM)
    log_f = jax.nn.log_sigmoid((f_logit + b_f).astype(jnp.float32))
    attn = forgetting_attention(q.reshape(shp), k.reshape(shp), v.reshape(shp), log_f)
    attn = attn.reshape(Bsz, L, D_ATTN)
    conv = gate_b * short_conv(gate_c * hc, conv_w)
    y = jnp.concatenate([attn, conv], axis=-1).reshape(Bsz, L, N_GROUPS, GROUP_DIM)
    y = rmsnorm(y, out_gain.reshape(N_GROUPS, GROUP_DIM)).reshape(Bsz, L, D_MIX)
    return y @ w_out

def swiglu(h, w_gate, w_up, w_down):
    return (jax.nn.silu(h @ w_gate) * (h @ w_up)) @ w_down

def first_inputs(seed: int = 0) -> dict:
    key = jax.random.key(seed)
    ks = jax.random.split(key, 13)
    f32 = jnp.float32
    nrm = lambda k, s, sc: jax.random.normal(k, s, f32) * sc
    x = nrm(ks[0], (BATCH, SEQ, D_MODEL), 1.0)
    meta = nrm(ks[1], (N_META, D_MODEL), 1.0)
    norm_mix = 1.0 + nrm(ks[2], (DEPTH, D_MODEL), 0.02)
    w_in = nrm(ks[3], (DEPTH, D_MODEL, D_IN), D_MODEL ** -0.5)
    b_f = (jnp.linspace(1.0, 6.0, N_ATTN_HEADS, dtype=f32)[None, :]
           + nrm(ks[4], (DEPTH, N_ATTN_HEADS), 0.1))
    conv_w = nrm(ks[5], (DEPTH, CONV_WIDTH, D_CONV), CONV_WIDTH ** -0.5)
    out_gain = 1.0 + nrm(ks[6], (DEPTH, D_MIX), 0.02)
    w_out = nrm(ks[7], (DEPTH, D_MIX, D_MODEL), D_MIX ** -0.5)
    norm_ffn = 1.0 + nrm(ks[8], (DEPTH, D_MODEL), 0.02)
    w_gate = nrm(ks[9], (DEPTH, D_MODEL, D_FF), D_MODEL ** -0.5)
    w_up = nrm(ks[10], (DEPTH, D_MODEL, D_FF), D_MODEL ** -0.5)
    w_down = nrm(ks[11], (DEPTH, D_FF, D_MODEL), D_FF ** -0.5)
    final_norm = 1.0 + nrm(ks[12], (D_MODEL,), 0.02)
    return {"x": x, "meta": meta, "norm_mix": norm_mix, "w_in": w_in, "b_f": b_f,
            "conv_w": conv_w, "out_gain": out_gain, "w_out": w_out,
            "norm_ffn": norm_ffn, "w_gate": w_gate, "w_up": w_up,
            "w_down": w_down, "final_norm": final_norm}

def first_block(x, meta, norm_mix, w_in, b_f, conv_w, out_gain, w_out,
              norm_ffn, w_gate, w_up, w_down, final_norm):
    Bsz = x.shape[0]
    m = jnp.broadcast_to(meta.astype(x.dtype)[None], (Bsz, N_META, D_MODEL))
    h = jnp.concatenate([m, x], axis=1)
    for l in range(DEPTH):
        h = h + hybrid_mixer(rmsnorm(h, norm_mix[l]), w_in[l], b_f[l], conv_w[l],
                             out_gain[l], w_out[l])
        h = h + swiglu(rmsnorm(h, norm_ffn[l]), w_gate[l], w_up[l], w_down[l])
    h = rmsnorm(h, final_norm)
    return h[:, N_META:]


GRID_W = 64
CTX_LEN = 256

MLA_HEADS = 8
MLA_NOPE = 128
MLA_ROPE = 64
MLA_V = 128
MLA_Q_RANK = 512
MLA_KV_RANK = 512
MLA_SCALE = (MLA_NOPE + MLA_ROPE) ** -0.5
ROPE_BASE = 10000.0

NA_HEADS = 4
NA_HEAD_DIM = 128
NA_KH = 8
NA_KW = 16
NA_SCALE = NA_HEAD_DIM ** -0.5

FN_GROUPS = 4
FN_CH = 128

MLA_WIDTH = MLA_HEADS * MLA_V
NA_WIDTH = NA_HEADS * NA_HEAD_DIM
FN_WIDTH = FN_GROUPS * FN_CH
MIX_WIDTH = MLA_WIDTH + NA_WIDTH + FN_WIDTH
IN_SPLITS = (MLA_Q_RANK, MLA_KV_RANK, MLA_ROPE, NA_WIDTH, NA_WIDTH, NA_WIDTH, FN_WIDTH)
IN_COLS = sum(IN_SPLITS)

D_FF_2 = 5632
CONV_W = 3
Q_BLOCK = 128


def rmsnorm_2(x, g):
    xf = x.astype(jnp.float32)
    y = xf * lax.rsqrt(jnp.mean(xf * xf, axis=-1, keepdims=True) + EPS)
    return (y * g.astype(jnp.float32)).astype(x.dtype)

def split_columns(u):
    offs = np.cumsum(IN_SPLITS)[:-1].tolist()
    return jnp.split(u, offs, axis=-1)

def axial_angles(rows, cols):
    n = MLA_ROPE // 4
    freqs = ROPE_BASE ** (-jnp.arange(n, dtype=jnp.float32) / n)
    ang_r = rows.astype(jnp.float32)[:, None, None] * freqs
    ang_c = cols.astype(jnp.float32)[:, None, None] * freqs
    return ang_r, ang_c

def rotate(x, ang):
    n = x.shape[-1] // 2
    x1, x2 = x[..., :n], x[..., n:]
    cos, sin = jnp.cos(ang).astype(x.dtype), jnp.sin(ang).astype(x.dtype)
    return jnp.concatenate([x1 * cos - x2 * sin, x2 * cos + x1 * sin], axis=-1)

def axial_rope(x, ang_r, ang_c):
    h = x.shape[-1] // 2
    return jnp.concatenate([rotate(x[..., :h], ang_r), rotate(x[..., h:], ang_c)], axis=-1)

def mla_qkv(c_q, c_kv, k_r, g_q, w_uq, g_kv, w_ukv, angles):
    B, L, _ = c_q.shape
    q = (rmsnorm_2(c_q, g_q) @ w_uq).reshape(B, L, MLA_HEADS, MLA_NOPE + MLA_ROPE)
    kv = (rmsnorm_2(c_kv, g_kv) @ w_ukv).reshape(B, L, MLA_HEADS, MLA_NOPE + MLA_V)
    q_nope, q_rope = q[..., :MLA_NOPE], q[..., MLA_NOPE:]
    k_nope, v = kv[..., :MLA_NOPE], kv[..., MLA_NOPE:]
    k_rope = k_r[:, :, None, :]
    if angles is not None:
        q_rope = axial_rope(q_rope, *angles)
        k_rope = axial_rope(k_rope, *angles)
    q = jnp.concatenate([q_nope, q_rope], axis=-1)
    k = jnp.concatenate([k_nope, jnp.broadcast_to(k_rope, (B, L, MLA_HEADS, MLA_ROPE))], axis=-1)
    return q, k, v

def blocked_attention(q, k, v, scale):
    B, L, H, dq = q.shape
    dv = v.shape[-1]
    nb = L // Q_BLOCK
    qb = q.reshape(B, nb, Q_BLOCK, H, dq).transpose(1, 0, 2, 3, 4)

    def one_block(qi):
        s = jnp.einsum('bqhd,bkhd->bhqk', qi, k, preferred_element_type=jnp.float32) * scale
        p = jax.nn.softmax(s, axis=-1).astype(v.dtype)
        return jnp.einsum('bhqk,bkhd->bqhd', p, v)

    o = lax.map(one_block, qb)
    return o.transpose(1, 0, 2, 3, 4).reshape(B, L, H * dv)

def neighborhood_attention(q, k, v, k_ctx, v_ctx, rpb):
    B, S, H, d = q.shape
    rows = S // GRID_W
    kh = min(NA_KH, rows)
    qg = q.reshape(B, rows, GRID_W, H, d)
    kg = k.reshape(B, rows, GRID_W, H, d)
    vg = v.reshape(B, rows, GRID_W, H, d)
    w_idx = jnp.arange(GRID_W)
    col_start = jnp.clip(w_idx - NA_KW // 2, 0, GRID_W - NA_KW)
    col_idx = col_start[:, None] + jnp.arange(NA_KW)
    rel_col = col_idx - w_idx[:, None] + (NA_KW - 1)
    nwin = kh * NA_KW

    def one_row(r):
        rs = jnp.clip(r - kh // 2, 0, rows - kh)
        q_r = lax.dynamic_index_in_dim(qg, r, axis=1, keepdims=False)
        k_rows = lax.dynamic_slice_in_dim(kg, rs, kh, axis=1)
        v_rows = lax.dynamic_slice_in_dim(vg, rs, kh, axis=1)
        k_win = k_rows[:, :, col_idx]
        v_win = v_rows[:, :, col_idx]
        rel_row = rs + jnp.arange(kh) - r + (NA_KH - 1)
        bias = rpb[:, rel_row[None, :, None], rel_col[:, None, :]]
        s_win = jnp.einsum('bwhd,bawjhd->bhwaj', q_r, k_win, preferred_element_type=jnp.float32) * NA_SCALE
        s_win = s_win + bias.astype(jnp.float32)
        s_ctx = jnp.einsum('bwhd,bchd->bhwc', q_r, k_ctx, preferred_element_type=jnp.float32) * NA_SCALE
        s = jnp.concatenate([s_win.reshape(B, H, GRID_W, nwin), s_ctx], axis=-1)
        p = jax.nn.softmax(s, axis=-1).astype(v.dtype)
        p_win = p[..., :nwin].reshape(B, H, GRID_W, kh, NA_KW)
        p_ctx = p[..., nwin:]
        return (jnp.einsum('bhwaj,bawjhd->bwhd', p_win, v_win)
                + jnp.einsum('bhwc,bchd->bwhd', p_ctx, v_ctx))

    o = lax.map(one_row, jnp.arange(rows))
    return o.transpose(1, 0, 2, 3, 4).reshape(B, S, H * d)

def fourier_mix(f, w_fnet):
    B, L, _ = f.shape
    fg = f.reshape(B, L, FN_GROUPS, FN_CH).astype(jnp.float32)
    spec = jnp.fft.fft2(fg, axes=(1, 3), norm='ortho').real.astype(f.dtype)
    return jnp.einsum('blgc,gcd->blgd', spec, w_fnet).reshape(B, L, FN_WIDTH)

def conv_ffn(h, w_up, conv_w, conv_b, w_down):
    L = h.shape[1]
    u = h @ w_up
    up = jnp.pad(u, ((0, 0), (CONV_W // 2, CONV_W // 2), (0, 0)))
    u = sum(up[:, j:j + L] * conv_w[j] for j in range(CONV_W)) + conv_b
    gate, val = jnp.split(u, 2, axis=-1)
    return (jax.nn.silu(gate) * val) @ w_down

def heads(t, n_heads):
    B, L, _ = t.shape
    return t.reshape(B, L, n_heads, -1)

def second_inputs(seed: int = 0) -> dict:
    key = jax.random.key(seed)
    ks = jax.random.split(key, 24)
    D = D_MODEL

    def nrm(k, shape, scale):
        return jax.random.normal(k, shape, jnp.float32) * scale

    return {
        'x': nrm(ks[0], (BATCH, SEQ, D), 1.0),
        'c': nrm(ks[1], (BATCH, D), 1.0),
        'ctx': nrm(ks[2], (BATCH, CTX_LEN, D), 1.0),
        'c_ctx': nrm(ks[3], (D,), 1.0),
        'w_mod': nrm(ks[4], (DEPTH, D, 6 * D), D ** -0.5),
        'b_mod': nrm(ks[5], (DEPTH, 6 * D), 0.02),
        'g_attn': 1.0 + nrm(ks[6], (DEPTH, D), 0.02),
        'g_ffn': 1.0 + nrm(ks[7], (DEPTH, D), 0.02),
        'w_in': nrm(ks[8], (DEPTH, D, IN_COLS), D ** -0.5),
        'g_q': 1.0 + nrm(ks[9], (DEPTH, MLA_Q_RANK), 0.02),
        'w_uq': nrm(ks[10], (DEPTH, MLA_Q_RANK, MLA_HEADS * (MLA_NOPE + MLA_ROPE)), MLA_Q_RANK ** -0.5),
        'g_kv': 1.0 + nrm(ks[11], (DEPTH, MLA_KV_RANK), 0.02),
        'w_ukv': nrm(ks[12], (DEPTH, MLA_KV_RANK, MLA_HEADS * (MLA_NOPE + MLA_V)), MLA_KV_RANK ** -0.5),
        'na_rpb': nrm(ks[13], (DEPTH, NA_HEADS, 2 * NA_KH - 1, 2 * NA_KW - 1), 0.1),
        'w_fnet': nrm(ks[14], (DEPTH, FN_GROUPS, FN_CH, FN_CH), FN_CH ** -0.5),
        'w_out': nrm(ks[15], (DEPTH, MIX_WIDTH, D), MIX_WIDTH ** -0.5),
        'w_up': nrm(ks[16], (DEPTH, D, 2 * D_FF_2), D ** -0.5),
        'conv_w': nrm(ks[17], (DEPTH, CONV_W, 2 * D_FF_2), CONV_W ** -0.5),
        'conv_b': nrm(ks[18], (DEPTH, 2 * D_FF_2), 0.02),
        'w_down': nrm(ks[19], (DEPTH, D_FF_2, D), D_FF_2 ** -0.5),
        'g_final': 1.0 + nrm(ks[20], (D,), 0.02),
    }

def second_block(x, c, ctx, c_ctx, w_mod, b_mod, g_attn, g_ffn, w_in, g_q, w_uq, g_kv, w_ukv,
              na_rpb, w_fnet, w_out, w_up, conv_w, conv_b, w_down, g_final):
    S = x.shape[1]
    pos = jnp.arange(S)
    angles = axial_angles(pos // GRID_W, pos % GRID_W)
    xc = ctx
    mod_in = jax.nn.silu(c)
    modc_in = jax.nn.silu(c_ctx)

    for l in range(DEPTH):
        ctx_out = l < DEPTH - 1
        sh1, sc1, gt1, sh2, sc2, gt2 = jnp.split((mod_in @ w_mod[l] + b_mod[l])[:, None, :], 6, axis=-1)
        csh1, csc1, cgt1, csh2, csc2, cgt2 = jnp.split(modc_in @ w_mod[l] + b_mod[l], 6, axis=-1)

        h = rmsnorm_2(x, g_attn[l]) * (1 + sc1) + sh1
        hc = rmsnorm_2(xc, g_attn[l]) * (1 + csc1) + csh1
        cq, ckv, kr, qn, kn, vn, f = split_columns(h @ w_in[l])
        cq_c, ckv_c, kr_c, qn_c, kn_c, vn_c, f_c = split_columns(hc @ w_in[l])

        q_m, k_m, v_m = mla_qkv(cq, ckv, kr, g_q[l], w_uq[l], g_kv[l], w_ukv[l], angles)
        q_mc, k_mc, v_mc = mla_qkv(cq_c, ckv_c, kr_c, g_q[l], w_uq[l], g_kv[l], w_ukv[l], None)
        o_mla = blocked_attention(q_m, jnp.concatenate([k_m, k_mc], axis=1),
                                  jnp.concatenate([v_m, v_mc], axis=1), MLA_SCALE)
        kn_c, vn_c = heads(kn_c, NA_HEADS), heads(vn_c, NA_HEADS)
        o_na = neighborhood_attention(heads(qn, NA_HEADS), heads(kn, NA_HEADS), heads(vn, NA_HEADS),
                                      kn_c, vn_c, na_rpb[l])
        o_fn = fourier_mix(f, w_fnet[l])
        x = x + gt1 * (jnp.concatenate([o_mla, o_na, o_fn], axis=-1) @ w_out[l])

        if ctx_out:
            o_mla_c = blocked_attention(q_mc, k_mc, v_mc, MLA_SCALE)
            o_na_c = blocked_attention(heads(qn_c, NA_HEADS), kn_c, vn_c, NA_SCALE)
            o_fn_c = fourier_mix(f_c, w_fnet[l])
            xc = xc + cgt1 * (jnp.concatenate([o_mla_c, o_na_c, o_fn_c], axis=-1) @ w_out[l])

        h2 = rmsnorm_2(x, g_ffn[l]) * (1 + sc2) + sh2
        x = x + gt2 * conv_ffn(h2, w_up[l], conv_w[l], conv_b[l], w_down[l])
        if ctx_out:
            h2c = rmsnorm_2(xc, g_ffn[l]) * (1 + csc2) + csh2
            xc = xc + cgt2 * conv_ffn(h2c, w_up[l], conv_w[l], conv_b[l], w_down[l])

    return rmsnorm_2(x, g_final)


def setup_inputs(seed=0):
    out = dict(first_inputs(seed))
    for name, value in second_inputs(seed + 1).items():
        if name != "x":
            out[name + "_2"] = value
    return out


def reference(
    x, meta, norm_mix, w_in, b_f, conv_w, out_gain, w_out, norm_ffn, w_gate, w_up, w_down,
    final_norm, c_2, ctx_2, c_ctx_2, w_mod_2, b_mod_2, g_attn_2, g_ffn_2, w_in_2, g_q_2, w_uq_2,
    g_kv_2, w_ukv_2, na_rpb_2, w_fnet_2, w_out_2, w_up_2, conv_w_2, conv_b_2, w_down_2,
    g_final_2,
):
    x = first_block(
        x, meta, norm_mix, w_in, b_f, conv_w, out_gain, w_out, norm_ffn, w_gate, w_up, w_down,
        final_norm,
    )
    return second_block(
        x, c_2, ctx_2, c_ctx_2, w_mod_2, b_mod_2, g_attn_2, g_ffn_2, w_in_2, g_q_2, w_uq_2,
        g_kv_2, w_ukv_2, na_rpb_2, w_fnet_2, w_out_2, w_up_2, conv_w_2, conv_b_2, w_down_2,
        g_final_2,
    )


_drawn_inputs = setup_inputs


def setup_inputs(seed=0):
    import zlib

    import numpy as np

    out = dict(_drawn_inputs(seed))
    spreads = {}
    factors = {'out_gain': 3.505,
     'norm_ffn': 4.808,
     'final_norm': 2.731,
     'g_attn_2': 8.0,
     'g_ffn_2': 4.315,
     'g_q_2': 8.0,
     'g_kv_2': 8.0,
     'na_rpb_2': 8.0,
     'conv_b_2': 4.97,
     'g_final_2': 2.781}
    for name, (base, spread) in spreads.items():
        noise = np.random.default_rng([zlib.crc32(name.encode()), seed]).standard_normal(out[name].shape)
        drawn = base * np.exp(spread * noise) if base else spread * noise
        out[name] = __import__('jax').numpy.asarray(drawn.astype(out[name].dtype))
    for name, factor in factors.items():
        out[name] = (out[name] * factor).astype(out[name].dtype)
    return out
```

```python
from contextlib import ExitStack

import numpy as np

import concourse.bass as bass
from concourse import mybir

F32 = mybir.dt.float32
F32R = mybir.dt.float32r
ALU = mybir.AluOpType
ACT = mybir.ActivationFunctionType
AX_X = mybir.AxisListType.X

P = 128
D = 2048
KT = D // P
NX = 256
NM = 16
N1 = NM + NX
HEADS = 8
F = 5632
FT = F // P
EPS = 1e-6
SCALE1 = 128.0 ** -0.5
MLA_SCALE = 192.0 ** -0.5
NA_SCALE = 128.0 ** -0.5
NA_HEADS = 4
FN_GROUPS = 4
NEG = -1e30
RING = 4
CW = 1024
HW = 256
MOD_TILES = 6 * D // P
MOD_GROUPS = MOD_TILES // 2
CTX_GROUPS = 2 * D // HW


class Layer:

    def __init__(self, name, its, halves, c, tiles=2, mod=0, ctx=False, loop=True):
        self.name, self.its, self.halves, self.c, self.tiles = name, its, halves, c, tiles
        self.mod, self.ctx, self.loop = mod, ctx, loop and its > 1
        self.cpi = halves * c
        self.tpi = halves * tiles


def ffn_layers(tag, mod):
    out = []
    for part, its in (("a", 8), ("b", 8), ("c", 6)):
        out.append(Layer("up" + tag + part, its, 2, 4, mod=2 * mod))
        if part == "c":
            out.append(Layer("dn" + tag + part, 2, 4, 3, mod=mod, loop=tag == "1"))
        else:
            out.append(Layer("dn" + tag + part, 4, 2, 4, mod=2 * mod))
    return out


LAYERS = ([Layer("in1", 12, 2, 4, mod=2, ctx=True), Layer("out1", 4, 2, 4, mod=2, ctx=True)]
          + ffn_layers("1", 1)
          + [Layer("joint", 2, 2, 4), Layer("kr", 1, 1, 2, tiles=1), Layer("xonly", 3, 2, 4),
             Layer("vn", 1, 2, 4, tiles=4), Layer("uk", 1, 4, 1), Layer("uv", 1, 4, 1, tiles=4),
             Layer("uq", 1, 6, 1), Layer("out2", 4, 2, 4)]
          + ffn_layers("2", 0))
_c = _t = _g = 0
for _l in LAYERS:
    _l.base, _l.tbase, _l.gbase = _c, _t, _g
    _c += _l.its * _l.cpi
    _t += _l.its * _l.tpi
    _g += _l.its if _l.mod else 0
N_CHUNKS = _c
assert _g == MOD_GROUPS
LY = {_l.name: _l for _l in LAYERS}

COLS, _o = {}, 0
for _n, _w in (("norm_mix", 16), ("out_gain", 16), ("norm_ffn", 16), ("final_norm", 16), ("g_attn", 16),
               ("g_ffn", 16), ("g_final", 16), ("g_q", 4), ("g_kv", 4), ("c", 16), ("c_ctx", 16),
               ("b_mod", MOD_TILES), ("conv1", 24), ("conv2_w0", 88), ("conv2_w1", 88), ("conv2_w2", 88),
               ("conv2_b", 88), ("b_f", 1), ("eps", 1)):
    COLS[_n] = (_o, _w)
    _o += _w
N_COLS = _o
TABS, _o = {}, 0
for _n, _w in (("ident", P), ("ones", P), ("causal", 2 * N1), ("e31", 31)):
    TABS[_n] = (_o, _w)
    _o += _w
N_TABS1 = _o
_o = TABS["causal"][0]
for _n, _w in (("swap", P), ("cos", NX), ("sin", NX), ("dft_c", 2 * P), ("dft_l_cos", 2 * NX),
               ("dft_l_sin", 2 * NX), ("na_mask", 64)):
    TABS[_n] = (_o, _w)
    _o += _w
N_TABS = _o


def build(nc, tokens, ctx_tokens, cols_d, tables1_d, tables2_d, wf_d, stream, mod_stream, na_bias_d, w_fnet_d, out):
    stack = ExitStack()
    with stack:
        def sem(name):
            return stack.enter_context(nc.semaphore(name))

        top = [nc.sbuf_base if isinstance(nc.sbuf_base, int) else 0]
        limit = nc.sbuf_usable_end if isinstance(nc.sbuf_usable_end, int) else 212863
        start = -(-top[0] // 64) * 64
        top[0] = start

        def at(name, shape, dt, offset):
            size = 4 * int(np.prod(shape[1:]))
            assert offset + size <= limit, (name, offset + size, limit)
            return nc.alloc_sbuf_tensor_at(name, shape, dt, offset=offset)

        def keep(name, shape, dt=F32):
            offset = top[0]
            top[0] += -(-4 * int(np.prod(shape[1:])) // 64) * 64
            return at(name, shape, dt, offset), offset

        raw, _ = keep("raw", [P, RING, CW])
        hi, _ = keep("hi", [P, RING, CW], F32R)
        lo, _ = keep("lo", [P, RING, CW], F32R)
        wm, o_wm = keep("wm", [P, 2, CW])
        acc, o_acc = keep("acc", [P, 2, 2, HW])
        accf, o_accf = keep("accf", [P, 2, HW])
        h, _ = keep("h", [P, KT, N1])
        cols, _ = keep("cols", [P, N_COLS])
        tabs, _ = keep("tabs", [P, N_TABS])
        mod, _ = keep("mod", [P, MOD_TILES])
        modx, _ = keep("modx", [P, 2 * CTX_GROUPS])
        csilu, _ = keep("csilu", [P, 2 * KT])
        gm, _ = keep("gm", [P, 3, KT])
        att, _ = keep("att", [P, 3, 2 * HEADS])
        std, _ = keep("std", [P, 2 * NX])
        rstd, _ = keep("rstd", [P, 2 * NX])
        _, o_work = keep("work_slab", [P, 2, 4, N1])
        sq = at("sq", [P, 2, 4 * N1], F32, o_work)
        xn = at("xn", [P, 2, 4 * N1], F32, o_work)
        tmp = at("tmp", [P, 4, HW], F32, o_work)
        tot = at("tot", [P, 4, HW], F32, o_work + 4096)
        arena = top[0]
        xs1 = at("xs1", [P, KT, 2, N1], F32R, arena)
        ys1 = at("ys1", [P, KT, 2, NX], F32R, arena)
        o = arena + 4 * KT * 2 * N1
        z = at("z", [P, 48, N1], F32, o)
        o += 4 * 48 * N1
        vtok = at("vtok", [P, 3, 1024], F32, o)
        o += 4 * 3 * 1024
        wf = at("wf", [P, KT, HEADS], F32, o)
        o += 4 * KT * HEADS
        fl = at("fl", [P, 3, N1], F32, o)
        p1 = at("p1", [P, 2, 2, N1], F32, o_work)
        pt1 = at("pt1", [P, 3, NX], F32, o_work + 4 * 4 * N1)
        o = arena
        hs = at("hs", [P, KT, 2, NX], F32R, o)
        o += 4 * KT * 2 * NX
        hid = at("hid", [P, KT, 2, NX], F32R, o)
        o += 4 * KT * 2 * NX
        o += 4 * KT * NX
        gt = at("gt", [P, 2, NX], F32, o)
        sg = at("sg", [P, 2, NX], F32, o + 2048)
        ut = at("ut", [P, 2, NX], F32, o + 4096)
        hv = at("hv", [P, 2, NX], F32, o + 6144)
        pad = at("pad", [P, 2, NX + 2], F32, o + 8192)
        cv = at("cv", [P, 2, 3, NX], F32, o + 8192 + 2112)
        o = arena
        hs2 = at("hs2", [P, KT, 2, 2 * NX], F32R, o)
        ysb = at("ysb", [P, 8, 2, NX], F32R, o)
        qn_m = at("qn_m", [P, HEADS, NX], F32, o + 16384)
        qr_m = at("qr_m", [P, 4, NX], F32, o + 24576)
        kn_m = at("kn_m", [P, HEADS, 2 * NX], F32, o + 28672)
        vt_m = at("vt_m", [P, 4, 1024], F32, o + 45056)
        krm = at("krm", [P, 2, 2 * NX], F32, o + 61440)
        o += 65536
        zj = at("zj", [P, 8, 2 * NX], F32, o)
        cx = at("cx", [P, KT, NX], F32, o)
        cqs = at("cqs", [P, 4, 2, NX], F32R, o + 8192)
        o += 16384
        kr = at("kr", [P, 2 * NX], F32, o)
        o += 2048
        zx = at("zx", [P, 12, NX], F32, o)
        ckvs = at("ckvs", [P, 4, 2, 2 * NX], F32R, o + 4096)
        ysa = at("ysa", [P, 8, 2, NX], F32R, o + 4096)
        o += 12288
        vn = at("vn", [P, 4, 512], F32, o)
        na = at("na", [P, NA_HEADS, 2, NX], F32, o_wm)
        pt2 = at("pt2", [P, 4, NX], F32, o_acc)
        wfn = at("wfn", [P, FN_GROUPS, P], F32, o_accf)
        p2 = at("p2", [P, 2, 2, 2 * NX], F32, o_work)
        ab = at("ab", [P, 2, 2, 2 * P], F32, o_work)
        sp = at("sp", [P, 2, NX], F32, o_work + 4096)
        rot = at("rot", [P, 2, 4, NX], F32, o_work)
        ps = stack.enter_context(nc.psum_tensor("ps", [P, 8, 512], F32))

        def col(name, i=0, n=1):
            return cols[:, COLS[name][0] + i:COLS[name][0] + i + n]

        def dcol(name, expr):
            return cols[:, bass.ds(expr + COLS[name][0], 1)]

        def tab(name):
            return tabs[:, TABS[name][0]:TABS[name][0] + TABS[name][1]]

        ident, ones = tab("ident"), tab("ones")
        causal = tab("causal").rearrange("p (a n) -> p a n", a=2)
        dft_lc = tab("dft_l_cos").rearrange("p (a n) -> p a n", a=2)
        dft_ls = tab("dft_l_sin").rearrange("p (a n) -> p a n", a=2)
        hx = h[:, :, NM:N1]

        tokens_in, tables_in, ctx_in, late_in = sem("tokens_in"), sem("tables_in"), sem("ctx_in"), sem("late_in")
        silu_c_done = sem("silu_c_done")
        raw_full = [sem(f"raw_full{s}") for s in range(RING)]
        hi_done = sem("hi_done")
        lo_done = sem("lo_done")
        chunk_used = sem("chunk_used")
        tmp_ready = sem("tmp_ready")
        bank_free = sem("bank_free")
        res_done = sem("res_done")
        wm_full = [sem(f"wm_full{s}") for s in range(2)]
        wm_used = sem("wm_used")
        wm_op = sem("wm_op")
        accf_ready = sem("accf_ready")
        mod_sum = sem("mod_sum")
        mod_done = sem("mod_done")
        gm_done = sem("gm_done")
        sq_ready, sq_used = sem("sq_ready"), sem("sq_used")
        stat_ready, std_ready, rstd_ready = sem("stat_ready"), sem("std_ready"), sem("rstd_ready")
        xn_ready, xs_hi, xs_ready = sem("xn_ready"), sem("xs_hi"), sem("xs_ready")
        f_used = sem("f_used")
        x_final = sem("x_final")
        f_act, f_dve = sem("f_act"), sem("f_dve")
        vt_ready, vtok_ready = sem("vt_ready"), sem("vtok_ready")
        q_scaled = sem("q_scaled")
        s_ready, s_taken, max_ready, exp_ready = sem("s_ready"), sem("s_taken"), sem("max_ready"), sem("exp_ready")
        rsum_ready, p_ready = sem("rsum_ready"), sem("p_ready")
        pt_psum, pt_ready, o_ready, y_ready = sem("pt_psum"), sem("pt_ready"), sem("o_ready"), sem("y_ready")
        conv_step, conv_ready = sem("conv_step"), sem("conv_ready")
        gn_sq, gn_stat, gn_std, gn_r = sem("gn_sq"), sem("gn_stat"), sem("gn_std"), sem("gn_r")
        gn_bc, gn_y, gn_hi, gn_ready = sem("gn_bc"), sem("gn_y"), sem("gn_hi"), sem("gn_ready")
        sg_ready, hv_ready, hid_hi, hid_ready = sem("sg_ready"), sem("hv_ready"), sem("hid_hi"), sem("hid_ready")
        cv_step, pads_zero = sem("cv_step"), sem("pads_zero")
        na_bias_ready = sem("na_bias_ready")
        fn_a, fn_ab, fn_b, fn_sp, fn_c = sem("fn_a"), sem("fn_ab"), sem("fn_b"), sem("fn_sp"), sem("fn_c")
        y2_hi, y2_ready = sem("y2_hi"), sem("y2_ready")
        s2_ready, s2_half, max2_ready, nmax2_ready = sem("s2_ready"), sem("s2_half"), sem("max2_ready"), sem("nmax2_ready")
        s2_bias = sem("s2_bias")
        exp2_ready, rsum2_ready, p2_ready = sem("exp2_ready"), sem("rsum2_ready"), sem("p2_ready")
        pt2_psum, pt2_ready, o2_ready = sem("pt2_psum"), sem("pt2_ready"), sem("o2_ready")
        rot_psum, rot_step, rope_ready, krm_zero = sem("rot_psum"), sem("rot_step"), sem("rope_ready"), sem("krm_zero")
        out_done = sem("out_done")

        NORMS = {}
        nb = ns = 0
        for name, n, batches, tiles in (("mix", N1, 4, 4), ("ffn1", NX, 4, 4), ("ctx", NX, 4, 4), ("final1", NX, 4, 4),
                                        ("attn2", NX, 4, 4), ("kv", 2 * NX, 2, 2), ("q", NX, 1, 4),
                                        ("ffn2", NX, 4, 4), ("final2", NX, 4, 4)):
            NORMS[name] = (ns, nb, n, batches, tiles)
            ns, nb = ns + 1, nb + batches
        SPLIT, n_split = {}, 0
        for name in ("mix", "ffn1", "ctx", "attn2", "kv", "q", "ffn2"):
            SPLIT[name] = n_split
            n_split += NORMS[name][3]
        CONCAT, n_concat = {}, 0
        for ly in LAYERS:
            CONCAT[ly.name] = n_concat
            if ly.name == "out1" or ly.name[:2] in ("up", "dn") or ly.name in ("xonly", "uq", "out2"):
                n_concat += ly.its * ly.tpi
        RES, n_res = {}, 0
        for ly in LAYERS:
            RES[ly.name] = n_res
            if ly.name[:2] == "dn" or ly.name[:3] == "out":
                n_res += ly.its * ly.tpi
        HID, n_hid = {}, 0
        for ly in LAYERS:
            HID[ly.name] = n_hid
            if ly.name[:2] == "up":
                n_hid += ly.its * 2

        def run(eng, ly, body):
            if ly.loop:
                with eng.Fori(0, ly.its) as it:
                    body(it)
            else:
                for it in range(ly.its):
                    body(it)

        def ahead(ly, it, hf, j):
            k = ly.base + RING + hf * ly.c + j
            if not ly.loop and k + it * ly.cpi >= N_CHUNKS:
                return None
            if ly.loop:
                return k + it * ly.cpi, k % RING, k // RING + it * (ly.cpi // RING)
            return k + it * ly.cpi, (k + it * ly.cpi) % RING, (k + it * ly.cpi) // RING

        def last_chunk(ly, it, hf):
            return ly.base + (hf + 1) * ly.c - 1 + it * ly.cpi

        block = stack.enter_context(nc.Block())

        @block.sync
        def _(sp_):
            sp_.dma_start(h[:, :, :], tokens).then_inc(tokens_in, 16)
            sp_.dma_start(cols[:, :], cols_d).then_inc(tables_in, 16)
            sp_.dma_start(tabs[:, 0:N_TABS1], tables1_d).then_inc(tables_in, 16)
            sp_.dma_start(wf[:, :, :], wf_d).then_inc(tables_in, 16)

            def load(v, slot):
                sp_.wait_ge(lo_done, v + 1)
                sp_.dma_start(raw[:, slot, :], stream[bass.ds(v, 1)].rearrange("a p n -> p (a n)"))\
                   .then_inc(raw_full[slot], 16)

            def load_mod(m, slot):
                sp_.wait_ge(wm_used, m + 1)
                sp_.dma_start(wm[:, slot, :], mod_stream[bass.ds(m, 1)].rearrange("a p n -> p (a n)"))\
                   .then_inc(wm_full[slot], 16)

            for v in range(RING):
                load(v, v)
            for ly in LAYERS:
                def body(it, ly=ly):
                    for hf in range(ly.halves):
                        for j in range(ly.c):
                            a = ahead(ly, it, hf, j)
                            if a is not None:
                                load(a[0], a[1])
                            if j < ly.mod:
                                m = hf * ly.mod + j
                                load_mod((ly.gbase * 4 + m) + it * 4, m % 2)
                run(sp_, ly, body)
                if ly.name == "out1":
                    sp_.wait_ge(gn_ready, 4)
                    sp_.dma_start(cx[:, :, :], ctx_tokens).then_inc(ctx_in, 16)
                    sp_.dma_start(tabs[:, TABS["swap"][0]:N_TABS], tables2_d).then_inc(late_in, 16)
                if ly.name == "dn1c":
                    sp_.wait_ge(wm_used, 4 * MOD_GROUPS + 2)
                    sp_.wait_ge(mod_sum, MOD_GROUPS + 1)
                    sp_.dma_start(na[:, :, :, :], na_bias_d).then_inc(late_in, 16)
                    sp_.dma_start(wfn[:, :, :], w_fnet_d).then_inc(late_in, 16)
            sp_.wait_ge(x_final, 2 * KT)
            sp_.dma_start(out, hx).then_inc(out_done, 16)
            sp_.wait_ge(out_done, 16)

        @block.scalar
        def _(act):
            def split_hi(v, slot, turn):
                act.wait_ge(raw_full[slot], 16 * (turn + 1))
                act.wait_ge(chunk_used, v + 1)
                act.activation(hi[:, slot, :], raw[:, slot, :], ACT.Copy).then_inc(hi_done, 1)

            def prepare(ly, it, hf):
                for j in range(ly.c):
                    a = ahead(ly, it, hf, j)
                    if a is not None:
                        split_hi(*a)

            def second_halves(ly, it, hf):
                act.wait_ge(chunk_used, last_chunk(ly, it, hf) + 5)
                for t in range(2):
                    bank = (2 * hf + t) % 4
                    n = CONCAT[ly.name] + it * ly.tpi + 2 * hf + t
                    if not ly.loop and n >= 4 or ly.loop and CONCAT[ly.name] >= 4:
                        pass
                    act.activation(tmp[:, bank, :], ps[:, bank, NX:2 * NX], ACT.Copy).then_inc(tmp_ready, 1)

            def norm_squares(name, src, ready):
                k, b0, n, batches, tiles = NORMS[name]
                for s, v in ready:
                    act.wait_ge(s, v)
                for b in range(batches):
                    if b >= 2:
                        act.wait_ge(sq_used, b0 - k + b - 1)
                    act.activation(sq[:, b % 2, 0:tiles * n].rearrange("p (k n) -> p k n", k=tiles), src(b),
                                   ACT.Square).then_inc(sq_ready, 1)
                act.wait_ge(stat_ready, k + 1)
                if k >= 1:
                    act.wait_ge(rstd_ready, k)
                act.activation(std[:, 0:n], ps[:, 4, 0:n], ACT.Sqrt, bias=col("eps"),
                               scale=1.0 / (batches * tiles * P)).then_inc(std_ready, 1)

            def norm_hi(name, dst, shift=None):
                _, _, n, batches, tiles = NORMS[name]
                for b in range(batches):
                    act.wait_ge(xn_ready, SPLIT[name] + b + 1)
                    src = xn[:, b % 2, 0:tiles * n].rearrange("p (k n) -> p k n", k=tiles)
                    if shift is None:
                        act.activation(dst(b), src, ACT.Copy).then_inc(xs_hi, 1)
                    else:
                        for k in range(tiles):
                            ins = act.activation(dst(b)[:, k, :], src[:, k, :], ACT.Identity,
                                                 bias=shift(b * tiles + k))
                        ins.then_inc(xs_hi, 1)

            act.wait_ge(tables_in, 48)
            act.activation(csilu[:, :], cols[:, COLS["c"][0]:COLS["c"][0] + 2 * KT], ACT.Silu).then_inc(silu_c_done, 1)
            norm_squares("mix", lambda b: h[:, 4 * b:4 * b + 4, :], [(tokens_in, 16)])
            for v in range(RING):
                split_hi(v, v, 0)
            norm_hi("mix", lambda b: xs1[:, 4 * b:4 * b + 4, 0, :])

            ly = LY["in1"]

            def body(it, ly=ly):
                for hf in range(2):
                    prepare(ly, it, hf)
                    act.wait_ge(chunk_used, last_chunk(ly, it, hf) + 5)
                    for t in range(2):
                        act.activation(z[:, bass.ds(it * 4 + 2 * hf + t, 1), :].rearrange("p a n -> p (a n)"),
                                       ps[:, 2 * hf + t, 0:N1], ACT.Copy).then_inc(bank_free, 1)
            run(act, ly, body)
            act.wait_ge(bank_free, 48 + 4)

            act.activation(z[:, 0:HEADS, NM:N1], z[:, 0:HEADS, NM:N1], ACT.Copy, scale=SCALE1).then_inc(q_scaled, 1)
            act.wait_ge(f_dve, 1)
            act.activation(fl[0:HEADS, 1, :], fl[0:HEADS, 0, :], ACT.Abs).then_inc(f_act, 1)
            act.wait_ge(f_act, 1)
            act.activation(fl[0:HEADS, 2, :], fl[0:HEADS, 1, :], ACT.Exp, scale=-1.0).then_inc(f_act, 1)
            act.wait_ge(f_act, 2)
            act.activation(fl[0:HEADS, 1, :], fl[0:HEADS, 2, :], ACT.Ln, bias=1.0).then_inc(f_act, 1)
            for i, bank in enumerate((0, 1, 2, 3, 6, 7)):
                rows = P if i < 4 else N1 - 2 * P
                act.wait_ge(vt_ready, i + 1)
                act.activation(vtok[0:rows, i // 2, 512 * (i % 2):512 * (i % 2) + 512], ps[0:rows, bank, :],
                               ACT.Copy).then_inc(vtok_ready, 1)

            def exps(hd):
                for qt in range(2):
                    u = 2 * hd + qt
                    act.wait_ge(max_ready, u + 1)
                    act.activation(p1[:, hd % 2, qt, :], p1[:, hd % 2, qt, :], ACT.Exp, bias=att[:, 0, u:u + 1],
                                   accum_out=att[:, 1, u:u + 1]).then_inc(exp_ready, 1)

            def take_y(hd):
                act.wait_ge(pt_psum, hd + 1)
                if hd >= 1:
                    act.wait_ge(o_ready, hd)
                act.activation(pt1[:, 0:2, :], ps[:, 6, :].rearrange("p (k n) -> p k n", k=2), ACT.Copy)
                act.activation(pt1[0:NM, 2, :], ps[0:NM, 7, 0:NX], ACT.Copy).then_inc(pt_ready, 1)
                act.wait_ge(o_ready, hd + 1)
                act.activation(z[:, hd, NM:N1], ps[:, hd % 2, 0:NX], ACT.Copy).then_inc(y_ready, 1)

            for hd in range(HEADS):
                exps(hd)
                if hd >= 1:
                    take_y(hd - 1)
            take_y(HEADS - 1)
            act.wait_ge(y_ready, HEADS)
            for b in range(4):
                if b == 2:
                    act.wait_ge(conv_ready, 8)
                if b >= 2:
                    act.wait_ge(gn_stat, 4 * (b - 1))
                t0 = 4 * b if b < 2 else 24 + 4 * (b - 2)
                act.activation(sq[:, b % 2, 0:4 * NX].rearrange("p (k n) -> p k n", k=4), z[:, t0:t0 + 4, NM:N1],
                               ACT.Square).then_inc(gn_sq, 1)
            act.wait_ge(gn_stat, 16)
            act.activation(std[0:16, 0:NX], ps[0:16, 2, 0:NX], ACT.Sqrt, bias=cols[0:16, COLS["eps"][0]:COLS["eps"][0] + 1],
                           scale=1.0 / P).then_inc(gn_std, 1)
            for b in range(4):
                act.wait_ge(gn_y, 4 * b + 4)
                act.activation(ys1[:, 4 * b:4 * b + 4, 0, :], xn[:, b % 2, 0:4 * NX].rearrange("p (k n) -> p k n", k=4),
                               ACT.Copy).then_inc(gn_hi, 1)

            def residual(ly):
                def body(it):
                    for hf in range(ly.halves):
                        prepare(ly, it, hf)
                        second_halves(ly, it, hf)
                run(act, ly, body)

            def gated(ly, gate_src, gate_step):
                def body(it):
                    prepare(ly, it, 0)
                    second_halves(ly, it, 0)
                    prepare(ly, it, 1)
                    for t in range(2):
                        act.wait_ge(*gate_step(it, t))
                        act.activation(sg[:, t, :], gate_src(t), ACT.Silu).then_inc(sg_ready, 1)
                    second_halves(ly, it, 1)
                    for t in range(2):
                        n = HID[ly.name] + it * 2 + t
                        act.wait_ge(hv_ready, n + 1)
                        act.activation(hid[:, bass.ds(it * 2 + t, 1), 0, :].rearrange("p a n -> p (a n)"), hv[:, t, :],
                                       ACT.Copy).then_inc(hid_hi, 1)
                run(act, ly, body)

            residual(LY["out1"])
            norm_squares("ffn1", lambda b: hx[:, 4 * b:4 * b + 4, :], [(res_done, RES["out1"] + KT)])
            norm_hi("ffn1", lambda b: hs[:, 4 * b:4 * b + 4, 0, :])
            for part in "abc":
                ly = LY["up1" + part]
                gated(ly, lambda t: gt[:, t, :], lambda it, t, ly=ly: (bank_free, ly.tbase + it * 4 + t + 5))
                residual(LY["dn1" + part])

            norm_squares("ctx", lambda b: cx[:, 4 * b:4 * b + 4, :],
                         [(ctx_in, 16), (res_done, RES["dn1c"] + KT)])
            act.wait_ge(mod_done, MOD_GROUPS + 1)
            norm_hi("ctx", lambda b: hs2[:, 4 * b:4 * b + 4, 0, NX:2 * NX], lambda k: modx[:, k:k + 1])
            norm_squares("final1", lambda b: hx[:, 4 * b:4 * b + 4, :], [(xs_ready, SPLIT["ctx"] + 4)])
            norm_squares("attn2", lambda b: hx[:, 4 * b:4 * b + 4, :], [(x_final, KT)])
            norm_hi("attn2", lambda b: hs2[:, 4 * b:4 * b + 4, 0, 0:NX], lambda k: mod[:, k:k + 1])

            def plain(ly):
                def body(it):
                    for hf in range(ly.halves):
                        prepare(ly, it, hf)
                run(act, ly, body)

            plain(LY["joint"])
            plain(LY["kr"])
            residual(LY["xonly"])
            plain(LY["vn"])

            for g in range(FN_GROUPS):
                act.wait_ge(fn_a, g + 1)
                act.activation(ab[:, g % 2, :, :], ps[:, 4:6, 0:2 * P], ACT.Copy).then_inc(fn_ab, 1)
                act.wait_ge(fn_c, g + 1)
                act.activation(ysb[:, 4 + g, 0, :], ps[:, 7, 0:NX], ACT.Copy).then_inc(y2_hi, 1)
            norm_squares("kv", lambda b: zj[:, 2 * b:2 * b + 2, :], [(bank_free, LY["kr"].tbase + 4)])
            norm_squares("q", lambda b: zx[:, 0:4, :], [(bank_free, LY["vn"].tbase + 4)])

            def attend(first, heads, scale, local):
                def exps2(hd):
                    for qt in range(2):
                        u = 2 * (first + hd) + qt
                        if local:
                            act.wait_ge(s2_ready, u + 1)
                            act.activation(p2[:, hd % 2, qt, NX:2 * NX], ps[:, 4 + qt, NX:2 * NX], ACT.Copy,
                                           scale=scale).then_inc(s2_half, 1)
                    for qt in range(2):
                        u = 2 * (first + hd) + qt
                        act.wait_ge(nmax2_ready, u + 1)
                        src = p2[:, hd % 2, qt, :] if local else ps[:, 4 + qt, :]
                        act.activation(p2[:, hd % 2, qt, :], src, ACT.Exp, bias=att[:, 0, u % 16:u % 16 + 1],
                                       scale=1.0 if local else scale,
                                       accum_out=att[:, 1, u % 16:u % 16 + 1]).then_inc(exp2_ready, 1)

                def take(hd):
                    n = first + hd
                    act.wait_ge(pt2_psum, n + 1)
                    if n >= 1:
                        act.wait_ge(o2_ready, n)
                    for qt in range(2):
                        ins = act.activation(pt2[:, :, qt * P:qt * P + P],
                                             ps[:, 6 + qt, :].rearrange("p (k n) -> p k n", k=4), ACT.Copy)
                    ins.then_inc(pt2_ready, 1)
                    act.wait_ge(o2_ready, n + 1)
                    y = ysb[:, hd, 0, :] if local else ysa[:, hd, 0, :]
                    act.activation(y, ps[:, hd % 2, 0:NX], ACT.Copy).then_inc(y2_hi, 1)

                for hd in range(heads):
                    exps2(hd)
                    if hd >= 1:
                        take(hd - 1)
                take(heads - 1)

            attend(0, NA_HEADS, NA_SCALE, True)
            norm_hi("kv", lambda b: ckvs[:, 2 * b:2 * b + 2, 0, :])
            norm_hi("q", lambda b: cqs[:, :, 0, :])
            plain(LY["uk"])
            plain(LY["uv"])
            residual(LY["uq"])
            attend(NA_HEADS, HEADS, MLA_SCALE, False)

            residual(LY["out2"])
            norm_squares("ffn2", lambda b: hx[:, 4 * b:4 * b + 4, :], [(res_done, RES["out2"] + KT)])
            norm_hi("ffn2", lambda b: hs[:, 4 * b:4 * b + 4, 0, :], lambda k: mod[:, 48 + k:49 + k])
            for part in "abc":
                ly = LY["up2" + part]
                gated(ly, lambda t: cv[:, t, 2, :],
                      lambda it, t, ly=ly: (cv_step, (HID[ly.name] - HID["up2a"]) * 6 + it * 12 + 5 + t))
                residual(LY["dn2" + part])
            norm_squares("final2", lambda b: hx[:, 4 * b:4 * b + 4, :], [(res_done, RES["dn2c"] + KT)])

        @block.tensor
        def _(pe):
            def weights(ly, it, hf, j):
                k = ly.base + hf * ly.c + j
                pe.wait_ge(lo_done, k + 5 + it * ly.cpi)
                return k % RING if ly.loop else (k + it * ly.cpi) % RING

            def wide(ly, it, hf, xs, x_ready=None, width=HW):
                kk = CW // width
                last_k = ly.c * kk - 1
                for j in range(ly.c):
                    slot = weights(ly, it, hf, j)
                    if x_ready is not None:
                        pe.wait_ge(*x_ready(j))
                    for t in range(ly.tiles):
                        bank = (2 * hf + t) % 4
                        if j == 0:
                            pe.wait_ge(bank_free, ly.tbase + 2 * hf + t + 1 + it * ly.tpi)
                        both = ps[:, bank, :].rearrange("p (a n) -> p a n", a=2)
                        for k in range(kk):
                            kt = j * kk + k
                            w = slice(k * width + t * P, k * width + t * P + P)
                            pair, x_hi = xs(kt)
                            if kt == last_k:
                                pe.matmul(ps[:, bank, 0:NX], lo[:, slot, w], x_hi, start=False, stop=False)
                            ins = pe.matmul(both, hi[:, slot, w], pair, start=kt == 0, stop=kt == last_k)
                            if kt != last_k:
                                ins = pe.matmul(ps[:, bank, 0:NX], lo[:, slot, w], x_hi, start=False, stop=False)
                    ins.then_inc(chunk_used, 1)

            def triple(ly, it, hf, n, xs, x_ready=None, width=HW):
                kk = CW // width
                last_k = ly.c * kk - 1
                for j in range(ly.c):
                    slot = weights(ly, it, hf, j)
                    if x_ready is not None:
                        pe.wait_ge(*x_ready(j))
                    for t in range(ly.tiles):
                        bank = (2 * hf + t) % 4
                        if j == 0:
                            pe.wait_ge(bank_free, ly.tbase + 2 * hf + t + 1 + it * ly.tpi)
                        for k in range(kk):
                            kt = j * kk + k
                            w = slice(k * width + t * P, k * width + t * P + P)
                            x_hi, x_lo = xs(kt)
                            acc_ = ps[:, bank, 0:n]
                            pe.matmul(acc_, hi[:, slot, w], x_hi, start=kt == 0, stop=False)
                            pe.matmul(acc_, hi[:, slot, w], x_lo, start=False, stop=False)
                            ins = pe.matmul(acc_, lo[:, slot, w], x_hi, start=False, stop=kt == last_k)
                    ins.then_inc(chunk_used, 1)

            def by_token(ly, hf, xs):
                banks = range(4 * (hf % 2), 4 * (hf % 2) + 4)
                if hf >= 2:
                    pe.wait_ge(bank_free, ly.tbase + 4 * (hf - 1) + 4)
                for j in range(ly.c):
                    slot = weights(ly, 0, hf, j)
                    for t, bank in enumerate(banks):
                        for k in range(4):
                            kt = 4 * j + k
                            w = slice(k * HW, k * HW + HW)
                            x_hi, x_lo = xs(kt, t)
                            acc_ = ps[:, bank, 0:HW]
                            pe.matmul(acc_, x_hi, hi[:, slot, w], start=kt == 0, stop=False)
                            pe.matmul(acc_, x_lo, hi[:, slot, w], start=False, stop=False)
                            ins = pe.matmul(acc_, x_hi, lo[:, slot, w], start=False, stop=kt == 4 * ly.c - 1)
                    ins.then_inc(chunk_used, 1)

            def mod_group(ly, it):
                g = ly.gbase + it
                pe.wait_ge(accf_ready, g + 1)
                pe.wait_ge(mod_done, g + 1)
                for v in range(2 if ly.ctx else 1):
                    for t in range(2):
                        ins = pe.matmul(ps[:, 7, 2 * v + t:2 * v + t + 1], accf[:, v, t * P:t * P + P], ones[:, 0:1],
                                        start=True, stop=True)
                ins.then_inc(mod_sum, 1)

            def norm_stats(name):
                k, b0, n, batches, tiles = NORMS[name]
                if k >= 1:
                    pe.wait_ge(std_ready, k)
                for b in range(batches):
                    pe.wait_ge(sq_ready, b0 + b + 1)
                    for t in range(tiles):
                        ins = pe.matmul(ps[:, 4, 0:n], ones, sq[:, b % 2, t * n:t * n + n],
                                        start=b == 0 and t == 0, stop=b == batches - 1 and t == tiles - 1)
                    if b < batches - 1:
                        ins.then_inc(sq_used, 1)
                ins.then_inc(stat_ready, 1)

            pe.wait_ge(tables_in, 48)
            norm_stats("mix")
            for b in range(4):
                pe.wait_ge(xn_ready, b + 1)
                for k in range(4):
                    ins = pe.matmul(ps[0:HEADS, 5, 0:N1], wf[:, 4 * b + k, :], xn[:, b % 2, k * N1:k * N1 + N1],
                                    start=b == 0 and k == 0, stop=b == 3 and k == 3)
                ins.then_inc(f_used, 1)

            ly = LY["in1"]

            def body(it, ly=ly):
                for hf in range(2):
                    triple(ly, it, hf, N1, lambda kt: (xs1[:, kt, 0, :], xs1[:, kt, 1, :]),
                           (lambda j: (xs_ready, j + 1)) if hf == 0 else None)
                mod_group(ly, it)
            run(pe, ly, body)

            pe.wait_ge(bank_free, LY["in1"].its * 4 + 4)
            pe.wait_ge(mod_done, 12 + 1)
            for kt in range(3):
                rows = P if kt < 2 else N1 - 2 * P
                for g in range(2):
                    bank = 2 * kt + g if kt < 2 else 6 + g
                    for k in range(4):
                        ins = pe.transpose(ps[0:rows, bank, k * P:k * P + P],
                                           z[:, 16 + 4 * g + k, kt * P:kt * P + rows], ident)
                    ins.then_inc(vt_ready, 1)

            pe.wait_ge(q_scaled, 1)
            pe.wait_ge(f_dve, 5)

            def scores(hd):
                pick = ident[0:HEADS, hd:hd + 1]
                for qt in range(2):
                    q0 = NM + qt * P
                    if hd >= 1:
                        pe.wait_ge(s_taken, 2 * (hd - 1) + qt + 1)
                    s = ps[:, 4 + qt, 0:N1]
                    pe.matmul(s, z[:, hd, q0:q0 + P], z[:, 8 + hd, :], start=True, stop=False)
                    pe.matmul(s, fl[0:HEADS, 0, q0:q0 + P], pick.to_broadcast([HEADS, N1]), start=False, stop=False)
                    pe.matmul(s, pick.to_broadcast([HEADS, P]), fl[0:HEADS, 2, :], start=False, stop=True)\
                      .then_inc(s_ready, 1)

            def mix(hd):
                pe.wait_ge(p_ready, 2 * hd + 2)
                if hd == 0:
                    pe.wait_ge(vtok_ready, 6)
                else:
                    pe.wait_ge(pt_ready, hd)
                for qt in range(2):
                    for kt in range(2):
                        pe.transpose(ps[:, 6, kt * NX + qt * P:kt * NX + qt * P + P],
                                     p1[:, hd % 2, qt, kt * P:kt * P + P], ident)
                    ins = pe.transpose(ps[0:NM, 7, qt * P:qt * P + P], p1[:, hd % 2, qt, 2 * P:N1], ident)
                ins.then_inc(pt_psum, 1)
                pe.wait_ge(pt_ready, hd + 1)
                if hd >= 2:
                    pe.wait_ge(y_ready, hd - 1)
                for kt in range(3):
                    rows = P if kt < 2 else N1 - 2 * P
                    ins = pe.matmul(ps[:, hd % 2, 0:NX], vtok[0:rows, kt, hd * P:hd * P + P], pt1[0:rows, kt, :],
                                    start=kt == 0, stop=kt == 2)
                ins.then_inc(o_ready, 1)

            for hd in range(HEADS):
                scores(hd)
                if hd >= 1:
                    mix(hd - 1)
            mix(HEADS - 1)
            for g in range(16):
                if g % 4 == 0:
                    pe.wait_ge(gn_sq, g // 4 + 1)
                e0 = TABS["e31"][0] + 15 - g
                pe.matmul(ps[0:16, 2, 0:NX], tabs[:, e0:e0 + 16], sq[:, (g // 4) % 2, (g % 4) * NX:(g % 4) * NX + NX],
                          start=g == 0, stop=g == 15).then_inc(gn_stat, 1)
            pe.wait_ge(gn_r, 1)
            for g in range(16):
                if g == 0:
                    pe.wait_ge(y_ready, HEADS)
                if g >= 2:
                    pe.wait_ge(gn_y, g - 1)
                pe.matmul(ps[:, g % 2, 0:NX], ident[0:16, g:g + 1].to_broadcast([16, P]), rstd[0:16, 0:NX],
                          start=True, stop=True).then_inc(gn_bc, 1)

            def project(ly, xs, x_ready=None, mods=True):
                def body(it):
                    for hf in range(ly.halves):
                        wide(ly, it, hf, xs, x_ready if hf == 0 else None)
                    if ly.mod and mods:
                        mod_group(ly, it)
                run(pe, ly, body)

            def pair_of(x):
                return lambda kt: (x[:, kt, :, :], x[:, kt, 0, :])

            pe.wait_ge(gn_y, 16)
            project(LY["out1"], pair_of(ys1), lambda j: (gn_ready, j + 1))
            norm_stats("ffn1")

            def feed_forward(tag, first_batch):
                for part in "abc":
                    up, dn = LY["up" + tag + part], LY["dn" + tag + part]
                    project(up, pair_of(hs), lambda j: (xs_ready, first_batch + j + 1))
                    project(dn, pair_of(hid), lambda j, up=up: (hid_ready, HID[up.name] + 4 * j + 4))

            feed_forward("1", SPLIT["ffn1"])

            norm_stats("ctx")
            norm_stats("final1")
            norm_stats("attn2")
            ly = LY["joint"]
            pe.wait_ge(bank_free, ly.tbase + 4)
            pe.wait_ge(xs_ready, SPLIT["ctx"] + 4)

            def both_of(kt):
                return hs2[:, kt, 0, :], hs2[:, kt, 1, :]

            def body(it, ly=ly):
                for hf in range(2):
                    triple(ly, it, hf, 2 * NX, both_of, lambda j: (xs_ready, SPLIT["attn2"] + j + 1))
            run(pe, ly, body)
            triple(LY["kr"], 0, 0, 2 * NX, both_of, width=P)
            pe.wait_ge(bank_free, LY["xonly"].tbase + 4)
            project(LY["xonly"], lambda kt: (hs2[:, kt, :, 0:NX], hs2[:, kt, 0, 0:NX]))
            pe.wait_ge(bank_free, LY["vn"].tbase + 4)
            for hf in range(2):
                by_token(LY["vn"], hf, lambda kt, t: (hs2[:, kt, 0, t * P:t * P + P], hs2[:, kt, 1, t * P:t * P + P]))
            pe.wait_ge(late_in, 48)
            pe.wait_ge(bank_free, LY["uk"].tbase + 4)

            def fourier_features(g):
                if g >= 1:
                    pe.wait_ge(fn_ab, g)
                for lt in range(2):
                    ins = pe.matmul(ps[:, 4 + lt, 0:2 * P], zx[:, 8 + g, lt * P:lt * P + P], tab("dft_c"),
                                    start=True, stop=True)
                ins.then_inc(fn_a, 1)

            fourier_features(0)
            for g in range(FN_GROUPS):
                if g + 1 < FN_GROUPS:
                    fourier_features(g + 1)
                pe.wait_ge(fn_ab, g + 1)
                if g >= 1:
                    pe.wait_ge(fn_sp, g)
                n = 0
                for part, table in ((0, dft_lc), (1, dft_ls)):
                    for lt in range(2):
                        ins = pe.matmul(ps[:, 6, 0:NX], ab[:, g % 2, lt, part * P:part * P + P], table[:, lt, :],
                                        start=n == 0, stop=n == 3)
                        n += 1
                ins.then_inc(fn_b, 1)
                pe.wait_ge(fn_sp, g + 1)
                if g >= 1:
                    pe.wait_ge(y2_ready, g)
                pe.matmul(ps[:, 7, 0:NX], wfn[:, g, :], sp[:, g % 2, :], start=True, stop=True).then_inc(fn_c, 1)

            norm_stats("kv")
            norm_stats("q")

            def attend(first, heads, score_terms, values, y0):
                def scores2(hd):
                    for qt in range(2):
                        u = 2 * (first + hd) + qt
                        if hd >= 1:
                            pe.wait_ge(exp2_ready, u - 1)
                        terms = score_terms(hd, qt)
                        for i, (q, k) in enumerate(terms):
                            ins = pe.matmul(ps[:, 4 + qt, :], q, k, start=i == 0, stop=i == len(terms) - 1)
                        ins.then_inc(s2_ready, 1)

                def mix2(hd):
                    n = first + hd
                    pe.wait_ge(p2_ready, 2 * n + 2)
                    if n >= 1:
                        pe.wait_ge(pt2_ready, n)
                    for qt in range(2):
                        for kt in range(4):
                            ins = pe.transpose(ps[:, 6 + qt, kt * P:kt * P + P],
                                               p2[:, hd % 2, qt, kt * P:kt * P + P], ident)
                    ins.then_inc(pt2_psum, 1)
                    pe.wait_ge(pt2_ready, n + 1)
                    if hd >= 2:
                        pe.wait_ge(y2_ready, y0 + hd - 1)
                    for kt in range(4):
                        ins = pe.matmul(ps[:, hd % 2, 0:NX], values[:, kt, hd * P:hd * P + P], pt2[:, kt, :],
                                        start=kt == 0, stop=kt == 3)
                    ins.then_inc(o2_ready, 1)

                for hd in range(heads):
                    scores2(hd)
                    if hd >= 1:
                        mix2(hd - 1)
                mix2(heads - 1)

            pe.wait_ge(std_ready, NORMS["q"][0] + 1)
            pe.wait_ge(y2_ready, FN_GROUPS)
            attend(0, NA_HEADS, lambda hd, qt: [(zx[:, 4 + hd, qt * P:qt * P + P], zj[:, 4 + hd, :])], vn, FN_GROUPS)
            pe.wait_ge(y2_ready, FN_GROUPS + NA_HEADS)
            for hf in range(4):
                triple(LY["uk"], 0, hf, 2 * NX, lambda kt: (ckvs[:, kt, 0, :], ckvs[:, kt, 1, :]),
                       lambda j: (xs_ready, SPLIT["kv"] + 2))
            pe.wait_ge(bank_free, LY["uv"].tbase + 4)
            for hf in range(4):
                by_token(LY["uv"], hf, lambda kt, t: (ckvs[:, kt, 0, t * P:t * P + P], ckvs[:, kt, 1, t * P:t * P + P]))
            pe.wait_ge(bank_free, LY["uq"].tbase + 4)
            project(LY["uq"], pair_of(cqs), lambda j: (xs_ready, SPLIT["q"] + 1))
            pe.wait_ge(bank_free, LY["out2"].tbase + 4)
            for j in range(4):
                pe.matmul(ps[:, 4 + j // 2, (j % 2) * NX:(j % 2) * NX + NX], tab("swap"), qr_m[:, j, :],
                          start=True, stop=True)
            pe.matmul(ps[:, 6, 0:NX], tab("swap"), kr[:, 0:NX], start=True, stop=True).then_inc(rot_psum, 1)
            pe.wait_ge(rope_ready, 6)
            attend(NA_HEADS, HEADS,
                   lambda hd, qt: [(qn_m[:, hd, qt * P:qt * P + P], kn_m[:, hd, :]),
                                   (qr_m[:, hd // 2, qt * P:qt * P + P], krm[:, hd % 2, :])],
                   vt_m, FN_GROUPS + NA_HEADS)
            pe.wait_ge(y2_ready, FN_GROUPS + NA_HEADS + HEADS)

            def mixed(kt):
                y = ysa[:, kt] if kt < 8 else ysb[:, kt - 8]
                return y[:, :, :], y[:, 0, :]

            project(LY["out2"], mixed)
            norm_stats("ffn2")
            feed_forward("2", SPLIT["ffn2"])
            norm_stats("final2")

        @block.vector
        def _(dve):
            def split_lo(v, slot):
                dve.wait_ge(hi_done, v + 1)
                dve.tensor_tensor(lo[:, slot, :], raw[:, slot, :], hi[:, slot, :].bitcast(F32), ALU.subtract)\
                   .then_inc(lo_done, 1)

            def mod_ops(ly):
                return 32 * min(ly.gbase, CTX_GROUPS) + 16 * max(ly.gbase - CTX_GROUPS, 0)

            def mod_chunk(ly, it, m):
                vecs = 2 if ly.ctx else 1
                turn = ly.gbase * 2 + it * 2 + m // 2
                dve.wait_ge(wm_full[m % 2], 16 * (turn + 1))
                first_op = mod_ops(ly) + it * 16 * vecs + m * 4 * vecs
                for k in range(4):
                    kt = 4 * m + k
                    for v in range(vecs):
                        n = first_op + k * vecs + v
                        w = wm[:, m % 2, k * HW:k * HW + HW]
                        a = acc[:, v, k % 2, :]
                        c = csilu[:, v * KT + kt:v * KT + kt + 1]
                        if kt < 2:
                            dve.wait_ge(accf_ready, ly.gbase + 1 + it - 1 + 1) if False else None
                            ins = dve.tensor_scalar(a, w, c, None, ALU.mult)
                        else:
                            dve.wait_ge(wm_op, n - 2 * vecs + 1)
                            ins = dve.scalar_tensor_tensor(a, w, c, a, ALU.mult, ALU.add)
                        ins.then_inc(wm_op, 1)
                dve.wait_ge(wm_op, first_op + 4 * vecs)
                dve.sem_inc(wm_used, 1)

            def mod_hand_over(ly, it):
                g = ly.gbase + it
                dve.wait_ge(mod_sum, g + 1)
                vecs = 2 if ly.ctx else 1
                dve.tensor_tensor(accf[:, 0:vecs, :], acc[:, 0:vecs, 0, :], acc[:, 0:vecs, 1, :], ALU.add)\
                   .then_inc(accf_ready, 1)

            def mod_take(ly, it):
                g = ly.gbase + it
                b0 = COLS["b_mod"][0]
                dve.wait_ge(mod_sum, g + 2)
                bias = cols[:, bass.ds(2 * g + b0, 2)]
                if ly.ctx:
                    dve.tensor_tensor(modx[:, bass.ds(2 * g, 2)], ps[:, 7, 2:4], bias, ALU.add)
                dve.tensor_tensor(mod[:, bass.ds(2 * g, 2)], ps[:, 7, 0:2], bias, ALU.add).then_inc(mod_done, 1)

            def prepare(ly, it, hf):
                for j in range(ly.c):
                    a = ahead(ly, it, hf, j)
                    if a is not None:
                        split_lo(a[0], a[1])
                    if j < ly.mod:
                        m = hf * ly.mod + j
                        mod_chunk(ly, it, m)
                        if m == 3:
                            mod_hand_over(ly, it)

            def add_half(ly, it, hf, t, dst, sem_after=True):
                bank = (2 * hf + t) % 4
                dve.wait_ge(tmp_ready, CONCAT[ly.name] + it * ly.tpi + 2 * hf + t + 1)
                dve.tensor_tensor(dst, ps[:, bank, 0:NX], tmp[:, bank, :], ALU.add).then_inc(bank_free, 1)

            def whole(ly, it, hf, t):
                return ly.tbase + it * ly.tpi + 2 * hf + t + 5

            def norm_scale(name):
                k, _, n, _, _ = NORMS[name]
                dve.wait_ge(std_ready, k + 1)
                dve.reciprocal(rstd[:, 0:n], std[:, 0:n]).then_inc(rstd_ready, 1)

            def norm_apply(name, src, gain, dst_hi, dst_lo, shift=None, also=None):
                k0, _, n, batches, tiles = NORMS[name]
                dve.wait_ge(rstd_ready, k0 + 1)

                def view(b):
                    return xn[:, b % 2, 0:tiles * n].rearrange("p (k n) -> p k n", k=tiles)

                def scale(b):
                    if also is not None and b >= 2:
                        dve.wait_ge(also, b - 1)
                    for k in range(tiles):
                        ins = dve.scalar_tensor_tensor(view(b)[:, k, :], src(b * tiles + k), gain(b * tiles + k),
                                                       rstd[:, 0:n], ALU.mult, ALU.mult)
                    ins.then_inc(xn_ready, 1)

                def rest(b):
                    dve.wait_ge(xs_hi, SPLIT[name] + b + 1)
                    if shift is None:
                        ins = dve.tensor_tensor(dst_lo(b), view(b), dst_hi(b).bitcast(F32), ALU.subtract)
                    else:
                        for k in range(tiles):
                            ins = dve.scalar_tensor_tensor(dst_lo(b)[:, k, :], view(b)[:, k, :], shift(b * tiles + k),
                                                           dst_hi(b)[:, k, :].bitcast(F32), ALU.add, ALU.subtract)
                    ins.then_inc(xs_ready, 1)

                scale(0)
                for b in range(batches):
                    if b + 1 < batches:
                        if b >= 1:
                            dve.wait_ge(xs_ready, SPLIT[name] + b)
                        scale(b + 1)
                    rest(b)

            def norm_in_place(name, gain, done):
                k0 = NORMS[name][0]
                dve.wait_ge(rstd_ready, k0 + 1)
                for k in range(KT):
                    dve.scalar_tensor_tensor(hx[:, k, :], hx[:, k, :], gain(k), rstd[:, 0:NX], ALU.mult, ALU.mult)\
                       .then_inc(done, 1)

            dve.memset(att[:, 0, :], 0.0).then_inc(lo_done, RING)
            dve.memset(att[:, 1, :], 0.0).then_inc(chunk_used, RING)
            dve.memset(att[:, 2, :], 0.0).then_inc(bank_free, 4)
            dve.memset(mod[:, 0:1], 0.0).then_inc(wm_used, 2)
            dve.memset(mod[:, 1:2], 0.0).then_inc(mod_sum, 1)
            dve.memset(mod[:, 2:3], 0.0).then_inc(mod_done, 1)

            norm_scale("mix")
            dve.wait_ge(tables_in, 48)
            norm_apply("mix", lambda k: h[:, k, :], lambda k: col("norm_mix", k),
                       lambda b: xs1[:, 4 * b:4 * b + 4, 0, :], lambda b: xs1[:, 4 * b:4 * b + 4, 1, :], also=f_used)
            for v in range(RING):
                split_lo(v, v)
            dve.wait_ge(silu_c_done, 1)
            ly = LY["in1"]

            def body(it, ly=ly):
                for hf in range(2):
                    prepare(ly, it, hf)
                mod_take(ly, it)
            run(dve, ly, body)

            dve.wait_ge(f_used, 4)
            dve.tensor_scalar(fl[0:HEADS, 0, :], ps[0:HEADS, 5, 0:N1],
                              cols[0:HEADS, COLS["b_f"][0]:COLS["b_f"][0] + 1], None, ALU.add).then_inc(f_dve, 1)
            dve.wait_ge(f_act, 3)
            dve.wait_ge(f_dve, 1)
            dve.scalar_tensor_tensor(fl[0:HEADS, 2, :], fl[0:HEADS, 0, :], 0.0, fl[0:HEADS, 1, :], ALU.min, ALU.subtract)\
               .then_inc(f_dve, 1)
            dve.wait_ge(f_dve, 2)
            dve.memset(fl[0:HEADS, 1, :], 0.0).then_inc(f_dve, 1)
            dve.wait_ge(f_dve, 3)
            dve.tensor_tensor_scan(fl[0:HEADS, 0, :], fl[0:HEADS, 2, :], fl[0:HEADS, 1, :], 0.0, ALU.add, ALU.add)\
               .then_inc(f_dve, 1)
            dve.wait_ge(f_dve, 4)
            dve.tensor_scalar(fl[0:HEADS, 2, :], fl[0:HEADS, 0, :], -1.0, None, ALU.mult).then_inc(f_dve, 1)

            dve.wait_ge(bank_free, 48 + 4)
            dve.tensor_tensor(z[:, 32:40, NM - 2:N1], z[:, 32:40, NM - 2:N1], z[:, 40:48, NM - 2:N1], ALU.mult)\
               .then_inc(conv_step, 1)

            def conv_group(g):
                n = 1 + 3 * g
                dst = z[:, 40 + g, 0:NX]
                dve.wait_ge(conv_step, 1)
                dve.tensor_scalar(dst, z[:, 32 + g, NM - 2:N1 - 2], col("conv1", g), None, ALU.mult).then_inc(conv_step, 1)
                dve.wait_ge(conv_step, n + 1)
                dve.scalar_tensor_tensor(dst, z[:, 32 + g, NM - 1:N1 - 1], col("conv1", 8 + g), dst, ALU.mult, ALU.add)\
                   .then_inc(conv_step, 1)
                dve.wait_ge(conv_step, n + 2)
                dve.scalar_tensor_tensor(dst, z[:, 32 + g, NM:N1], col("conv1", 16 + g), dst, ALU.mult, ALU.add)\
                   .then_inc(conv_step, 1)
                dve.wait_ge(conv_step, n + 3)
                dve.tensor_tensor(z[:, 24 + g, NM:N1], dst, z[:, 24 + g, NM:N1], ALU.mult).then_inc(conv_ready, 1)

            for hd in range(HEADS):
                for qt in range(2):
                    u = 2 * hd + qt
                    dve.wait_ge(s_ready, u + 1)
                    if hd >= 2:
                        dve.wait_ge(pt_psum, hd - 1)
                    dve.tensor_tensor(p1[:, hd % 2, qt, :], ps[:, 4 + qt, 0:N1], causal[:, qt, :], ALU.add)\
                       .then_inc(s_taken, 1)
                for qt in range(2):
                    u = 2 * hd + qt
                    dve.wait_ge(s_taken, u + 1)
                    dve.tensor_reduce(att[:, 0, u:u + 1], p1[:, hd % 2, qt, :], AX_X, ALU.max, negate=True)\
                       .then_inc(max_ready, 1)
                for qt in range(2):
                    u = 2 * hd + qt
                    dve.wait_ge(exp_ready, u + 1)
                    dve.reciprocal(att[:, 2, u:u + 1], att[:, 1, u:u + 1]).then_inc(rsum_ready, 1)
                for qt in range(2):
                    u = 2 * hd + qt
                    dve.wait_ge(rsum_ready, u + 1)
                    dve.tensor_scalar(p1[:, hd % 2, qt, :], p1[:, hd % 2, qt, :], att[:, 2, u:u + 1], None, ALU.mult)\
                       .then_inc(p_ready, 1)
                conv_group(hd)
            dve.wait_ge(gn_std, 1)
            dve.reciprocal(rstd[0:16, 0:NX], std[0:16, 0:NX]).then_inc(gn_r, 1)

            def gn_rest(b):
                dve.wait_ge(gn_hi, b + 1)
                dve.tensor_tensor(ys1[:, 4 * b:4 * b + 4, 1, :], xn[:, b % 2, 0:4 * NX].rearrange("p (k n) -> p k n", k=4),
                                  ys1[:, 4 * b:4 * b + 4, 0, :].bitcast(F32), ALU.subtract).then_inc(gn_ready, 1)

            for b in range(4):
                if b >= 2:
                    dve.wait_ge(gn_ready, b - 1)
                for k in range(4):
                    g = 4 * b + k
                    y = z[:, g if g < 8 else 16 + g, NM:N1]
                    dve.wait_ge(gn_bc, g + 1)
                    dve.scalar_tensor_tensor(xn[:, b % 2, k * NX:k * NX + NX], y, col("out_gain", g), ps[:, g % 2, 0:NX],
                                             ALU.mult, ALU.mult).then_inc(gn_y, 1)
                if b >= 1:
                    gn_rest(b - 1)
            gn_rest(3)

            def residual(ly, gate=None):
                def body(it):
                    for hf in range(ly.halves):
                        prepare(ly, it, hf)
                        for t in range(2):
                            add_half(ly, it, hf, t, tot[:, (2 * hf + t) % 4, :])
                        for t in range(2):
                            n = 2 * hf + t
                            hk = h[:, bass.ds(it * ly.tpi + n, 1), NM:N1].rearrange("p a n -> p (a n)")
                            dve.wait_ge(bank_free, whole(ly, it, hf, t))
                            if gate is None:
                                ins = dve.tensor_tensor(hk, tot[:, n % 4, :], hk, ALU.add)
                            else:
                                ins = dve.scalar_tensor_tensor(hk, tot[:, n % 4, :], mod[:, bass.ds(it * ly.tpi + gate + n, 1)],
                                                               hk, ALU.mult, ALU.add)
                            ins.then_inc(res_done, 1)
                    if ly.mod:
                        mod_take(ly, it)
                run(dve, ly, body)

            def hidden(ly, it, ready):
                for t in range(2):
                    n = HID[ly.name] + it * 2 + t
                    s, v, value = ready(t)
                    dve.wait_ge(s, v)
                    dve.wait_ge(sg_ready, n + 1)
                    dve.tensor_tensor(hv[:, t, :], value, sg[:, t, :], ALU.mult).then_inc(hv_ready, 1)
                for t in range(2):
                    n = HID[ly.name] + it * 2 + t
                    part = hid[:, bass.ds(it * 2 + t, 1), :, :].rearrange("p a b n -> p (a b) n")
                    dve.wait_ge(hid_hi, n + 1)
                    dve.tensor_tensor(part[:, 1, :], hv[:, t, :], part[:, 0, :].bitcast(F32), ALU.subtract)\
                       .then_inc(hid_ready, 1)

            residual(LY["out1"])
            norm_scale("ffn1")
            norm_apply("ffn1", lambda k: hx[:, k, :], lambda k: col("norm_ffn", k),
                       lambda b: hs[:, 4 * b:4 * b + 4, 0, :], lambda b: hs[:, 4 * b:4 * b + 4, 1, :])
            for part in "abc":
                ly = LY["up1" + part]

                def body(it, ly=ly):
                    prepare(ly, it, 0)
                    for t in range(2):
                        add_half(ly, it, 0, t, gt[:, t, :])
                    prepare(ly, it, 1)
                    for t in range(2):
                        add_half(ly, it, 1, t, ut[:, t, :])
                    hidden(ly, it, lambda t: (bank_free, whole(ly, it, 1, t), ut[:, t, :]))
                    mod_take(ly, it)
                run(dve, ly, body)
                residual(LY["dn1" + part])

            dve.wait_ge(mod_done, MOD_GROUPS + 1)
            dve.scalar_tensor_tensor(gm[:, 0, :], mod[:, KT:2 * KT], 1.0, col("g_attn", 0, KT), ALU.add, ALU.mult)\
               .then_inc(gm_done, 1)
            dve.scalar_tensor_tensor(gm[:, 1, :], modx[:, KT:2 * KT], 1.0, col("g_attn", 0, KT), ALU.add, ALU.mult)\
               .then_inc(gm_done, 1)
            dve.scalar_tensor_tensor(gm[:, 2, :], mod[:, 4 * KT:5 * KT], 1.0, col("g_ffn", 0, KT), ALU.add, ALU.mult)\
               .then_inc(gm_done, 1)
            norm_scale("ctx")
            dve.wait_ge(gm_done, 3)
            norm_apply("ctx", lambda k: cx[:, k, :], lambda k: gm[:, 1, k:k + 1],
                       lambda b: hs2[:, 4 * b:4 * b + 4, 0, NX:2 * NX], lambda b: hs2[:, 4 * b:4 * b + 4, 1, NX:2 * NX],
                       shift=lambda k: modx[:, k:k + 1])
            norm_scale("final1")
            norm_in_place("final1", lambda k: col("final_norm", k), x_final)
            norm_scale("attn2")
            dve.wait_ge(x_final, KT)
            norm_apply("attn2", lambda k: hx[:, k, :], lambda k: gm[:, 0, k:k + 1],
                       lambda b: hs2[:, 4 * b:4 * b + 4, 0, 0:NX], lambda b: hs2[:, 4 * b:4 * b + 4, 1, 0:NX],
                       shift=lambda k: mod[:, k:k + 1])

            def straight(ly, dst, n):
                def body(it):
                    for hf in range(ly.halves):
                        prepare(ly, it, hf)
                        dve.wait_ge(chunk_used, last_chunk(ly, it, hf) + 5)
                        for t in range(ly.tiles):
                            bank = 4 * (hf % 2) + t if ly.tiles == 4 else (2 * hf + t) % 4
                            dve.tensor_copy(dst(it, hf, t), ps[:, bank, 0:n]).then_inc(bank_free, 1)
                run(dve, ly, body)

            def summed(ly, dst):
                def body(it):
                    for hf in range(ly.halves):
                        prepare(ly, it, hf)
                        for t in range(2):
                            add_half(ly, it, hf, t, dst(it, hf, t))
                run(dve, ly, body)

            straight(LY["joint"], lambda it, hf, t: zj[:, bass.ds(it * 4 + 2 * hf + t, 1), :].rearrange("p a n -> p (a n)"),
                     2 * NX)
            straight(LY["kr"], lambda it, hf, t: kr[:, :], 2 * NX)
            summed(LY["xonly"], lambda it, hf, t: zx[:, bass.ds(it * 4 + 2 * hf + t, 1), :].rearrange("p a n -> p (a n)"))
            straight(LY["vn"], lambda it, hf, t: vn[:, t, hf * HW:hf * HW + HW], HW)
            for g in range(FN_GROUPS):
                dve.wait_ge(fn_b, g + 1)
                dve.tensor_copy(sp[:, g % 2, :], ps[:, 6, 0:NX]).then_inc(fn_sp, 1)
                dve.wait_ge(y2_hi, g + 1)
                dve.tensor_tensor(ysb[:, 4 + g, 1, :], ps[:, 7, 0:NX], ysb[:, 4 + g, 0, :].bitcast(F32), ALU.subtract)\
                   .then_inc(y2_ready, 1)
            dve.wait_ge(late_in, 48)
            window = tab("na_mask").rearrange("p (a n) -> p a n", a=1).to_broadcast([P, 32, 64])
            flat = na[:, :, :, :].rearrange("p h q (a n) -> p (h q a) n", n=64)
            dve.tensor_tensor(flat, flat, window, ALU.add).then_inc(na_bias_ready, 1)

            def attend(first, heads, scale, local, y0):
                def softmax(hd):
                    for qt in range(2):
                        u = 2 * (first + hd) + qt
                        dve.wait_ge(s2_ready, u + 1)
                        if local:
                            if hd >= 2:
                                dve.wait_ge(pt2_psum, first + hd - 1)
                            dve.wait_ge(s2_half, u + 1)
                            dve.scalar_tensor_tensor(p2[:, hd % 2, qt, 0:NX], ps[:, 4 + qt, 0:NX], scale,
                                                     na[:, hd, qt, :], ALU.mult, ALU.add).then_inc(s2_bias, 1)
                        else:
                            dve.tensor_reduce(att[:, 2, u % 16:u % 16 + 1], ps[:, 4 + qt, :], AX_X, ALU.max, negate=True)\
                               .then_inc(max2_ready, 1)
                    for qt in range(2):
                        u = 2 * (first + hd) + qt
                        if local:
                            dve.wait_ge(s2_bias, u + 1)
                            dve.tensor_reduce(att[:, 0, u % 16:u % 16 + 1], p2[:, hd % 2, qt, :], AX_X, ALU.max, negate=True)\
                               .then_inc(nmax2_ready, 1)
                        else:
                            if hd >= 2:
                                dve.wait_ge(pt2_psum, first + hd - 1)
                            dve.wait_ge(max2_ready, 2 * hd + qt + 1)
                            dve.tensor_scalar(att[:, 0, u % 16:u % 16 + 1], att[:, 2, u % 16:u % 16 + 1], scale, None, ALU.mult)\
                               .then_inc(nmax2_ready, 1)
                    for qt in range(2):
                        u = 2 * (first + hd) + qt
                        dve.wait_ge(exp2_ready, u + 1)
                        dve.reciprocal(att[:, 2, u % 16:u % 16 + 1], att[:, 1, u % 16:u % 16 + 1]).then_inc(rsum2_ready, 1)
                    for qt in range(2):
                        u = 2 * (first + hd) + qt
                        dve.wait_ge(rsum2_ready, u + 1)
                        dve.tensor_scalar(p2[:, hd % 2, qt, :], p2[:, hd % 2, qt, :], att[:, 2, u % 16:u % 16 + 1], None, ALU.mult)\
                           .then_inc(p2_ready, 1)

                def rest(hd):
                    y = ysb[:, hd] if local else ysa[:, hd]
                    dve.wait_ge(y2_hi, y0 + hd + 1)
                    dve.tensor_tensor(y[:, 1, :], ps[:, hd % 2, 0:NX], y[:, 0, :].bitcast(F32), ALU.subtract)\
                       .then_inc(y2_ready, 1)

                for hd in range(heads):
                    softmax(hd)
                    if hd >= 1:
                        rest(hd - 1)
                rest(heads - 1)

            norm_scale("kv")
            dve.wait_ge(na_bias_ready, 1)
            attend(0, NA_HEADS, NA_SCALE, True, FN_GROUPS)
            norm_apply("kv", lambda k: zj[:, k, :], lambda k: col("g_kv", k),
                       lambda b: ckvs[:, 2 * b:2 * b + 2, 0, :], lambda b: ckvs[:, 2 * b:2 * b + 2, 1, :])
            norm_scale("q")
            norm_apply("q", lambda k: zx[:, k, :], lambda k: col("g_q", k),
                       lambda b: cqs[:, :, 0, :], lambda b: cqs[:, :, 1, :])
            straight(LY["uk"], lambda it, hf, t: kn_m[:, 2 * hf + t, :], 2 * NX)
            straight(LY["uv"], lambda it, hf, t: vt_m[:, t, hf * HW:hf * HW + HW], HW)
            dve.memset(krm[:, :, :], 0.0).then_inc(krm_zero, 1)
            summed(LY["uq"], lambda it, hf, t: qn_m[:, 2 * hf + t, :] if hf < 4 else qr_m[:, 2 * (hf - 4) + t, :])
            dve.wait_ge(rot_psum, 1)
            dve.wait_ge(bank_free, LY["out2"].tbase + 4)
            cos = tab("cos")
            sin = tab("sin")
            cos4 = cos.rearrange("p (a n) -> p a n", a=1).to_broadcast([P, 4, NX])
            sin2 = sin.rearrange("p (a n) -> p a n", a=1).to_broadcast([P, 2, NX])
            dve.tensor_tensor(rot[:, 0, :, :], qr_m[:, :, :], cos4, ALU.mult).then_inc(rot_step, 1)
            for j in range(2):
                dve.tensor_tensor(rot[:, 1, 2 * j:2 * j + 2, :], ps[:, 4 + j, :].rearrange("p (a n) -> p a n", a=2), sin2,
                                  ALU.mult).then_inc(rot_step, 1)
            dve.wait_ge(rot_step, 3)
            dve.tensor_tensor(qr_m[:, :, :], rot[:, 0, :, :], rot[:, 1, :, :], ALU.add).then_inc(rope_ready, 1)
            dve.wait_ge(rope_ready, 1)
            dve.tensor_tensor(rot[:, 0, 0, :], kr[:, 0:NX], cos, ALU.mult).then_inc(rot_step, 1)
            dve.tensor_tensor(rot[:, 1, 0, :], ps[:, 6, 0:NX], sin, ALU.mult).then_inc(rot_step, 1)
            dve.wait_ge(rot_step, 5)
            dve.wait_ge(krm_zero, 1)
            for half, rows in ((0, slice(0, 64)), (1, slice(64, 128))):
                dve.tensor_tensor(krm[rows, half, 0:NX], rot[rows, 0, 0, :], rot[rows, 1, 0, :], ALU.add).then_inc(rope_ready, 1)
                dve.tensor_copy(krm[rows, half, NX:2 * NX], kr[rows, NX:2 * NX]).then_inc(rope_ready, 1)
            dve.wait_ge(rope_ready, 5)
            dve.memset(att[:, 1, :], 0.0).then_inc(rope_ready, 1)
            attend(NA_HEADS, HEADS, MLA_SCALE, False, FN_GROUPS + NA_HEADS)

            residual(LY["out2"], gate=2 * KT)
            dve.memset(pad[:, :, 0:1], 0.0).then_inc(pads_zero, 1)
            dve.memset(pad[:, :, NX + 1:NX + 2], 0.0).then_inc(pads_zero, 1)
            norm_scale("ffn2")
            norm_apply("ffn2", lambda k: hx[:, k, :], lambda k: gm[:, 2, k:k + 1],
                       lambda b: hs[:, 4 * b:4 * b + 4, 0, :], lambda b: hs[:, 4 * b:4 * b + 4, 1, :],
                       shift=lambda k: mod[:, 3 * KT + k:3 * KT + k + 1])
            dve.wait_ge(pads_zero, 2)
            for part in "abc":
                ly = LY["up2" + part]

                def body(it, ly=ly):
                    tile0 = (HID[ly.name] - HID["up2a"])
                    step0 = tile0 * 6
                    for hf in range(2):
                        prepare(ly, it, hf)
                        for t in range(2):
                            add_half(ly, it, hf, t, pad[:, t, 1:NX + 1])
                        for step in range(3):
                            for t in range(2):
                                c = tile0 + hf * FT + t
                                n = step0 + it * 12 + hf * 6 + 2 * step + t
                                if step == 0:
                                    dve.wait_ge(bank_free, whole(ly, it, hf, t))
                                    ins = dve.tensor_scalar(cv[:, t, 0, :], pad[:, t, 1:NX + 1], dcol("conv2_w1", it * 2 + c),
                                                            dcol("conv2_b", it * 2 + c), ALU.mult, ALU.add)
                                elif step == 1:
                                    dve.wait_ge(cv_step, n - 1)
                                    ins = dve.scalar_tensor_tensor(cv[:, t, 1, :], pad[:, t, 0:NX], dcol("conv2_w0", it * 2 + c),
                                                                   cv[:, t, 0, :], ALU.mult, ALU.add)
                                else:
                                    dve.wait_ge(cv_step, n - 1)
                                    if hf == 1:
                                        dve.wait_ge(sg_ready, HID[ly.name] + it * 2 + t + 1)
                                    ins = dve.scalar_tensor_tensor(cv[:, t, 2, :], pad[:, t, 2:NX + 2], dcol("conv2_w2", it * 2 + c),
                                                                   cv[:, t, 1, :], ALU.mult, ALU.add)
                                ins.then_inc(cv_step, 1)
                    hidden(ly, it, lambda t: (cv_step, step0 + it * 12 + 6 + 4 + t + 1, cv[:, t, 2, :]))
                run(dve, ly, body)
                residual(LY["dn2" + part], gate=5 * KT)
            norm_scale("final2")
            norm_in_place("final2", lambda k: col("g_final", k), x_final)


def tables():
    t = {"ident": np.eye(P), "ones": np.ones((P, P))}
    key = np.arange(N1)[None, :]
    row = np.arange(P)[:, None]
    t["causal"] = np.concatenate([np.where(key <= NM + qt * P + row, 0.0, NEG) for qt in range(2)], 1)
    d = np.arange(P) % 64
    partner = np.arange(P) + np.where(d % 32 < 16, 16, -16)
    swap = np.zeros((P, P))
    swap[partner, np.arange(P)] = 1.0
    t["swap"] = swap
    freqs = np.float32(10000.0) ** (-np.arange(16, dtype=np.float32) / np.float32(16))
    pos = np.arange(NX)
    where = np.where(d[:, None] < 32, pos[None, :] // 64, pos[None, :] % 64).astype(np.float32)
    angle = (where * freqs[d % 16][:, None].astype(np.float32)).astype(np.float64)
    t["cos"] = np.cos(angle)
    t["sin"] = np.sin(angle) * np.where(d % 32 < 16, -1.0, 1.0)[:, None]
    ca = 2 * np.pi * (np.outer(np.arange(P), np.arange(P)) % P) / P
    t["dft_c"] = np.concatenate([np.cos(ca), np.sin(ca)], 1)
    la = 2 * np.pi * (np.outer(np.arange(NX), np.arange(NX)) % NX) / NX
    norm = (NX * P) ** -0.5
    for name, m in (("dft_l_cos", np.cos(la) * norm), ("dft_l_sin", -np.sin(la) * norm)):
        t[name] = m.reshape(2, P, NX).transpose(1, 0, 2).reshape(P, 2 * NX)
    w = (np.arange(P) % 64)[:, None]
    first = np.clip(w - 8, 0, 48)
    c = np.arange(64)[None, :]
    t["na_mask"] = np.where((c >= first) & (c < first + 16), 0.0, NEG)
    e = np.zeros((P, 31))
    e[:, 15] = 1.0
    t["e31"] = e
    names = list(TABS)
    return tuple(np.concatenate([t[n] for n in part], 1).astype(np.float32) for part in (names[:4], names[4:]))


def kernel(**inputs):
    import concourse.bacc as bacc
    from concourse.bass_utils import run_bass_kernel_spmd

    a = {k: np.asarray(v) for k, v in inputs.items()}

    def chunks(w, per=4):
        k, n = w.shape
        width = CW // per
        w = w.reshape(k // (per * P), per, P, n // width, width)
        return w.transpose(3, 0, 2, 1, 4).reshape(-1, P, CW)

    def halves(first, second):
        f, s = chunks(first), chunks(second)
        per = first.shape[0] // (4 * P)
        f, s = f.reshape(-1, per, P, CW), s.reshape(-1, per, P, CW)
        return np.stack([f, s], 1).reshape(-1, P, CW)

    def feed_forward(gate, value, down):
        out = []
        for f0, f1 in ((0, 2048), (2048, 4096), (4096, F)):
            out += [halves(gate[:, f0:f1], value[:, f0:f1]), chunks(down[f0:f1])]
        return out

    w_in, w_in2 = a["w_in"][0], a["w_in_2"][0]
    o = np.cumsum([0, 512, 512, 64, 512, 512, 512, 512])
    cq, ckv, kr, qn, kn, vn, fn = (w_in2[:, o[i]:o[i + 1]] for i in range(7))
    uq = a["w_uq_2"][0].reshape(512, HEADS, 192)
    ukv = a["w_ukv_2"][0].reshape(512, HEADS, 2, P)
    up2 = a["w_up_2"][0]
    stream = np.concatenate(
        [chunks(w_in[:, :6144]), chunks(a["w_out"][0])]
        + feed_forward(a["w_gate"][0], a["w_up"][0], a["w_down"][0])
        + [chunks(ckv), chunks(kn), chunks(np.concatenate([kr, kr], 1), per=8), chunks(cq), chunks(qn), chunks(fn),
           chunks(vn), chunks(ukv[:, :, 0].reshape(512, 1024)), chunks(ukv[:, :, 1].reshape(512, 1024)),
           chunks(uq[:, :, :P].reshape(512, 1024)), chunks(uq[:, :, P:].reshape(512, 512)), chunks(a["w_out_2"][0])]
        + feed_forward(up2[:, :F], up2[:, F:], a["w_down_2"][0]))
    assert len(stream) == N_CHUNKS

    def features(x):
        return x.T.reshape(-1, P, x.shape[0]).transpose(1, 0, 2)

    def columns(v):
        return v.reshape(-1, P).T

    conv_w2 = a["conv_w_2"][0]
    b_f = np.zeros((P, 1), np.float32)
    b_f[:HEADS, 0] = a["b_f"][0]
    vectors = {"norm_mix": a["norm_mix"], "out_gain": a["out_gain"], "norm_ffn": a["norm_ffn"],
               "final_norm": a["final_norm"], "g_attn": a["g_attn_2"], "g_ffn": a["g_ffn_2"], "g_final": a["g_final_2"],
               "g_q": a["g_q_2"], "g_kv": a["g_kv_2"], "c": a["c_2"], "c_ctx": a["c_ctx_2"], "b_mod": a["b_mod_2"],
               "conv1": a["conv_w"], "conv2_w0": conv_w2[0], "conv2_w1": conv_w2[1], "conv2_w2": conv_w2[2],
               "conv2_b": a["conv_b_2"]}
    packed = [columns(vectors[n]) if n in vectors else b_f if n == "b_f" else np.full((P, 1), EPS, np.float32)
              for n in COLS]
    rpb = a["na_rpb_2"][0]
    padded = np.zeros((NA_HEADS, 15, 127), np.float32)
    padded[:, :, 48:79] = rpb
    toeplitz = np.stack([padded[:, :, 63 - w:127 - w] for w in range(64)], 2)
    bias = np.stack([toeplitz[:, 7 - r:11 - r] for r in range(4)], 1)
    na_bias = bias.reshape(NA_HEADS, 2, 2, 4, 64, 64).transpose(2, 4, 0, 1, 3, 5).reshape(P, NA_HEADS, 2, NX)

    arrays = {
        "tokens": features(np.concatenate([a["meta"], a["x"][0]], 0)),
        "ctx_tokens": features(a["ctx_2"][0]),
        "cols": np.concatenate(packed, 1),
        "tables1": tables()[0],
        "tables2": tables()[1],
        "w_forget": w_in[:, 6144:].reshape(KT, P, HEADS).transpose(1, 0, 2),
        "stream": stream,
        "mod_stream": chunks(a["w_mod_2"][0]),
        "na_bias": na_bias,
        "w_fnet": a["w_fnet_2"][0].transpose(1, 0, 2),
    }
    nc = bacc.Bacc("TRN2", target_bir_lowering=False, num_devices=1)
    args = []
    for name in arrays:
        arrays[name] = np.ascontiguousarray(arrays[name])
        args.append(nc.dram_tensor("in_" + name, arrays[name].shape, F32, kind="ExternalInput").ap())
    args.append(nc.dram_tensor("out_tokens", (P, KT, NX), F32, kind="ExternalOutput").ap())
    build(nc, *args)
    r = run_bass_kernel_spmd(nc, [{"in_" + k: v for k, v in arrays.items()}], core_ids=[0])
    got = r.results[0]["out_tokens"]
    return np.ascontiguousarray(got.transpose(2, 1, 0)).reshape(1, NX, D)
```

```python
from contextlib import ExitStack

import numpy as np

import concourse.bass as bass
from concourse import mybir

F32 = mybir.dt.float32
F32R = mybir.dt.float32r
ALU = mybir.AluOpType
ACT = mybir.ActivationFunctionType
AX_X = mybir.AxisListType.X

P = 128
D = 2048
KT = D // P
NX = 256
NM = 16
N1 = NM + NX
HEADS = 8
F = 5632
FT = F // P
EPS = 1e-6
SCALE1 = 128.0 ** -0.5
MLA_SCALE = 192.0 ** -0.5
NA_SCALE = 128.0 ** -0.5
NA_HEADS = 4
FN_GROUPS = 4
NEG = -1e30
RING = 4
CW = 1024
HW = 256
MOD_TILES = 6 * D // P
CTX_TILES = 2 * KT


class Layer:

    def __init__(self, name, its, halves, c, tiles=2, mod=0, ctx=False, loop=True):
        self.name, self.its, self.halves, self.c, self.tiles = name, its, halves, c, tiles
        self.mod, self.ctx, self.loop = mod, ctx, loop and its > 1
        self.mtiles = 4 if ctx else 2
        if ctx:
            self.mod_at = (0, 1, 3, 5, 7, 9, 11, 12)
        else:
            self.mod_at = (0, 1, 3, 4) if mod else ()
        self.cpi = halves * c
        self.tpi = halves * tiles


def ffn_layers(tag, mod):
    out = []
    for part, its in (("a", 8), ("b", 8), ("c", 6)):
        out.append(Layer("up" + tag + part, its, 2, 4, mod=2 * mod))
        if part == "c":
            out.append(Layer("dn" + tag + part, 2, 4, 3, loop=tag == "1"))
        else:
            out.append(Layer("dn" + tag + part, 4, 2, 4, mod=2 * mod))
    return out


LAYERS = ([Layer("kv1", 2, 4, 4, mod=2, ctx=True), Layer("f1", 1, 1, 2, tiles=1),
           Layer("q1", 1, 4, 4, mod=2, ctx=True),
           Layer("conv1", 3, 4, 4, mod=2, ctx=True), Layer("out1", 2, 4, 4, mod=2, ctx=True)]
          + ffn_layers("1", 1)
          + [Layer("joint", 2, 2, 4, mod=2), Layer("kr", 1, 1, 2, tiles=1), Layer("xonly", 3, 2, 4),
             Layer("vn", 1, 2, 4, tiles=4), Layer("uk", 1, 4, 1), Layer("uv", 1, 4, 1, tiles=4),
             Layer("uq", 1, 6, 1), Layer("out2", 4, 2, 4)]
          + ffn_layers("2", 0))
_c = _t = _g = _m = _mt = 0
for _l in LAYERS:
    _l.base, _l.tbase, _l.gbase, _l.mbase, _l.mtbase = _c, _t, _g, _m, _mt
    _c += _l.its * _l.cpi
    _t += _l.its * _l.tpi
    _g += _l.its if _l.mod else 0
    _m += _l.its * len(_l.mod_at)
    _mt += _l.its * _l.mtiles if _l.mod else 0
N_CHUNKS, MOD_GROUPS, MOD_CHUNKS = _c, _g, _m
assert _mt == MOD_TILES
LY = {_l.name: _l for _l in LAYERS}

COLS, _o = {}, 0
for _n, _w in (("norm_mix", 16), ("out_gain", 16), ("norm_ffn", 16), ("final_norm", 16), ("g_attn", 16),
               ("g_ffn", 16), ("g_final", 16), ("g_q", 4), ("g_kv", 4), ("c", 16), ("c_ctx", 16),
               ("b_mod", MOD_TILES), ("conv1", 24), ("conv2_w0", 88), ("conv2_w1", 88), ("conv2_w2", 88),
               ("conv2_b", 88), ("b_f", 1), ("eps", 1), ("one", 1), ("scratch", 1)):
    COLS[_n] = (_o, _w)
    _o += _w
N_COLS = _o
TABS, _o = {}, 0
for _n, _w in (("ident", P), ("mean", P), ("causal", 2 * N1), ("e31", 31)):
    TABS[_n] = (_o, _w)
    _o += _w
N_TABS1 = _o
_o = TABS["causal"][0]
for _n, _w in (("swap", P), ("cos", NX), ("sin", NX), ("dft_c", 2 * P), ("dft_l_cos", 2 * NX),
               ("dft_l_sin", 2 * NX), ("na_mask", 64)):
    TABS[_n] = (_o, _w)
    _o += _w
N_TABS = _o


def build(nc, tokens, ctx_tokens, cols_d, tables1_d, tables2_d, stream, mod_stream, na_bias_d, w_fnet_d, out):
    stack = ExitStack()
    with stack:
        def sem(name):
            return stack.enter_context(nc.semaphore(name))

        top = [nc.sbuf_base if isinstance(nc.sbuf_base, int) else 0]
        limit = nc.sbuf_usable_end if isinstance(nc.sbuf_usable_end, int) else 212863
        start = -(-top[0] // 64) * 64
        top[0] = start

        def at(name, shape, dt, offset):
            size = 4 * int(np.prod(shape[1:]))
            assert offset + size <= limit, (name, offset + size, limit)
            return nc.alloc_sbuf_tensor_at(name, shape, dt, offset=offset)

        def keep(name, shape, dt=F32):
            offset = top[0]
            top[0] += -(-4 * int(np.prod(shape[1:])) // 64) * 64
            return at(name, shape, dt, offset), offset

        raw, _ = keep("raw", [P, RING, CW])
        hi, _ = keep("hi", [P, RING, CW], F32R)
        lo, _ = keep("lo", [P, RING, CW], F32R)
        wm, o_wm = keep("wm", [P, 2, CW])
        acc, o_acc = keep("acc", [P, 2, 2 * HW])
        accf, o_accf = keep("accf", [P, 2, 2 * HW])
        h, _ = keep("h", [P, KT, N1])
        cols, _ = keep("cols", [P, N_COLS])
        tabs, _ = keep("tabs", [P, N_TABS])
        mod, _ = keep("mod", [P, MOD_TILES])
        modx, _ = keep("modx", [P, CTX_TILES])
        csilu, _ = keep("csilu", [P, 2 * KT])
        gm, _ = keep("gm", [P, 3, KT])
        att, _ = keep("att", [P, 3, 2 * HEADS])
        cq, _ = keep("cq", [P, 2, HEADS])
        std, _ = keep("std", [P, 2 * NX])
        rstd_q, tok = std[:, 0:NX], std[:, NX:2 * NX]
        rstd, o_rstd = keep("rstd", [P, 2 * NX])
        ssum = at("ssum", [P, 2, NX], F32, o_rstd)
        _, o_work = keep("work_slab", [P, 2, 4, N1])
        sq = at("sq", [P, 2, 4 * N1], F32, o_work)
        xn = at("xn", [P, 2, 4 * N1], F32, o_work)
        tmp = at("tmp", [P, 4, HW], F32, o_work)
        sqb = at("sqb", [P, 2, 2, HW], F32, o_work + 4096)
        arena = top[0]
        xs1 = at("xs1", [P, KT, 2, N1], F32R, arena)
        ys1 = at("ys1", [P, KT, 2, NX], F32R, arena)
        o = arena + 4 * KT * 2 * N1
        z = at("z", [P, 48, N1], F32, o)
        o += 4 * 48 * N1
        vtok = at("vtok", [P, 3, 1024], F32, o)
        o += 4 * 3 * 1024
        fl = at("fl", [P, 3, N1], F32, o)
        p1 = at("p1", [P, 2, 2, N1], F32, o_work)
        pt1 = at("pt1", [P, 3, NX], F32, o_work + 4 * 4 * N1)
        o = arena
        hid = at("hid", [P, KT, 2, NX], F32R, o)
        o += 4 * KT * 2 * NX
        hs = at("hs", [P, KT, 2, NX], F32R, o)
        o += 4 * KT * 2 * NX
        o += 4 * KT * NX
        gt = at("gt", [P, 2, NX], F32, o)
        sg = at("sg", [P, 2, NX], F32, o + 2048)
        ut = at("ut", [P, 2, NX], F32, o + 4096)
        hv = at("hv", [P, 2, NX], F32, o + 6144)
        pad = at("pad", [P, 2, NX + 2], F32, o + 8192)
        cv = at("cv", [P, 2, 3, NX], F32, o + 8192 + 2112)
        csq = at("csq", [P, 4, NX], F32, o + 8192)
        csum = at("csum", [P, 4, NX], F32, o + 8192 + 4096)
        gsqb = at("gsqb", [P, 2, 2, NX], F32, o + 8192)
        gsum = at("gsum", [P, 2, NX], F32, o + 8192 + 4096)
        o = arena
        hs2 = at("hs2", [P, 2, KT, 2, NX], F32R, o)
        ysb = at("ysb", [P, 8, 2, NX], F32R, o)
        qn_m = at("qn_m", [P, HEADS, NX], F32, o + 16384)
        qr_m = at("qr_m", [P, 4, NX], F32, o + 24576)
        kn_m = at("kn_m", [P, HEADS, 2 * NX], F32, o + 28672)
        vt_m = at("vt_m", [P, 4, 1024], F32, o + 45056)
        krm = at("krm", [P, 2, 2 * NX], F32, o + 61440)
        o += 65536
        zj = at("zj", [P, 8, 2 * NX], F32, o)
        cx = at("cx", [P, KT, NX], F32, o)
        cqs = at("cqs", [P, 4, 2, NX], F32R, o + 8192)
        o += 16384
        kr = at("kr", [P, 2 * NX], F32, o)
        o += 2048
        zx = at("zx", [P, 12, NX], F32, o)
        ckvs = at("ckvs", [P, 4, 2, 2 * NX], F32R, o + 4096)
        ysa = at("ysa", [P, 8, 2, NX], F32R, o + 4096)
        o += 12288
        vn = at("vn", [P, 4, 512], F32, o)
        kvsq = at("kvsq", [P, 4, 512], F32, o)
        na = at("na", [P, NA_HEADS, 2, NX], F32, o_wm)
        pt2 = at("pt2", [P, 4, NX], F32, o_acc)
        wfn = at("wfn", [P, FN_GROUPS, P], F32, o_accf)
        p2 = at("p2", [P, 2, 2, 2 * NX], F32, o_work)
        ab = at("ab", [P, 2, 2, 2 * P], F32, o_work)
        sp = at("sp", [P, 2, NX], F32, o_work + 4096)
        rot = at("rot", [P, 2, 4, NX], F32, o_work)
        ps = stack.enter_context(nc.psum_tensor("ps", [P, 8, 512], F32))

        def col(name, i=0, n=1):
            return cols[:, COLS[name][0] + i:COLS[name][0] + i + n]

        def dcol(name, expr):
            return cols[:, bass.ds(expr + COLS[name][0], 1)]

        def tab(name):
            return tabs[:, TABS[name][0]:TABS[name][0] + TABS[name][1]]

        ident, mean = tab("ident"), tab("mean")
        causal = tab("causal").rearrange("p (a n) -> p a n", a=2)
        dft_lc = tab("dft_l_cos").rearrange("p (a n) -> p a n", a=2)
        dft_ls = tab("dft_l_sin").rearrange("p (a n) -> p a n", a=2)
        hx = h[:, :, NM:N1]

        tokens_in = [sem(f"tokens_in{b}") for b in range(4)]
        tables_in, ctx_in, late_in = sem("tables_in"), sem("ctx_in"), sem("late_in")
        silu_c_done = sem("silu_c_done")
        raw_full = [sem(f"raw_full{s}") for s in range(RING)]
        hi_done = sem("hi_done")
        lo_done = sem("lo_done")
        chunk_used = sem("chunk_used")
        tmp_ready = sem("tmp_ready")
        bank_free = sem("bank_free")
        res_done = sem("res_done")
        wm_full = [sem(f"wm_full{s}") for s in range(2)]
        wm_used = sem("wm_used")
        wm_op = sem("wm_op")
        accf_ready = sem("accf_ready")
        mod_sum = sem("mod_sum")
        mod_done = sem("mod_done")
        gm_done = sem("gm_done")
        sq_ready, sq_added = sem("sq_ready"), sem("sq_added")
        stat_ready, std_ready, inv_ready, rstd_ready = sem("stat_ready"), sem("std_ready"), sem("inv_ready"), sem("rstd_ready")
        sum_sq, sum_added = sem("sum_sq"), sem("sum_added")
        gsum_step, rstd_copied, qsq_ready, kvsq_ready = sem("gsum_step"), sem("rstd_copied"), sem("qsq_ready"), sem("kvsq_ready")
        csq_ready, csq_added = sem("csq_ready"), sem("csq_added")
        cxn_ready, cx_hi, cx_done = sem("cxn_ready"), sem("cx_hi"), sem("cx_done")
        xn_ready, xs_hi, xs_ready = sem("xn_ready"), sem("xs_hi"), sem("xs_ready")
        x_final = sem("x_final")
        f_act, f_dve, cq_psum, cq_ready = sem("f_act"), sem("f_dve"), sem("cq_psum"), sem("cq_ready")
        vt_ready, vtok_ready = sem("vt_ready"), sem("vtok_ready")
        s_ready, s_taken, max_ready, exp_ready = sem("s_ready"), sem("s_taken"), sem("max_ready"), sem("exp_ready")
        rsum_ready, p_ready = sem("rsum_ready"), sem("p_ready")
        pt_psum, pt_ready, o_ready, y_ready = sem("pt_psum"), sem("pt_ready"), sem("o_ready"), sem("y_ready")
        conv_step, conv_ready = sem("conv_step"), sem("conv_ready")
        gn_sq, gn_stat, gn_std, gn_r, gn_bc = sem("gn_sq"), sem("gn_stat"), sem("gn_std"), sem("gn_r"), sem("gn_bc")
        gn_y, gn_hi, gn_ready = sem("gn_y"), sem("gn_hi"), sem("gn_ready")
        sg_ready, hv_ready, hid_hi, hid_ready = sem("sg_ready"), sem("hv_ready"), sem("hid_hi"), sem("hid_ready")
        cv_step, pads_zero = sem("cv_step"), sem("pads_zero")
        na_bias_ready = sem("na_bias_ready")
        fn_a, fn_ab, fn_b, fn_sp, fn_c = sem("fn_a"), sem("fn_ab"), sem("fn_b"), sem("fn_sp"), sem("fn_c")
        y2_hi, y2_ready = sem("y2_hi"), sem("y2_ready")
        s2_ready, s2_half, max2_ready, nmax2_ready = sem("s2_ready"), sem("s2_half"), sem("max2_ready"), sem("nmax2_ready")
        s2_bias = sem("s2_bias")
        exp2_ready, rsum2_ready, p2_ready = sem("exp2_ready"), sem("rsum2_ready"), sem("p2_ready")
        pt2_psum, pt2_ready, o2_ready = sem("pt2_psum"), sem("pt2_ready"), sem("o2_ready")
        rot_psum, rot_step, rope_ready, krm_zero = sem("rot_psum"), sem("rot_step"), sem("rope_ready"), sem("krm_zero")
        out_done = sem("out_done")

        NORMS = {"mix": (N1, 4, 4), "ffn1": (NX, 4, 4), "ctx": (NX, 4, 4), "final1": (NX, 4, 4), "attn2": (NX, 4, 4),
                 "kv": (2 * NX, 2, 2), "q": (NX, 1, 4), "ffn2": (NX, 4, 4), "final2": (NX, 4, 4)}
        NTH = {name: i for i, name in enumerate(NORMS)}
        STAT = {name: NTH[name] - (NTH[name] > NTH["final1"]) for name in NORMS}

        def token_tiles(name):
            n = NORMS[name][0]
            return [(th, min(P, n - th * P)) for th in range(-(-n // P))]

        def token_columns(name):
            whole, rest = divmod(NORMS[name][0], P)
            return [(P, 0, whole)] + ([(rest, whole, whole + 1)] if rest else [])

        def tok_std(name):
            return tok[:, 4 * NTH[name]:4 * NTH[name] + 4]

        def tok_inv(name):
            return tok[:, 64 + 4 * NTH[name]:64 + 4 * NTH[name] + 4]

        SPLIT, n_split = {}, 0
        for name in ("mix", "ffn1", "attn2", "kv", "q", "ffn2"):
            SPLIT[name] = n_split
            n_split += NORMS[name][1]
        SUMS, ADD0, n_sum = {}, {}, 0
        for name in ("out1", "dn1c", "out2", "dn2c"):
            SUMS[name], ADD0[name] = n_sum, n_sum + 2 * len(SUMS)
            n_sum += LY[name].its * LY[name].halves
        CONCAT, n_concat = {}, 0
        for ly in LAYERS:
            CONCAT[ly.name] = n_concat
            if ly.name[:2] in ("up", "dn") or ly.name in ("xonly", "uq", "out2"):
                n_concat += ly.its * ly.tpi
        RES, n_res = {}, 0
        for ly in LAYERS:
            RES[ly.name] = n_res
            if ly.name[:2] == "dn" or ly.name == "out2":
                n_res += ly.its * ly.tpi

        def tiles_added(ly, n):
            return (bank_free, ly.tbase + 4 + n) if ly.name == "out1" else (res_done, RES[ly.name] + n)

        HID, n_hid = {}, 0
        for ly in LAYERS:
            HID[ly.name] = n_hid
            if ly.name[:2] == "up":
                n_hid += ly.its * 2

        def run(eng, ly, body):
            if ly.loop:
                with eng.Fori(0, ly.its) as it:
                    body(it)
            else:
                for it in range(ly.its):
                    body(it)

        def ahead(ly, it, hf, j):
            k = ly.base + RING + hf * ly.c + j
            if not ly.loop and k + it * ly.cpi >= N_CHUNKS:
                return None
            if ly.loop:
                return k + it * ly.cpi, k % RING, k // RING + it * (ly.cpi // RING)
            return k + it * ly.cpi, (k + it * ly.cpi) % RING, (k + it * ly.cpi) // RING

        def last_chunk(ly, it, hf):
            return ly.base + (hf + 1) * ly.c - 1 + it * ly.cpi

        def gsq(hd):
            return z[:, 8 + 2 * (hd % 2):10 + 2 * (hd % 2), 0:NX]

        def score_bank2(hd, qt):
            return (4 if hd % 2 == 0 else 2) + qt

        block = stack.enter_context(nc.Block())

        @block.sync
        def _(sp_):
            for b in range(4):
                sp_.dma_start(h[:, 4 * b:4 * b + 4, :], tokens[:, 4 * b:4 * b + 4, :]).then_inc(tokens_in[b], 16)
            sp_.dma_start(cols[:, :], cols_d).then_inc(tables_in, 16)
            sp_.dma_start(tabs[:, 0:N_TABS1], tables1_d).then_inc(tables_in, 16)

            def load(v, slot):
                sp_.wait_ge(lo_done, v + 1)
                sp_.dma_start(raw[:, slot, :], stream[bass.ds(v, 1)].rearrange("a p n -> p (a n)"))\
                   .then_inc(raw_full[slot], 16)

            def load_mod(m, slot):
                sp_.wait_ge(wm_used, m + 1)
                sp_.dma_start(wm[:, slot, :], mod_stream[bass.ds(m, 1)].rearrange("a p n -> p (a n)"))\
                   .then_inc(wm_full[slot], 16)

            for v in range(RING):
                load(v, v)
            for ly in LAYERS:
                def body(it, ly=ly):
                    for hf in range(ly.halves):
                        for j in range(ly.c):
                            a = ahead(ly, it, hf, j)
                            if a is not None:
                                load(a[0], a[1])
                            if hf * ly.c + j in ly.mod_at:
                                m = ly.mod_at.index(hf * ly.c + j)
                                load_mod(ly.mbase + m + it * len(ly.mod_at), m % 2)
                run(sp_, ly, body)
                if ly.name == "out1":
                    sp_.wait_ge(gn_ready, 4)
                    sp_.dma_start(cx[:, :, :], ctx_tokens).then_inc(ctx_in, 16)
                    sp_.dma_start(tabs[:, TABS["swap"][0]:N_TABS], tables2_d).then_inc(late_in, 16)
                if ly.name == "joint":
                    sp_.wait_ge(wm_used, MOD_CHUNKS + 2)
                    sp_.wait_ge(mod_sum, MOD_GROUPS + 1)
                    sp_.dma_start(na[:, :, :, :], na_bias_d).then_inc(late_in, 16)
                    sp_.dma_start(wfn[:, :, :], w_fnet_d).then_inc(late_in, 16)
            sp_.wait_ge(x_final, 2 * KT)
            sp_.dma_start(out, hx).then_inc(out_done, 16)
            sp_.wait_ge(out_done, 16)

        @block.scalar
        def _(act):
            def split_hi(v, slot, turn):
                act.wait_ge(raw_full[slot], 16 * (turn + 1))
                act.wait_ge(chunk_used, v + 1)
                act.activation(hi[:, slot, :], raw[:, slot, :], ACT.Copy).then_inc(hi_done, 1)

            def prepare(ly, it, hf, after_first=None):
                for j in range(ly.c):
                    a = ahead(ly, it, hf, j)
                    if a is not None:
                        split_hi(*a)
                    if j == 0 and after_first is not None:
                        after_first(it, hf)
                    if ly.ctx and hf * ly.c + j == ly.mod_at[-1] + 1:
                        act.wait_ge(wm_used, ly.mbase + (it + 1) * 8 + 2)
                        act.wait_ge(mod_sum, ly.gbase + it + 1)
                        act.activation(accf[:, :, :], acc[:, :, :], ACT.Copy).then_inc(accf_ready, 1)

            def second_halves(ly, it, hf):
                act.wait_ge(chunk_used, last_chunk(ly, it, hf) + 5)
                for t in range(2):
                    bank = (2 * hf + t) % 4
                    n = CONCAT[ly.name] + it * ly.tpi + 2 * hf + t
                    if not ly.loop and n >= 4 or ly.loop and CONCAT[ly.name] >= 4:
                        pass
                    act.activation(tmp[:, bank, :], ps[:, bank, NX:2 * NX], ACT.Copy).then_inc(tmp_ready, 1)

            def load_sqrt():
                act.activation(col("scratch"), col("one"), ACT.Sqrt)

            def token_std(name, bank=4):
                act.wait_ge(stat_ready, STAT[name] + 1)
                for rows, c0, c1 in token_columns(name):
                    ins = act.activation(tok_std(name)[0:rows, c0:c1], ps[0:rows, bank, c0:c1], ACT.Sqrt,
                                         bias=cols[0:rows, COLS["eps"][0]:COLS["eps"][0] + 1])
                ins.then_inc(std_ready, 1)

            def norm_hi(name, dst, shift=None):
                n, batches, tiles = NORMS[name]
                for b in range(batches):
                    act.wait_ge(xn_ready, SPLIT[name] + b + 1)
                    src = xn[:, b % 2, 0:tiles * n].rearrange("p (k n) -> p k n", k=tiles)
                    if shift is None:
                        act.activation(dst(b), src, ACT.Copy).then_inc(xs_hi, 1)
                    else:
                        for k in range(tiles):
                            ins = act.activation(dst(b)[:, k, :], src[:, k, :], ACT.Identity,
                                                 bias=shift(b * tiles + k))
                        ins.then_inc(xs_hi, 1)

            for b in range(4):
                act.wait_ge(tokens_in[b], 16)
                if b >= 2:
                    act.wait_ge(sq_added, b - 1)
                act.activation(sq[:, min(b, 1), :].rearrange("p (k n) -> p k n", k=4), h[:, 4 * b:4 * b + 4, :], ACT.Square,
                               scale=KT ** -0.5).then_inc(sq_ready, 1)
            act.wait_ge(tables_in, 32)
            load_sqrt()
            token_std("mix")
            norm_hi("mix", lambda b: xs1[:, 4 * b:4 * b + 4, 0, :])
            for v in range(RING):
                split_hi(v, v, 0)
            act.activation(csilu[:, :], cols[:, COLS["c"][0]:COLS["c"][0] + 2 * KT], ACT.Silu).then_inc(silu_c_done, 1)

            def to_z(name, z0, first_token, scale=1.0):
                ly = LY[name]

                def body(it):
                    for hf in range(ly.halves):
                        prepare(ly, it, hf)
                        act.wait_ge(chunk_used, last_chunk(ly, it, hf) + 5)
                        for t in range(2):
                            act.activation(z[:, bass.ds(it * ly.tpi + z0 + 2 * hf + t, 1), first_token:N1]
                                           .rearrange("p a n -> p (a n)"), ps[:, (2 * hf + t) % 4, 0:N1 - first_token],
                                           ACT.Copy, scale=scale).then_inc(bank_free, 1)
                run(act, ly, body)

            to_z("kv1", 0, 0)
            prepare(LY["f1"], 0, 0)
            act.wait_ge(bank_free, LY["q1"].tbase + 4)
            act.activation(fl[0:HEADS, 1, :], fl[0:HEADS, 0, :], ACT.Abs).then_inc(f_act, 1)
            act.wait_ge(f_act, 1)
            act.activation(fl[0:HEADS, 2, :], fl[0:HEADS, 1, :], ACT.Exp, scale=-1.0).then_inc(f_act, 1)
            act.wait_ge(f_act, 2)
            act.activation(fl[0:HEADS, 1, :], fl[0:HEADS, 2, :], ACT.Ln, bias=1.0).then_inc(f_act, 1)
            for i in range(6):
                rows = P if i % 3 < 2 else N1 - 2 * P
                act.wait_ge(vt_ready, i + 1)
                act.activation(vtok[0:rows, i % 3, 512 * (i // 3):512 * (i // 3) + 512], ps[0:rows, 4 + i % 3, :],
                               ACT.Copy).then_inc(vtok_ready, 1)
            to_z("q1", 16, NM - 2, SCALE1)
            to_z("conv1", 24, NM - 2)

            def exps(hd):
                for qt in range(2):
                    u = 2 * hd + qt
                    act.wait_ge(max_ready, u + 1)
                    act.activation(p1[:, hd % 2, qt, :], p1[:, hd % 2, qt, :], ACT.Exp, bias=att[:, 0, u:u + 1],
                                   accum_out=att[:, 1, u:u + 1]).then_inc(exp_ready, 1)

            def take_pt(hd):
                act.wait_ge(pt_psum, hd + 1)
                if hd >= 1:
                    act.wait_ge(o_ready, hd)
                act.activation(pt1[:, 0:2, :], ps[:, 6, :].rearrange("p (k n) -> p k n", k=2), ACT.Copy)
                act.activation(pt1[0:NM, 2, :], ps[0:NM, 7, 0:NX], ACT.Copy).then_inc(pt_ready, 1)

            def take_y(hd):
                act.wait_ge(o_ready, hd + 1)
                act.activation(z[:, 16 + hd, NM:N1], ps[:, 0, 0:NX], ACT.Copy)
                if hd >= 2:
                    act.wait_ge(gn_stat, hd - 1)
                act.activation(gsq(hd)[:, 0, :], ps[:, 0, 0:NX], ACT.Square).then_inc(y_ready, 1)
                act.wait_ge(conv_ready, hd + 1)
                act.activation(gsq(hd)[:, 1, :], z[:, 24 + hd, NM:N1], ACT.Square).then_inc(gn_sq, 1)

            exps(0)
            for hd in range(HEADS):
                if hd + 1 < HEADS:
                    exps(hd + 1)
                if hd >= 1:
                    take_y(hd - 1)
                take_pt(hd)
            act.activation(col("scratch"), col("one"), ACT.Sqrt)
            take_y(HEADS - 1)
            act.wait_ge(gn_stat, HEADS)
            act.activation(std[0:16, 0:NX], ps[0:16, 1, 0:NX], ACT.Sqrt, bias=cols[0:16, COLS["eps"][0]:COLS["eps"][0] + 1])\
               .then_inc(gn_std, 1)
            for b in range(4):
                act.wait_ge(gn_y, 4 * b + 4)
                act.activation(ys1[:, 4 * b:4 * b + 4, 0, :], xn[:, b % 2, 0:4 * NX].rearrange("p (k n) -> p k n", k=4),
                               ACT.Copy).then_inc(gn_hi, 1)

            def residual(ly, sums=False, gain=None, after_first=None):
                def body(it):
                    for hf in range(ly.halves):
                        prepare(ly, it, hf, after_first)
                        if ly.name != "out1":
                            second_halves(ly, it, hf)
                        if sums:
                            n0 = it * ly.tpi + 2 * hf
                            act.wait_ge(*tiles_added(ly, n0 + 2))
                            if gain is not None:
                                for t in range(2):
                                    act.activation(gsqb[:, hf % 2, t, :],
                                                   hx[:, bass.ds(n0 + t, 1), :].rearrange("p a n -> p (a n)"),
                                                   ACT.Square, scale=dcol(gain, n0 + t))
                            act.activation(sqb[:, hf % 2, :, :], hx[:, bass.ds(n0, 2), :], ACT.Square,
                                           scale=KT ** -0.5).then_inc(sum_sq, 1)
                run(act, ly, body)

            def gated(ly, gate_src, gate_step):
                def body(it):
                    prepare(ly, it, 0)
                    second_halves(ly, it, 0)
                    prepare(ly, it, 1)
                    for t in range(2):
                        act.wait_ge(*gate_step(it, t))
                        act.activation(sg[:, t, :], gate_src(t), ACT.Silu).then_inc(sg_ready, 1)
                    second_halves(ly, it, 1)
                    for t in range(2):
                        n = HID[ly.name] + it * 2 + t
                        act.wait_ge(hv_ready, n + 1)
                        act.activation(hid[:, bass.ds(it * 2 + t, 1), 0, :].rearrange("p a n -> p (a n)"), hv[:, t, :],
                                       ACT.Copy).then_inc(hid_hi, 1)
                run(act, ly, body)

            load_sqrt()
            residual(LY["out1"], sums=True)
            token_std("ffn1")
            norm_hi("ffn1", lambda b: hs[:, 4 * b:4 * b + 4, 0, :])

            def gated1(part):
                ly = LY["up1" + part]
                gated(ly, lambda t: gt[:, t, :], lambda it, t: (bank_free, ly.tbase + it * 4 + t + 5))

            gated1("a")
            ly = LY["dn1a"]
            act.wait_ge(ctx_in, 16)

            def body(it, ly=ly):
                for hf in range(ly.halves):
                    prepare(ly, it, hf)
                    second_halves(ly, it, hf)
                act.wait_ge(csq_added, it + 1)
                act.activation(csq[:, :, :], cx[:, bass.ds(it * 4, 4), :], ACT.Square, scale=KT ** -0.5).then_inc(csq_ready, 1)
            run(act, ly, body)
            gated1("b")
            load_sqrt()
            token_std("ctx")
            residual(LY["dn1b"])
            gated1("c")

            def ctx_hi(it, hf):
                n0 = it * LY["dn1c"].tpi + 2 * hf
                act.wait_ge(cxn_ready, it * LY["dn1c"].halves + hf + 1)
                for t in range(2):
                    ins = act.activation(hs2[:, 1, bass.ds(n0 + t, 1), 0, :].rearrange("p a n -> p (a n)"),
                                         cx[:, bass.ds(n0 + t, 1), :].rearrange("p a n -> p (a n)"), ACT.Identity,
                                         bias=modx[:, bass.ds(n0 + t, 1)])
                ins.then_inc(cx_hi, 1)

            act.wait_ge(mod_done, LY["joint"].gbase + 1)
            load_sqrt()
            residual(LY["dn1c"], sums=True, gain="final_norm", after_first=ctx_hi)
            token_std("final1")
            act.wait_ge(gsum_step, 2)
            act.activation(tok_std("attn2")[:, 0:2], tok[:, 130:132], ACT.Sqrt, bias=col("eps")).then_inc(std_ready, 1)
            norm_hi("attn2", lambda b: hs2[:, 0, 4 * b:4 * b + 4, 0, :], lambda k: mod[:, k:k + 1])

            def plain(ly):
                def body(it):
                    for hf in range(ly.halves):
                        prepare(ly, it, hf)
                run(act, ly, body)

            plain(LY["joint"])
            act.wait_ge(bank_free, LY["joint"].tbase + 4 + 4)
            act.activation(kvsq[:, :, :], zj[:, 0:4, :], ACT.Square, scale=0.5).then_inc(kvsq_ready, 1)
            plain(LY["kr"])
            residual(LY["xonly"])
            load_sqrt()
            token_std("kv")
            act.wait_ge(bank_free, LY["vn"].tbase + 4)
            act.activation(sq[:, 1, 0:4 * NX].rearrange("p (k n) -> p k n", k=4), zx[:, 0:4, :], ACT.Square, scale=0.5)\
               .then_inc(qsq_ready, 1)
            for hf in range(2):
                prepare(LY["vn"], 0, hf)
                if hf == 0:
                    token_std("q", 7)
                act.wait_ge(rstd_ready, NTH["kv"] + 1 + hf)
                if hf == 0:
                    act.activation(rstd[:, :], ps[:, 6, :], ACT.Copy).then_inc(rstd_copied, 1)
                else:
                    act.activation(rstd_q, ps[:, 0, 0:NX], ACT.Copy).then_inc(rstd_copied, 1)

            for g in range(FN_GROUPS):
                act.wait_ge(fn_a, g + 1)
                act.activation(ab[:, g % 2, :, :], ps[:, 4:6, 0:2 * P], ACT.Copy).then_inc(fn_ab, 1)
                act.wait_ge(fn_c, g + 1)
                act.activation(ysb[:, 4 + g, 0, :], ps[:, 7, 0:NX], ACT.Copy).then_inc(y2_hi, 1)

            def attend(first, heads, scale, local):
                def exps2(hd):
                    for qt in range(2):
                        u = 2 * (first + hd) + qt
                        if local:
                            act.wait_ge(s2_ready, u + 1)
                            act.activation(p2[:, hd % 2, qt, NX:2 * NX], ps[:, score_bank2(hd, qt), NX:2 * NX], ACT.Copy,
                                           scale=scale).then_inc(s2_half, 1)
                    for qt in range(2):
                        u = 2 * (first + hd) + qt
                        act.wait_ge(nmax2_ready, u + 1)
                        src = p2[:, hd % 2, qt, :] if local else ps[:, score_bank2(hd, qt), :]
                        act.activation(p2[:, hd % 2, qt, :], src, ACT.Exp, bias=att[:, 0, u % 16:u % 16 + 1],
                                       scale=1.0 if local else scale,
                                       accum_out=att[:, 1, u % 16:u % 16 + 1]).then_inc(exp2_ready, 1)

                def take_pt2(hd):
                    n = first + hd
                    act.wait_ge(pt2_psum, n + 1)
                    if n >= 1:
                        act.wait_ge(o2_ready, n)
                    for qt in range(2):
                        ins = act.activation(pt2[:, :, qt * P:qt * P + P],
                                             ps[:, 6 + qt, :].rearrange("p (k n) -> p k n", k=4), ACT.Copy)
                    ins.then_inc(pt2_ready, 1)

                def take_y2(hd):
                    act.wait_ge(o2_ready, first + hd + 1)
                    y = ysb[:, hd, 0, :] if local else ysa[:, hd, 0, :]
                    act.activation(y, ps[:, hd % 2, 0:NX], ACT.Copy).then_inc(y2_hi, 1)

                exps2(0)
                for hd in range(heads):
                    if hd + 1 < heads:
                        exps2(hd + 1)
                    take_pt2(hd)
                    if hd >= 1:
                        take_y2(hd - 1)
                take_y2(heads - 1)

            attend(0, NA_HEADS, NA_SCALE, True)
            norm_hi("kv", lambda b: ckvs[:, 2 * b:2 * b + 2, 0, :])
            norm_hi("q", lambda b: cqs[:, :, 0, :])
            plain(LY["uk"])
            plain(LY["uv"])
            residual(LY["uq"])
            attend(NA_HEADS, HEADS, MLA_SCALE, False)

            load_sqrt()
            residual(LY["out2"], sums=True)
            token_std("ffn2")
            norm_hi("ffn2", lambda b: hs[:, 4 * b:4 * b + 4, 0, :], lambda k: mod[:, 48 + k:49 + k])
            for part in "abc":
                ly = LY["up2" + part]
                gated(ly, lambda t: cv[:, t, 2, :],
                      lambda it, t, ly=ly: (cv_step, (HID[ly.name] - HID["up2a"]) * 6 + it * 12 + 5 + t))
                if part == "c":
                    load_sqrt()
                residual(LY["dn2" + part], sums=part == "c")
            token_std("final2")

        @block.tensor
        def _(pe):
            def weights(ly, it, hf, j):
                k = ly.base + hf * ly.c + j
                pe.wait_ge(lo_done, k + 5 + it * ly.cpi)
                return k % RING if ly.loop else (k + it * ly.cpi) % RING

            def wide(ly, it, hf, xs, x_ready=None, width=HW):
                kk = CW // width
                last_k = ly.c * kk - 1
                for j in range(ly.c):
                    slot = weights(ly, it, hf, j)
                    if x_ready is not None:
                        pe.wait_ge(*x_ready(j))
                    for t in range(ly.tiles):
                        bank = (2 * hf + t) % 4
                        if j == 0:
                            pe.wait_ge(bank_free, ly.tbase + 2 * hf + t + 1 + it * ly.tpi)
                        both = ps[:, bank, :].rearrange("p (a n) -> p a n", a=2)
                        for k in range(kk):
                            kt = j * kk + k
                            w = slice(k * width + t * P, k * width + t * P + P)
                            pair, x_hi = xs(kt)
                            if kt == last_k:
                                pe.matmul(ps[:, bank, 0:NX], lo[:, slot, w], x_hi, start=False, stop=False)
                            ins = pe.matmul(both, hi[:, slot, w], pair, start=kt == 0, stop=kt == last_k)
                            if kt != last_k:
                                ins = pe.matmul(ps[:, bank, 0:NX], lo[:, slot, w], x_hi, start=False, stop=False)
                    ins.then_inc(chunk_used, 1)

            def triple(ly, it, hf, n, xs, x_ready=None, width=HW):
                kk = CW // width
                last_k = ly.c * kk - 1
                for j in range(ly.c):
                    slot = weights(ly, it, hf, j)
                    if x_ready is not None:
                        pe.wait_ge(*x_ready(j))
                    for t in range(ly.tiles):
                        bank = (2 * hf + t) % 4
                        if j == 0:
                            pe.wait_ge(bank_free, ly.tbase + 2 * hf + t + 1 + it * ly.tpi)
                        for k in range(kk):
                            kt = j * kk + k
                            w = slice(k * width + t * P, k * width + t * P + P)
                            x_hi, x_lo = xs(kt)
                            acc_ = ps[:, bank, 0:n]
                            if len(x_hi.shape) == 3:
                                acc_ = acc_.rearrange("p (a n) -> p a n", a=2)
                            pe.matmul(acc_, hi[:, slot, w], x_hi, start=kt == 0, stop=False)
                            pe.matmul(acc_, hi[:, slot, w], x_lo, start=False, stop=False)
                            ins = pe.matmul(acc_, lo[:, slot, w], x_hi, start=False, stop=kt == last_k)
                    ins.then_inc(chunk_used, 1)

            def by_token(ly, hf, xs):
                banks = range(4 * (hf % 2), 4 * (hf % 2) + 4)
                if hf >= 2:
                    pe.wait_ge(bank_free, ly.tbase + 4 * (hf - 1) + 4)
                for j in range(ly.c):
                    slot = weights(ly, 0, hf, j)
                    for t, bank in enumerate(banks):
                        for k in range(4):
                            kt = 4 * j + k
                            w = slice(k * HW, k * HW + HW)
                            x_hi, x_lo = xs(kt, t)
                            acc_ = ps[:, bank, 0:HW]
                            pe.matmul(acc_, x_hi, hi[:, slot, w], start=kt == 0, stop=False)
                            pe.matmul(acc_, x_lo, hi[:, slot, w], start=False, stop=False)
                            ins = pe.matmul(acc_, x_hi, lo[:, slot, w], start=False, stop=kt == 4 * ly.c - 1)
                    ins.then_inc(chunk_used, 1)

            def mod_group(ly, it):
                g = ly.gbase + it
                pe.wait_ge(accf_ready, g + 2)
                pe.wait_ge(mod_done, g + 1)
                for v in range(2 if ly.ctx else 1):
                    for t in range(ly.mtiles):
                        ins = pe.matmul(ps[:, 7, 4 * v + t:4 * v + t + 1], accf[:, v, t * P:t * P + P], col("one"),
                                        start=True, stop=True)
                ins.then_inc(mod_sum, 1)

            def token_stats(name, sums, bank=4, col0=0, last=True):
                if NTH[name] >= 1:
                    pe.wait_ge(std_ready, NTH[name])
                for th, rows in token_tiles(name):
                    for i, x in enumerate(sums):
                        ins = pe.matmul(ps[0:rows, bank, col0 + th:col0 + th + 1], x[:, th * P:th * P + rows], mean[:, 0:1],
                                        start=i == 0, stop=i == len(sums) - 1)
                if last:
                    ins.then_inc(stat_ready, 1)

            def spread(name, bank):
                pe.wait_ge(inv_ready, NTH[name] + 1)
                for th, rows in token_tiles(name):
                    ins = pe.matmul(ps[:, bank, th * P:th * P + rows], tok_inv(name)[0:rows, th:th + 1].to_broadcast([rows, P]),
                                    ident[0:rows, 0:rows], start=True, stop=True)
                ins.then_inc(rstd_ready, 1)

            def residual_stats(ly, name, col0=0, sums=None, last=True):
                halves = LY[ly].its * LY[ly].halves
                pe.wait_ge(sum_added, ADD0[ly] + halves + 2)
                token_stats(name, [(ssum if sums is None else sums)[:, t, :] for t in range(2)], col0=col0, last=last)

            pe.wait_ge(tables_in, 32)
            pe.wait_ge(sq_added, 3)
            token_stats("mix", [sq[:, 0, k * N1:k * N1 + N1] for k in range(4)])
            spread("mix", 5)

            def to_z(name, first_token, x_ready=None):
                ly = LY[name]

                def body(it):
                    for hf in range(ly.halves):
                        triple(ly, it, hf, N1 - first_token,
                               lambda kt: (xs1[:, kt, 0, first_token:N1], xs1[:, kt, 1, first_token:N1]),
                               x_ready if hf == 0 else None)
                    mod_group(ly, it)
                run(pe, ly, body)

            to_z("kv1", 0, lambda j: (xs_ready, j + 1))
            triple(LY["f1"], 0, 0, N1, lambda kt: (xs1[:, kt, 0, :], xs1[:, kt, 1, :]), width=P)
            for g in range(2):
                pe.wait_ge(bank_free, 16 + 4 if g == 1 else 12 + 4)
                for kt in range(3):
                    rows = P if kt < 2 else N1 - 2 * P
                    if g == 1:
                        pe.wait_ge(vtok_ready, kt + 1)
                    for k in range(4):
                        ins = pe.transpose(ps[0:rows, 4 + kt, k * P:k * P + P],
                                           z[:, 8 + 4 * g + k, kt * P:kt * P + rows], ident)
                    ins.then_inc(vt_ready, 1)
            pe.wait_ge(bank_free, LY["q1"].tbase + 4)
            to_z("q1", NM - 2)
            to_z("conv1", NM - 2)

            pe.wait_ge(bank_free, LY["conv1"].tbase + 4)
            pe.wait_ge(vtok_ready, 6)
            pe.wait_ge(f_dve, 4)
            for qt in range(2):
                ins = pe.transpose(ps[:, 5, qt * HEADS:qt * HEADS + HEADS], fl[0:HEADS, 0, NM + qt * P:NM + qt * P + P],
                                   ident[0:HEADS, 0:HEADS])
            ins.then_inc(cq_psum, 1)

            def score_bank(hd, qt):
                return (4 if hd % 2 == 0 else 2) + qt

            def scores(hd):
                pick = ident[0:HEADS, hd:hd + 1]
                for qt in range(2):
                    q0 = NM + qt * P
                    if hd == 0:
                        pe.wait_ge(cq_ready, 1)
                    elif hd == 1:
                        pe.wait_ge(bank_free, LY["out1"].tbase + 4)
                    else:
                        pe.wait_ge(s_taken, 2 * (hd - 2) + qt + 1)
                    s = ps[:, score_bank(hd, qt), 0:N1]
                    pe.matmul(s, z[:, 16 + hd, q0:q0 + P], z[:, hd, :], start=True, stop=False)
                    pe.matmul(s, pick.to_broadcast([HEADS, P]), fl[0:HEADS, 2, :], start=False, stop=True)\
                      .then_inc(s_ready, 1)

            def transposed(hd):
                pe.wait_ge(p_ready, 2 * hd + 2)
                if hd == 0:
                    pe.wait_ge(mod_done, LY["out1"].gbase + 1)
                else:
                    pe.wait_ge(pt_ready, hd)
                for qt in range(2):
                    for kt in range(2):
                        pe.transpose(ps[:, 6, kt * NX + qt * P:kt * NX + qt * P + P],
                                     p1[:, hd % 2, qt, kt * P:kt * P + P], ident)
                    ins = pe.transpose(ps[0:NM, 7, qt * P:qt * P + P], p1[:, hd % 2, qt, 2 * P:N1], ident)
                ins.then_inc(pt_psum, 1)

            def mix(hd):
                pe.wait_ge(pt_ready, hd + 1)
                if hd >= 1:
                    pe.wait_ge(y_ready, hd)
                for kt in range(3):
                    rows = P if kt < 2 else N1 - 2 * P
                    ins = pe.matmul(ps[:, 0, 0:NX], vtok[0:rows, kt, hd * P:hd * P + P], pt1[0:rows, kt, :],
                                    start=kt == 0, stop=kt == 2)
                ins.then_inc(o_ready, 1)

            def group_stats(hd):
                pe.wait_ge(gn_sq, hd + 1)
                for a in range(2):
                    e0 = TABS["e31"][0] + 15 - (8 * a + hd)
                    ins = pe.matmul(ps[0:16, 1, 0:NX], tabs[:, e0:e0 + 16], gsq(hd)[:, a, :],
                                    start=hd == 0 and a == 0, stop=hd == HEADS - 1 and a == 1)
                ins.then_inc(gn_stat, 1)

            scores(0)
            scores(1)
            for hd in range(HEADS):
                transposed(hd)
                if hd + 2 < HEADS:
                    scores(hd + 2)
                mix(hd)
                if hd >= 1:
                    group_stats(hd - 1)
            group_stats(HEADS - 1)
            pe.wait_ge(gn_r, 1)
            pe.wait_ge(s_taken, 2 * HEADS)
            for g in range(16):
                if g >= 2:
                    pe.wait_ge(gn_y, g - 1)
                pe.matmul(ps[:, 2 + g % 2, 0:NX], ident[0:16, g:g + 1].to_broadcast([16, P]), rstd[0:16, 0:NX],
                          start=True, stop=True).then_inc(gn_bc, 1)

            def project(ly, xs, x_ready=None, mods=True):
                def body(it):
                    for hf in range(ly.halves):
                        wide(ly, it, hf, xs, x_ready if hf == 0 else None)
                    if ly.mod and mods:
                        mod_group(ly, it)
                run(pe, ly, body)

            def pair_of(x):
                return lambda kt: (x[:, kt, :, :], x[:, kt, 0, :])

            pe.wait_ge(y_ready, HEADS)
            pe.wait_ge(gn_y, 16)
            ly = LY["out1"]

            def body(it, ly=ly):
                for hf in range(ly.halves):
                    triple(ly, it, hf, NX, lambda kt: (ys1[:, kt, 0, :], ys1[:, kt, 1, :]),
                           (lambda j: (gn_ready, j + 1)) if hf == 0 else None)
                mod_group(ly, it)
            run(pe, ly, body)
            residual_stats("out1", "ffn1")
            spread("ffn1", 5)

            def gated_part(tag, part, first_batch):
                project(LY["up" + tag + part], pair_of(hs), lambda j: (xs_ready, first_batch + j + 1))

            def down_part(tag, part):
                up = LY["up" + tag + part]
                project(LY["dn" + tag + part], pair_of(hid), lambda j: (hid_ready, HID[up.name] + 4 * j + 4))

            for part in "abc":
                gated_part("1", part, SPLIT["ffn1"])
                if part == "c":
                    spread("ctx", 6)
                if part == "b":
                    pe.wait_ge(csq_added, 4 + 1)
                    token_stats("ctx", [csum[:, k, :] for k in range(4)])
                down_part("1", part)

            residual_stats("dn1c", "final1", last=False)
            for th in range(2):
                for t in range(2):
                    ins = pe.matmul(ps[:, 4, 2 + th:3 + th], gsum[:, t, th * P:th * P + P], mean[:, 0:1],
                                    start=t == 0, stop=t == 1)
            ins.then_inc(stat_ready, 1)
            spread("final1", 5)
            pe.wait_ge(cx_done, 8)
            spread("attn2", 6)
            ly = LY["joint"]
            pe.wait_ge(bank_free, ly.tbase + 4)

            def both_of(kt):
                return hs2[:, :, kt, 0, :], hs2[:, :, kt, 1, :]

            def body(it, ly=ly):
                for hf in range(2):
                    triple(ly, it, hf, 2 * NX, both_of, lambda j: (xs_ready, SPLIT["attn2"] + j + 1))
                mod_group(ly, it)
            run(pe, ly, body)
            triple(LY["kr"], 0, 0, 2 * NX, both_of, width=P)
            pe.wait_ge(bank_free, LY["xonly"].tbase + 4)
            project(LY["xonly"], lambda kt: (hs2[:, 0, kt, :, :], hs2[:, 0, kt, 0, :]))
            pe.wait_ge(kvsq_ready, 1)
            token_stats("kv", [kvsq[:, k, :] for k in range(4)])
            pe.wait_ge(bank_free, LY["vn"].tbase + 4)

            def tokens_of(kt, t):
                x = hs2[:, t // 2, kt, :, (t % 2) * P:(t % 2) * P + P]
                return x[:, 0, :], x[:, 1, :]

            pe.wait_ge(mod_done, MOD_GROUPS + 1)
            by_token(LY["vn"], 0, tokens_of)
            pe.wait_ge(qsq_ready, 1)
            token_stats("q", [sq[:, 1, k * NX:k * NX + NX] for k in range(4)], 7)
            spread("kv", 6)
            pe.wait_ge(std_ready, NTH["q"] + 1)
            pe.wait_ge(rstd_copied, 1)
            by_token(LY["vn"], 1, tokens_of)
            pe.wait_ge(bank_free, LY["vn"].tbase + 4 + 4)
            spread("q", 0)
            pe.wait_ge(late_in, 48)
            pe.wait_ge(bank_free, LY["uk"].tbase + 4)

            def fourier_features(g):
                if g >= 1:
                    pe.wait_ge(fn_ab, g)
                for lt in range(2):
                    ins = pe.matmul(ps[:, 4 + lt, 0:2 * P], zx[:, 8 + g, lt * P:lt * P + P], tab("dft_c"),
                                    start=True, stop=True)
                ins.then_inc(fn_a, 1)

            fourier_features(0)
            for g in range(FN_GROUPS):
                if g + 1 < FN_GROUPS:
                    fourier_features(g + 1)
                pe.wait_ge(fn_ab, g + 1)
                if g >= 1:
                    pe.wait_ge(fn_sp, g)
                n = 0
                for part, table in ((0, dft_lc), (1, dft_ls)):
                    for lt in range(2):
                        ins = pe.matmul(ps[:, 6, 0:NX], ab[:, g % 2, lt, part * P:part * P + P], table[:, lt, :],
                                        start=n == 0, stop=n == 3)
                        n += 1
                ins.then_inc(fn_b, 1)
                pe.wait_ge(fn_sp, g + 1)
                if g >= 1:
                    pe.wait_ge(y2_ready, g)
                pe.matmul(ps[:, 7, 0:NX], wfn[:, g, :], sp[:, g % 2, :], start=True, stop=True).then_inc(fn_c, 1)

            def attend(first, heads, score_terms, values, y0):
                def scores2(hd):
                    for qt in range(2):
                        u = 2 * (first + hd) + qt
                        if hd >= 2:
                            pe.wait_ge(exp2_ready, u - 3)
                        terms = score_terms(hd, qt)
                        for i, (q, k) in enumerate(terms):
                            ins = pe.matmul(ps[:, score_bank2(hd, qt), :], q, k, start=i == 0, stop=i == len(terms) - 1)
                        ins.then_inc(s2_ready, 1)

                def transposed2(hd):
                    n = first + hd
                    pe.wait_ge(p2_ready, 2 * n + 2)
                    if n >= 1:
                        pe.wait_ge(pt2_ready, n)
                    for qt in range(2):
                        for kt in range(4):
                            ins = pe.transpose(ps[:, 6 + qt, kt * P:kt * P + P],
                                               p2[:, hd % 2, qt, kt * P:kt * P + P], ident)
                    ins.then_inc(pt2_psum, 1)

                def mix2(hd):
                    pe.wait_ge(pt2_ready, first + hd + 1)
                    if hd >= 2:
                        pe.wait_ge(y2_ready, y0 + hd - 1)
                    for kt in range(4):
                        ins = pe.matmul(ps[:, hd % 2, 0:NX], values[:, kt, hd * P:hd * P + P], pt2[:, kt, :],
                                        start=kt == 0, stop=kt == 3)
                    ins.then_inc(o2_ready, 1)

                scores2(0)
                scores2(1)
                for hd in range(heads):
                    transposed2(hd)
                    if hd + 2 < heads:
                        scores2(hd + 2)
                    mix2(hd)

            pe.wait_ge(rstd_copied, 2)
            pe.wait_ge(y2_ready, FN_GROUPS)
            attend(0, NA_HEADS, lambda hd, qt: [(zx[:, 4 + hd, qt * P:qt * P + P], zj[:, 4 + hd, :])], vn, FN_GROUPS)
            pe.wait_ge(y2_ready, FN_GROUPS + NA_HEADS)
            for hf in range(4):
                triple(LY["uk"], 0, hf, 2 * NX, lambda kt: (ckvs[:, kt, 0, :], ckvs[:, kt, 1, :]),
                       lambda j: (xs_ready, SPLIT["kv"] + 2))
            pe.wait_ge(bank_free, LY["uv"].tbase + 4)
            for hf in range(4):
                by_token(LY["uv"], hf, lambda kt, t: (ckvs[:, kt, 0, t * P:t * P + P], ckvs[:, kt, 1, t * P:t * P + P]))
            pe.wait_ge(bank_free, LY["uq"].tbase + 4)
            project(LY["uq"], pair_of(cqs), lambda j: (xs_ready, SPLIT["q"] + 1))
            pe.wait_ge(bank_free, LY["out2"].tbase + 4)
            for j in range(4):
                pe.matmul(ps[:, 4 + j // 2, (j % 2) * NX:(j % 2) * NX + NX], tab("swap"), qr_m[:, j, :],
                          start=True, stop=True)
            pe.matmul(ps[:, 6, 0:NX], tab("swap"), kr[:, 0:NX], start=True, stop=True).then_inc(rot_psum, 1)
            pe.wait_ge(rope_ready, 6)
            attend(NA_HEADS, HEADS,
                   lambda hd, qt: [(qn_m[:, hd, qt * P:qt * P + P], kn_m[:, hd, :]),
                                   (qr_m[:, hd // 2, qt * P:qt * P + P], krm[:, hd % 2, :])],
                   vt_m, FN_GROUPS + NA_HEADS)
            pe.wait_ge(y2_ready, FN_GROUPS + NA_HEADS + HEADS)

            def mixed(kt):
                y = ysa[:, kt] if kt < 8 else ysb[:, kt - 8]
                return y[:, :, :], y[:, 0, :]

            project(LY["out2"], mixed)
            residual_stats("out2", "ffn2")
            spread("ffn2", 5)
            for part in "abc":
                gated_part("2", part, SPLIT["ffn2"])
                down_part("2", part)
            residual_stats("dn2c", "final2")
            spread("final2", 5)

        @block.vector
        def _(dve):
            def split_lo(v, slot):
                dve.wait_ge(hi_done, v + 1)
                dve.tensor_tensor(lo[:, slot, :], raw[:, slot, :], hi[:, slot, :].bitcast(F32), ALU.subtract)\
                   .then_inc(lo_done, 1)

            def mod_chunk(ly, it, m):
                n = ly.mbase + m + it * len(ly.mod_at)
                dve.wait_ge(wm_full[m % 2], 16 * ((ly.mbase + m) // 2 + 1 + it * (len(ly.mod_at) // 2)))
                width = 2 * HW if ly.ctx else HW
                for i in range(4):
                    k, v = (i // 2, i % 2) if ly.ctx else (i, 0)
                    kt = (2 if ly.ctx else 4) * m + k
                    w = wm[:, m % 2, k * width:k * width + width]
                    a = acc[:, i % 2, 0:width]
                    c = csilu[:, v * KT + kt:v * KT + kt + 1]
                    if m == 0 and i < 2:
                        dve.wait_ge(accf_ready, ly.gbase + 1 + it)
                        ins = dve.tensor_scalar(a, w, c, None, ALU.mult)
                    else:
                        if i == 1:
                            dve.wait_ge(wm_used, n + 2)
                        else:
                            dve.wait_ge(wm_op, 3 * n + (0 if i == 0 else i - 1))
                        ins = dve.scalar_tensor_tensor(a, w, c, a, ALU.mult, ALU.add)
                    ins.then_inc(wm_used if i == 3 else wm_op, 1)

            def mod_hand_over(ly, it):
                dve.wait_ge(mod_sum, ly.gbase + it + 1)
                dve.wait_ge(wm_used, ly.mbase + (it + 1) * 4 + 2)
                dve.tensor_tensor(accf[:, 0, 0:HW], acc[:, 0, 0:HW], acc[:, 1, 0:HW], ALU.add).then_inc(accf_ready, 1)

            def mod_take(ly, it):
                n, b0 = ly.mtiles, COLS["b_mod"][0]
                dve.wait_ge(mod_sum, ly.gbase + it + 2)
                bias = cols[:, bass.ds(it * n + ly.mtbase + b0, n)]
                if ly.ctx:
                    dve.tensor_tensor(modx[:, bass.ds(it * n + ly.mtbase, n)], ps[:, 7, 4:4 + n], bias, ALU.add)
                dve.tensor_tensor(mod[:, bass.ds(it * n + ly.mtbase, n)], ps[:, 7, 0:n], bias, ALU.add).then_inc(mod_done, 1)

            def prepare(ly, it, hf):
                for j in range(ly.c):
                    a = ahead(ly, it, hf, j)
                    if a is not None:
                        split_lo(a[0], a[1])
                    if hf * ly.c + j in ly.mod_at:
                        m = ly.mod_at.index(hf * ly.c + j)
                        mod_chunk(ly, it, m)
                        if m == 3 and not ly.ctx:
                            mod_hand_over(ly, it)

            def add_half(ly, it, hf, t, dst, sem_after=True):
                bank = (2 * hf + t) % 4
                dve.wait_ge(tmp_ready, CONCAT[ly.name] + it * ly.tpi + 2 * hf + t + 1)
                dve.tensor_tensor(dst, ps[:, bank, 0:NX], tmp[:, bank, :], ALU.add).then_inc(bank_free, 1)

            def whole(ly, it, hf, t):
                return ly.tbase + it * ly.tpi + 2 * hf + t + 5

            def token_inv(name):
                dve.wait_ge(std_ready, NTH[name] + 1)
                for rows, c0, c1 in token_columns(name):
                    ins = dve.reciprocal(tok_inv(name)[0:rows, c0:c1], tok_std(name)[0:rows, c0:c1])
                ins.then_inc(inv_ready, 1)

            def norm_apply(name, rs, src, gain, dst_hi, dst_lo, shift=None, before=None):
                n, batches, tiles = NORMS[name]
                dve.wait_ge(rstd_ready, NTH[name] + 1)
                if SPLIT[name]:
                    dve.wait_ge(xs_ready, SPLIT[name])

                def view(b):
                    return xn[:, b % 2, 0:tiles * n].rearrange("p (k n) -> p k n", k=tiles)

                def scale(b):
                    for k in range(tiles):
                        if before is not None:
                            before(b * tiles + k)
                        ins = dve.scalar_tensor_tensor(view(b)[:, k, :], src(b * tiles + k), gain(b * tiles + k), rs,
                                                       ALU.mult, ALU.mult)
                    ins.then_inc(xn_ready, 1)

                def rest(b):
                    dve.wait_ge(xs_hi, SPLIT[name] + b + 1)
                    if shift is None:
                        ins = dve.tensor_tensor(dst_lo(b), view(b), dst_hi(b).bitcast(F32), ALU.subtract)
                    else:
                        for k in range(tiles):
                            ins = dve.scalar_tensor_tensor(dst_lo(b)[:, k, :], view(b)[:, k, :], shift(b * tiles + k),
                                                           dst_hi(b)[:, k, :].bitcast(F32), ALU.add, ALU.subtract)
                    ins.then_inc(xs_ready, 1)

                scale(0)
                for b in range(batches):
                    if b + 1 < batches:
                        if b >= 1:
                            dve.wait_ge(xs_ready, SPLIT[name] + b)
                        scale(b + 1)
                    rest(b)

            dve.memset(att[:, 0, :], 0.0).then_inc(lo_done, RING)
            dve.memset(att[:, 1, :], 0.0).then_inc(chunk_used, RING)
            dve.memset(att[:, 2, :], 0.0).then_inc(bank_free, 4)
            dve.memset(mod[:, 0:1], 0.0).then_inc(wm_used, 2)
            dve.memset(mod[:, 1:2], 0.0).then_inc(mod_sum, 1)
            dve.memset(mod[:, 2:3], 0.0).then_inc(mod_done, 1)
            dve.memset(mod[:, 3:4], 0.0).then_inc(accf_ready, 1)
            dve.memset(mod[:, 4:5], 0.0).then_inc(sum_sq, 1)

            for b in range(1, 4):
                dve.wait_ge(sq_ready, b + 1)
                if b >= 2:
                    dve.wait_ge(sq_added, b - 1)
                dve.tensor_tensor(sq[:, 0, :], sq[:, 0, :], sq[:, 1, :], ALU.add).then_inc(sq_added, 1)
            token_inv("mix")
            dve.wait_ge(tables_in, 32)
            norm_apply("mix", ps[:, 5, 0:N1], lambda k: h[:, k, :], lambda k: col("norm_mix", k),
                       lambda b: xs1[:, 4 * b:4 * b + 4, 0, :], lambda b: xs1[:, 4 * b:4 * b + 4, 1, :])
            for v in range(RING):
                split_lo(v, v)
            dve.wait_ge(silu_c_done, 1)
            def only_prepare(ly):
                def body(it):
                    for hf in range(ly.halves):
                        prepare(ly, it, hf)
                    mod_take(ly, it)
                run(dve, ly, body)

            only_prepare(LY["kv1"])
            prepare(LY["f1"], 0, 0)
            dve.wait_ge(chunk_used, last_chunk(LY["f1"], 0, 0) + 5)
            dve.tensor_scalar(fl[0:HEADS, 0, :], ps[0:HEADS, 0, 0:N1],
                              cols[0:HEADS, COLS["b_f"][0]:COLS["b_f"][0] + 1], None, ALU.add).then_inc(bank_free, 1)
            dve.wait_ge(f_act, 3)
            dve.wait_ge(bank_free, LY["q1"].tbase + 4)
            dve.scalar_tensor_tensor(fl[0:HEADS, 2, :], fl[0:HEADS, 0, :], 0.0, fl[0:HEADS, 1, :], ALU.min, ALU.subtract)\
               .then_inc(f_dve, 1)
            dve.wait_ge(f_dve, 1)
            dve.memset(fl[0:HEADS, 1, :], 0.0).then_inc(f_dve, 1)
            dve.wait_ge(f_dve, 2)
            dve.tensor_tensor_scan(fl[0:HEADS, 0, :], fl[0:HEADS, 2, :], fl[0:HEADS, 1, :], 0.0, ALU.add, ALU.add)\
               .then_inc(f_dve, 1)
            dve.wait_ge(f_dve, 3)
            dve.tensor_scalar(fl[0:HEADS, 2, :], fl[0:HEADS, 0, :], -1.0, None, ALU.mult).then_inc(f_dve, 1)

            only_prepare(LY["q1"])
            only_prepare(LY["conv1"])

            def conv_group(g):
                n = 1 + 4 * g
                dst = z[:, 40 + g, 0:NX]
                u = z[:, 32 + g, NM - 2:N1]
                if g == 0:
                    dve.wait_ge(bank_free, LY["out1"].tbase + 4)
                dve.tensor_tensor(u, u, z[:, 40 + g, NM - 2:N1], ALU.mult).then_inc(conv_step, 1)
                dve.wait_ge(conv_step, n)
                dve.tensor_scalar(dst, z[:, 32 + g, NM - 2:N1 - 2], col("conv1", g), None, ALU.mult).then_inc(conv_step, 1)
                dve.wait_ge(conv_step, n + 1)
                dve.scalar_tensor_tensor(dst, z[:, 32 + g, NM - 1:N1 - 1], col("conv1", 8 + g), dst, ALU.mult, ALU.add)\
                   .then_inc(conv_step, 1)
                dve.wait_ge(conv_step, n + 2)
                dve.scalar_tensor_tensor(dst, z[:, 32 + g, NM:N1], col("conv1", 16 + g), dst, ALU.mult, ALU.add)\
                   .then_inc(conv_step, 1)
                dve.wait_ge(conv_step, n + 3)
                dve.tensor_tensor(z[:, 24 + g, NM:N1], dst, z[:, 24 + g, NM:N1], ALU.mult).then_inc(conv_ready, 1)

            dve.wait_ge(cq_psum, 1)
            dve.tensor_copy(cq[:, :, :], ps[:, 5, 0:2 * HEADS].rearrange("p (a n) -> p a n", a=2)).then_inc(cq_ready, 1)
            dve.wait_ge(cq_ready, 1)

            def masked(hd):
                for qt in range(2):
                    u = 2 * hd + qt
                    dve.wait_ge(s_ready, u + 1)
                    dve.scalar_tensor_tensor(p1[:, hd % 2, qt, :], ps[:, (4 if hd % 2 == 0 else 2) + qt, 0:N1],
                                             cq[:, qt, hd:hd + 1], causal[:, qt, :], ALU.add, ALU.add).then_inc(s_taken, 1)
                for qt in range(2):
                    u = 2 * hd + qt
                    dve.wait_ge(s_taken, u + 1)
                    dve.tensor_reduce(att[:, 0, u:u + 1], p1[:, hd % 2, qt, :], AX_X, ALU.max, negate=True)\
                       .then_inc(max_ready, 1)

            def normalised(hd):
                for qt in range(2):
                    u = 2 * hd + qt
                    dve.wait_ge(exp_ready, u + 1)
                    dve.reciprocal(att[:, 2, u:u + 1], att[:, 1, u:u + 1]).then_inc(rsum_ready, 1)
                for qt in range(2):
                    u = 2 * hd + qt
                    dve.wait_ge(rsum_ready, u + 1)
                    dve.tensor_scalar(p1[:, hd % 2, qt, :], p1[:, hd % 2, qt, :], att[:, 2, u:u + 1], None, ALU.mult)\
                       .then_inc(p_ready, 1)

            masked(0)
            for hd in range(HEADS):
                if hd + 1 < HEADS:
                    masked(hd + 1)
                normalised(hd)
                conv_group(hd)
            dve.wait_ge(gn_std, 1)
            dve.reciprocal(rstd[0:16, 0:NX], std[0:16, 0:NX]).then_inc(gn_r, 1)

            def gn_rest(b):
                dve.wait_ge(gn_hi, b + 1)
                dve.tensor_tensor(ys1[:, 4 * b:4 * b + 4, 1, :], xn[:, b % 2, 0:4 * NX].rearrange("p (k n) -> p k n", k=4),
                                  ys1[:, 4 * b:4 * b + 4, 0, :].bitcast(F32), ALU.subtract).then_inc(gn_ready, 1)

            for b in range(4):
                if b >= 2:
                    dve.wait_ge(gn_ready, b - 1)
                for k in range(4):
                    g = 4 * b + k
                    dve.wait_ge(gn_bc, g + 1)
                    dve.scalar_tensor_tensor(xn[:, b % 2, k * NX:k * NX + NX], z[:, 16 + g, NM:N1], col("out_gain", g),
                                             ps[:, 2 + g % 2, 0:NX], ALU.mult, ALU.mult).then_inc(gn_y, 1)
                    if b >= 1 and k == 1:
                        gn_rest(b - 1)
            gn_rest(3)

            def residual(ly, gate=None, sums=False, gsums=False, before=None, after=None, finish=None, free=None):
                halves = ly.its * ly.halves

                def body(it):
                    for hf in range(ly.halves):
                        if before is not None:
                            before(it, hf)
                        prepare(ly, it, hf)
                        if after is not None:
                            after(it, hf)
                        if sums:
                            add_last(it * ly.halves + hf, (hf + 1) % 2)
                        if ly.name == "out1":
                            dve.wait_ge(chunk_used, last_chunk(ly, it, hf) + 5)
                            for t in range(2):
                                hk = h[:, bass.ds(it * ly.tpi + 2 * hf + t, 1), NM:N1].rearrange("p a n -> p (a n)")
                                dve.tensor_tensor(hk, ps[:, (2 * hf + t) % 4, 0:NX], hk, ALU.add).then_inc(bank_free, 1)
                            continue
                        for t in range(2):
                            add_half(ly, it, hf, t, tmp[:, (2 * hf + t) % 4, :])
                        for t in range(2):
                            n = 2 * hf + t
                            hk = h[:, bass.ds(it * ly.tpi + n, 1), NM:N1].rearrange("p a n -> p (a n)")
                            dve.wait_ge(bank_free, whole(ly, it, hf, t))
                            if gate is None:
                                ins = dve.tensor_tensor(hk, tmp[:, n % 4, :], hk, ALU.add)
                            else:
                                ins = dve.scalar_tensor_tensor(hk, tmp[:, n % 4, :], mod[:, bass.ds(it * ly.tpi + gate + n, 1)],
                                                               hk, ALU.mult, ALU.add)
                            ins.then_inc(res_done, 1)
                        if finish is not None:
                            finish(it, hf)
                    if ly.mod:
                        mod_take(ly, it)

                def add_last(n, slot):
                    dve.wait_ge(sum_sq, SUMS[ly.name] + n + 1)
                    dve.wait_ge(sum_added, ADD0[ly.name] + n + 1)
                    if gsums:
                        dve.tensor_tensor(gsum[:, :, :], gsum[:, :, :], gsqb[:, slot, :, :], ALU.add)
                    dve.tensor_tensor(ssum[:, :, :], ssum[:, :, :], sqb[:, slot, :, :], ALU.add).then_inc(sum_added, 1)

                if sums:
                    if free is not None:
                        dve.wait_ge(*free)
                    if gsums:
                        dve.memset(gsum[:, :, :], 0.0)
                        dve.memset(gsqb[:, 1, :, :], 0.0)
                    dve.memset(ssum[:, :, :], 0.0)
                    dve.memset(sqb[:, 1, :, :], 0.0).then_inc(sum_added, 1)
                run(dve, ly, body)
                if sums:
                    add_last(halves, 1)

            def hidden(ly, it, ready):
                for t in range(2):
                    n = HID[ly.name] + it * 2 + t
                    s, v, value = ready(t)
                    dve.wait_ge(s, v)
                    dve.wait_ge(sg_ready, n + 1)
                    dve.tensor_tensor(hv[:, t, :], value, sg[:, t, :], ALU.mult).then_inc(hv_ready, 1)
                for t in range(2):
                    n = HID[ly.name] + it * 2 + t
                    part = hid[:, bass.ds(it * 2 + t, 1), :, :].rearrange("p a b n -> p (a b) n")
                    dve.wait_ge(hid_hi, n + 1)
                    dve.tensor_tensor(part[:, 1, :], hv[:, t, :], part[:, 0, :].bitcast(F32), ALU.subtract)\
                       .then_inc(hid_ready, 1)

            residual(LY["out1"], sums=True, free=(gn_ready, 4))
            token_inv("ffn1")
            norm_apply("ffn1", ps[:, 5, 0:NX], lambda k: hx[:, k, :], lambda k: col("norm_ffn", k),
                       lambda b: hs[:, 4 * b:4 * b + 4, 0, :], lambda b: hs[:, 4 * b:4 * b + 4, 1, :])

            def gated1(part):
                ly = LY["up1" + part]

                def body(it):
                    prepare(ly, it, 0)
                    for t in range(2):
                        add_half(ly, it, 0, t, gt[:, t, :])
                    prepare(ly, it, 1)
                    for t in range(2):
                        add_half(ly, it, 1, t, ut[:, t, :])
                    hidden(ly, it, lambda t: (bank_free, whole(ly, it, 1, t), ut[:, t, :]))
                    mod_take(ly, it)
                run(dve, ly, body)

            gated1("a")
            dve.memset(csum[:, :, :], 0.0).then_inc(csq_added, 1)

            def add_ctx(it, hf):
                if hf == 1:
                    dve.wait_ge(csq_added, it + 1)
                    dve.wait_ge(csq_ready, it + 1)
                    dve.tensor_tensor(csum[:, :, :], csum[:, :, :], csq[:, :, :], ALU.add).then_inc(csq_added, 1)

            residual(LY["dn1a"], finish=add_ctx)
            gated1("b")
            residual(LY["dn1b"])
            token_inv("ctx")
            gated1("c")

            dve.wait_ge(mod_done, LY["joint"].gbase + 1)
            dve.scalar_tensor_tensor(gm[:, 0, :], mod[:, KT:2 * KT], 1.0, col("g_attn", 0, KT), ALU.add, ALU.mult)\
               .then_inc(gm_done, 1)
            dve.scalar_tensor_tensor(gm[:, 1, :], modx[:, KT:2 * KT], 1.0, col("g_attn", 0, KT), ALU.add, ALU.mult)\
               .then_inc(gm_done, 1)
            dve.scalar_tensor_tensor(gm[:, 2, :], mod[:, 4 * KT:5 * KT], 1.0, col("g_ffn", 0, KT), ALU.add, ALU.mult)\
               .then_inc(gm_done, 1)
            dve.wait_ge(gm_done, 3)
            dve.wait_ge(rstd_ready, NTH["ctx"] + 1)

            def one(x, n):
                return x[:, bass.ds(n, 1), :].rearrange("p a n -> p (a n)")

            def ctx_scale(it, hf):
                for t in range(2):
                    n = it * LY["dn1c"].tpi + 2 * hf + t
                    ins = dve.scalar_tensor_tensor(one(cx, n), one(cx, n), gm[:, 1, bass.ds(n, 1)], ps[:, 6, 0:NX],
                                                   ALU.mult, ALU.mult)
                ins.then_inc(cxn_ready, 1)

            def ctx_lo(it, hf):
                dve.wait_ge(cx_hi, it * LY["dn1c"].halves + hf + 1)
                for t in range(2):
                    n = it * LY["dn1c"].tpi + 2 * hf + t
                    part = hs2[:, 1, bass.ds(n, 1), :, :].rearrange("p a b n -> p (a b) n")
                    ins = dve.scalar_tensor_tensor(part[:, 1, :], one(cx, n), modx[:, bass.ds(n, 1)], part[:, 0, :].bitcast(F32),
                                                   ALU.add, ALU.subtract)
                ins.then_inc(cx_done, 1)

            residual(LY["dn1c"], sums=True, gsums=True, before=ctx_scale, after=ctx_lo)
            token_inv("final1")
            dve.wait_ge(inv_ready, NTH["final1"] + 1)
            dve.scalar_tensor_tensor(tok[:, 128:130], ps[:, 4, 2:4], 1.0 / KT, tok_inv("final1")[:, 0:2], ALU.mult, ALU.mult)\
               .then_inc(gsum_step, 1)
            dve.wait_ge(gsum_step, 1)
            dve.tensor_tensor(tok[:, 130:132], tok[:, 128:130], tok_inv("final1")[:, 0:2], ALU.mult).then_inc(gsum_step, 1)
            token_inv("attn2")

            def finish_block1(k):
                dve.scalar_tensor_tensor(hx[:, k, :], hx[:, k, :], col("final_norm", k), ps[:, 5, 0:NX], ALU.mult, ALU.mult)\
                   .then_inc(x_final, 1)
                dve.wait_ge(x_final, k + 1)

            dve.wait_ge(rstd_ready, NTH["final1"] + 1)
            norm_apply("attn2", ps[:, 6, 0:NX], lambda k: hx[:, k, :], lambda k: gm[:, 0, k:k + 1],
                       lambda b: hs2[:, 0, 4 * b:4 * b + 4, 0, :], lambda b: hs2[:, 0, 4 * b:4 * b + 4, 1, :],
                       shift=lambda k: mod[:, k:k + 1], before=finish_block1)

            def straight(ly, dst, n):
                def body(it):
                    for hf in range(ly.halves):
                        prepare(ly, it, hf)
                        dve.wait_ge(chunk_used, last_chunk(ly, it, hf) + 5)
                        for t in range(ly.tiles):
                            bank = 4 * (hf % 2) + t if ly.tiles == 4 else (2 * hf + t) % 4
                            dve.tensor_copy(dst(it, hf, t), ps[:, bank, 0:n]).then_inc(bank_free, 1)
                        if ly.name == "vn" and hf == 0:
                            token_inv("q")
                    if ly.mod:
                        mod_take(ly, it)
                run(dve, ly, body)

            def summed(ly, dst):
                def body(it):
                    for hf in range(ly.halves):
                        prepare(ly, it, hf)
                        for t in range(2):
                            add_half(ly, it, hf, t, dst(it, hf, t))
                run(dve, ly, body)

            straight(LY["joint"], lambda it, hf, t: zj[:, bass.ds(it * 4 + 2 * hf + t, 1), :].rearrange("p a n -> p (a n)"),
                     2 * NX)
            straight(LY["kr"], lambda it, hf, t: kr[:, :], 2 * NX)
            summed(LY["xonly"], lambda it, hf, t: zx[:, bass.ds(it * 4 + 2 * hf + t, 1), :].rearrange("p a n -> p (a n)"))
            token_inv("kv")
            straight(LY["vn"], lambda it, hf, t: vn[:, t, hf * HW:hf * HW + HW], HW)
            for g in range(FN_GROUPS):
                dve.wait_ge(fn_b, g + 1)
                dve.tensor_copy(sp[:, g % 2, :], ps[:, 6, 0:NX]).then_inc(fn_sp, 1)
                dve.wait_ge(y2_hi, g + 1)
                dve.tensor_tensor(ysb[:, 4 + g, 1, :], ps[:, 7, 0:NX], ysb[:, 4 + g, 0, :].bitcast(F32), ALU.subtract)\
                   .then_inc(y2_ready, 1)
            dve.wait_ge(late_in, 48)
            window = tab("na_mask").rearrange("p (a n) -> p a n", a=1).to_broadcast([P, 32, 64])
            flat = na[:, :, :, :].rearrange("p h q (a n) -> p (h q a) n", n=64)
            dve.tensor_tensor(flat, flat, window, ALU.add).then_inc(na_bias_ready, 1)

            def attend(first, heads, scale, local, y0):
                def peaks(hd):
                    for qt in range(2):
                        u = 2 * (first + hd) + qt
                        dve.wait_ge(s2_ready, u + 1)
                        if local:
                            dve.wait_ge(s2_half, u + 1)
                            dve.scalar_tensor_tensor(p2[:, hd % 2, qt, 0:NX], ps[:, score_bank2(hd, qt), 0:NX], scale,
                                                     na[:, hd, qt, :], ALU.mult, ALU.add).then_inc(s2_bias, 1)
                        else:
                            dve.tensor_reduce(att[:, 2, u % 16:u % 16 + 1], ps[:, score_bank2(hd, qt), :], AX_X, ALU.max,
                                              negate=True).then_inc(max2_ready, 1)
                    for qt in range(2):
                        u = 2 * (first + hd) + qt
                        if local:
                            dve.wait_ge(s2_bias, u + 1)
                            dve.tensor_reduce(att[:, 0, u % 16:u % 16 + 1], p2[:, hd % 2, qt, :], AX_X, ALU.max, negate=True)\
                               .then_inc(nmax2_ready, 1)
                        else:
                            dve.wait_ge(max2_ready, 2 * hd + qt + 1)
                            dve.tensor_scalar(att[:, 0, u % 16:u % 16 + 1], att[:, 2, u % 16:u % 16 + 1], scale, None, ALU.mult)\
                               .then_inc(nmax2_ready, 1)

                def normalised2(hd):
                    for qt in range(2):
                        u = 2 * (first + hd) + qt
                        dve.wait_ge(exp2_ready, u + 1)
                        dve.reciprocal(att[:, 2, u % 16:u % 16 + 1], att[:, 1, u % 16:u % 16 + 1]).then_inc(rsum2_ready, 1)
                    for qt in range(2):
                        u = 2 * (first + hd) + qt
                        dve.wait_ge(rsum2_ready, u + 1)
                        dve.tensor_scalar(p2[:, hd % 2, qt, :], p2[:, hd % 2, qt, :], att[:, 2, u % 16:u % 16 + 1], None, ALU.mult)\
                           .then_inc(p2_ready, 1)

                def rest(hd):
                    y = ysb[:, hd] if local else ysa[:, hd]
                    dve.wait_ge(y2_hi, y0 + hd + 1)
                    dve.tensor_tensor(y[:, 1, :], ps[:, hd % 2, 0:NX], y[:, 0, :].bitcast(F32), ALU.subtract)\
                       .then_inc(y2_ready, 1)

                peaks(0)
                for hd in range(heads):
                    if hd + 1 < heads:
                        peaks(hd + 1)
                    normalised2(hd)
                    if hd >= 1:
                        rest(hd - 1)
                rest(heads - 1)

            dve.wait_ge(na_bias_ready, 1)
            attend(0, NA_HEADS, NA_SCALE, True, FN_GROUPS)
            dve.wait_ge(rstd_copied, 2)
            norm_apply("kv", rstd[:, :], lambda k: zj[:, k, :], lambda k: col("g_kv", k),
                       lambda b: ckvs[:, 2 * b:2 * b + 2, 0, :], lambda b: ckvs[:, 2 * b:2 * b + 2, 1, :])
            norm_apply("q", rstd_q, lambda k: zx[:, k, :], lambda k: col("g_q", k),
                       lambda b: cqs[:, :, 0, :], lambda b: cqs[:, :, 1, :])
            straight(LY["uk"], lambda it, hf, t: kn_m[:, 2 * hf + t, :], 2 * NX)
            straight(LY["uv"], lambda it, hf, t: vt_m[:, t, hf * HW:hf * HW + HW], HW)
            dve.memset(krm[:, :, :], 0.0).then_inc(krm_zero, 1)
            summed(LY["uq"], lambda it, hf, t: qn_m[:, 2 * hf + t, :] if hf < 4 else qr_m[:, 2 * (hf - 4) + t, :])
            dve.wait_ge(rot_psum, 1)
            dve.wait_ge(bank_free, LY["out2"].tbase + 4)
            cos = tab("cos")
            sin = tab("sin")
            cos4 = cos.rearrange("p (a n) -> p a n", a=1).to_broadcast([P, 4, NX])
            sin2 = sin.rearrange("p (a n) -> p a n", a=1).to_broadcast([P, 2, NX])
            dve.tensor_tensor(rot[:, 0, :, :], qr_m[:, :, :], cos4, ALU.mult).then_inc(rot_step, 1)
            for j in range(2):
                dve.tensor_tensor(rot[:, 1, 2 * j:2 * j + 2, :], ps[:, 4 + j, :].rearrange("p (a n) -> p a n", a=2), sin2,
                                  ALU.mult).then_inc(rot_step, 1)
            dve.wait_ge(rot_step, 3)
            dve.tensor_tensor(qr_m[:, :, :], rot[:, 0, :, :], rot[:, 1, :, :], ALU.add).then_inc(rope_ready, 1)
            dve.wait_ge(rope_ready, 1)
            dve.tensor_tensor(rot[:, 0, 0, :], kr[:, 0:NX], cos, ALU.mult).then_inc(rot_step, 1)
            dve.tensor_tensor(rot[:, 1, 0, :], ps[:, 6, 0:NX], sin, ALU.mult).then_inc(rot_step, 1)
            dve.wait_ge(rot_step, 5)
            dve.wait_ge(krm_zero, 1)
            for half, rows in ((0, slice(0, 64)), (1, slice(64, 128))):
                dve.tensor_tensor(krm[rows, half, 0:NX], rot[rows, 0, 0, :], rot[rows, 1, 0, :], ALU.add).then_inc(rope_ready, 1)
                dve.tensor_copy(krm[rows, half, NX:2 * NX], kr[rows, NX:2 * NX]).then_inc(rope_ready, 1)
            dve.wait_ge(rope_ready, 5)
            dve.memset(att[:, 1, :], 0.0).then_inc(rope_ready, 1)
            attend(NA_HEADS, HEADS, MLA_SCALE, False, FN_GROUPS + NA_HEADS)

            residual(LY["out2"], gate=2 * KT, sums=True, free=(y2_ready, FN_GROUPS + NA_HEADS + HEADS))
            dve.memset(pad[:, :, 0:1], 0.0).then_inc(pads_zero, 1)
            dve.memset(pad[:, :, NX + 1:NX + 2], 0.0).then_inc(pads_zero, 1)
            token_inv("ffn2")
            norm_apply("ffn2", ps[:, 5, 0:NX], lambda k: hx[:, k, :], lambda k: gm[:, 2, k:k + 1],
                       lambda b: hs[:, 4 * b:4 * b + 4, 0, :], lambda b: hs[:, 4 * b:4 * b + 4, 1, :],
                       shift=lambda k: mod[:, 3 * KT + k:3 * KT + k + 1])
            dve.wait_ge(pads_zero, 2)
            for part in "abc":
                ly = LY["up2" + part]

                def body(it, ly=ly):
                    tile0 = (HID[ly.name] - HID["up2a"])
                    step0 = tile0 * 6
                    for hf in range(2):
                        prepare(ly, it, hf)
                        for t in range(2):
                            add_half(ly, it, hf, t, pad[:, t, 1:NX + 1])
                        for step in range(3):
                            for t in range(2):
                                c = tile0 + hf * FT + t
                                n = step0 + it * 12 + hf * 6 + 2 * step + t
                                if step == 0:
                                    dve.wait_ge(bank_free, whole(ly, it, hf, t))
                                    ins = dve.tensor_scalar(cv[:, t, 0, :], pad[:, t, 1:NX + 1], dcol("conv2_w1", it * 2 + c),
                                                            dcol("conv2_b", it * 2 + c), ALU.mult, ALU.add)
                                elif step == 1:
                                    dve.wait_ge(cv_step, n - 1)
                                    ins = dve.scalar_tensor_tensor(cv[:, t, 1, :], pad[:, t, 0:NX], dcol("conv2_w0", it * 2 + c),
                                                                   cv[:, t, 0, :], ALU.mult, ALU.add)
                                else:
                                    dve.wait_ge(cv_step, n - 1)
                                    if hf == 1:
                                        dve.wait_ge(sg_ready, HID[ly.name] + it * 2 + t + 1)
                                    ins = dve.scalar_tensor_tensor(cv[:, t, 2, :], pad[:, t, 2:NX + 2], dcol("conv2_w2", it * 2 + c),
                                                                   cv[:, t, 1, :], ALU.mult, ALU.add)
                                ins.then_inc(cv_step, 1)
                    hidden(ly, it, lambda t: (cv_step, step0 + it * 12 + 6 + 4 + t + 1, cv[:, t, 2, :]))
                run(dve, ly, body)
                residual(LY["dn2" + part], gate=5 * KT, sums=part == "c")
            token_inv("final2")
            dve.wait_ge(rstd_ready, NTH["final2"] + 1)
            for k in range(KT):
                dve.scalar_tensor_tensor(hx[:, k, :], hx[:, k, :], col("g_final", k), ps[:, 5, 0:NX], ALU.mult, ALU.mult)\
                   .then_inc(x_final, 1)


def tables():
    t = {"ident": np.eye(P), "mean": np.full((P, P), 1 / P)}
    key = np.arange(N1)[None, :]
    row = np.arange(P)[:, None]
    t["causal"] = np.concatenate([np.where(key <= NM + qt * P + row, 0.0, NEG) for qt in range(2)], 1)
    d = np.arange(P) % 64
    partner = np.arange(P) + np.where(d % 32 < 16, 16, -16)
    swap = np.zeros((P, P))
    swap[partner, np.arange(P)] = 1.0
    t["swap"] = swap
    freqs = np.float32(10000.0) ** (-np.arange(16, dtype=np.float32) / np.float32(16))
    pos = np.arange(NX)
    where = np.where(d[:, None] < 32, pos[None, :] // 64, pos[None, :] % 64).astype(np.float32)
    angle = (where * freqs[d % 16][:, None].astype(np.float32)).astype(np.float64)
    t["cos"] = np.cos(angle)
    t["sin"] = np.sin(angle) * np.where(d % 32 < 16, -1.0, 1.0)[:, None]
    ca = 2 * np.pi * (np.outer(np.arange(P), np.arange(P)) % P) / P
    t["dft_c"] = np.concatenate([np.cos(ca), np.sin(ca)], 1)
    la = 2 * np.pi * (np.outer(np.arange(NX), np.arange(NX)) % NX) / NX
    norm = (NX * P) ** -0.5
    for name, m in (("dft_l_cos", np.cos(la) * norm), ("dft_l_sin", -np.sin(la) * norm)):
        t[name] = m.reshape(2, P, NX).transpose(1, 0, 2).reshape(P, 2 * NX)
    w = (np.arange(P) % 64)[:, None]
    first = np.clip(w - 8, 0, 48)
    c = np.arange(64)[None, :]
    t["na_mask"] = np.where((c >= first) & (c < first + 16), 0.0, NEG)
    e = np.zeros((P, 31))
    e[:, 15] = 1 / P
    t["e31"] = e
    names = list(TABS)
    return tuple(np.concatenate([t[n] for n in part], 1).astype(np.float32) for part in (names[:4], names[4:]))


def kernel(**inputs):
    import concourse.bacc as bacc
    from concourse.bass_utils import run_bass_kernel_spmd

    a = {k: np.asarray(v) for k, v in inputs.items()}

    def chunks(w, per=4):
        k, n = w.shape
        width = CW // per
        w = w.reshape(k // (per * P), per, P, n // width, width)
        return w.transpose(3, 0, 2, 1, 4).reshape(-1, P, CW)

    def halves(first, second):
        f, s = chunks(first), chunks(second)
        per = first.shape[0] // (4 * P)
        f, s = f.reshape(-1, per, P, CW), s.reshape(-1, per, P, CW)
        return np.stack([f, s], 1).reshape(-1, P, CW)

    def feed_forward(gate, value, down):
        out = []
        for f0, f1 in ((0, 2048), (2048, 4096), (4096, F)):
            out += [halves(gate[:, f0:f1], value[:, f0:f1]), chunks(down[f0:f1])]
        return out

    w_in, w_in2 = a["w_in"][0], a["w_in_2"][0]
    o = np.cumsum([0, 512, 512, 64, 512, 512, 512, 512])
    cq, ckv, kr, qn, kn, vn, fn = (w_in2[:, o[i]:o[i + 1]] for i in range(7))
    uq = a["w_uq_2"][0].reshape(512, HEADS, 192)
    ukv = a["w_ukv_2"][0].reshape(512, HEADS, 2, P)
    up2 = a["w_up_2"][0]
    w_f = np.zeros((D, P), np.float32)
    w_f[:, :HEADS] = w_in[:, 6144:]
    stream = np.concatenate(
        [chunks(w_in[:, 1024:3072]), chunks(w_f, per=8), chunks(w_in[:, :1024]), chunks(w_in[:, 3072:6144]), chunks(a["w_out"][0])]
        + feed_forward(a["w_gate"][0], a["w_up"][0], a["w_down"][0])
        + [chunks(ckv), chunks(kn), chunks(np.concatenate([kr, kr], 1), per=8), chunks(cq), chunks(qn), chunks(fn),
           chunks(vn), chunks(ukv[:, :, 0].reshape(512, 1024)), chunks(ukv[:, :, 1].reshape(512, 1024)),
           chunks(uq[:, :, :P].reshape(512, 1024)), chunks(uq[:, :, P:].reshape(512, 512)), chunks(a["w_out_2"][0])]
        + feed_forward(up2[:, :F], up2[:, F:], a["w_down_2"][0]))
    assert len(stream) == N_CHUNKS

    def features(x):
        return x.T.reshape(-1, P, x.shape[0]).transpose(1, 0, 2)

    def columns(v):
        return v.reshape(-1, P).T

    conv_w2 = a["conv_w_2"][0]
    b_f = np.zeros((P, 1), np.float32)
    b_f[:HEADS, 0] = a["b_f"][0]
    vectors = {"norm_mix": a["norm_mix"], "out_gain": a["out_gain"], "norm_ffn": a["norm_ffn"],
               "final_norm": a["final_norm"], "g_attn": a["g_attn_2"], "g_ffn": a["g_ffn_2"], "g_final": a["g_final_2"],
               "g_q": a["g_q_2"], "g_kv": a["g_kv_2"], "c": a["c_2"], "c_ctx": a["c_ctx_2"], "b_mod": a["b_mod_2"],
               "conv1": a["conv_w"], "conv2_w0": conv_w2[0], "conv2_w1": conv_w2[1], "conv2_w2": conv_w2[2],
               "conv2_b": a["conv_b_2"]}
    packed = [columns(vectors[n]) if n in vectors else b_f if n == "b_f" else np.full((P, 1), {"eps": EPS, "one": 1.0, "scratch": 0.0}[n], np.float32)
              for n in COLS]
    rpb = a["na_rpb_2"][0]
    padded = np.zeros((NA_HEADS, 15, 127), np.float32)
    padded[:, :, 48:79] = rpb
    toeplitz = np.stack([padded[:, :, 63 - w:127 - w] for w in range(64)], 2)
    bias = np.stack([toeplitz[:, 7 - r:11 - r] for r in range(4)], 1)
    na_bias = bias.reshape(NA_HEADS, 2, 2, 4, 64, 64).transpose(2, 4, 0, 1, 3, 5).reshape(P, NA_HEADS, 2, NX)

    arrays = {
        "tokens": features(np.concatenate([a["meta"], a["x"][0]], 0)),
        "ctx_tokens": features(a["ctx_2"][0]),
        "cols": np.concatenate(packed, 1),
        "tables1": tables()[0],
        "tables2": tables()[1],
        "stream": stream,
        "mod_stream": np.concatenate([chunks(a["w_mod_2"][0][:, :CTX_TILES * P], per=2),
                                      chunks(a["w_mod_2"][0][:, CTX_TILES * P:])]),
        "na_bias": na_bias,
        "w_fnet": a["w_fnet_2"][0].transpose(1, 0, 2),
    }
    nc = bacc.Bacc("TRN2", target_bir_lowering=False, num_devices=1)
    args = []
    for name in arrays:
        arrays[name] = np.ascontiguousarray(arrays[name])
        args.append(nc.dram_tensor("in_" + name, arrays[name].shape, F32, kind="ExternalInput").ap())
    args.append(nc.dram_tensor("out_tokens", (P, KT, NX), F32, kind="ExternalOutput").ap())
    build(nc, *args)
    r = run_bass_kernel_spmd(nc, [{"in_" + k: v for k, v in arrays.items()}], core_ids=[0])
    got = r.results[0]["out_tokens"]
    return np.ascontiguousarray(got.transpose(2, 1, 0)).reshape(1, NX, D)
```

```python
from contextlib import ExitStack

import numpy as np

import concourse.bass as bass
from concourse import mybir

F32 = mybir.dt.float32
F32R = mybir.dt.float32r
ALU = mybir.AluOpType
ACT = mybir.ActivationFunctionType
AX_X = mybir.AxisListType.X

P = 128
D = 2048
KT = D // P
NX = 256
NM = 16
N1 = NM + NX
HEADS = 8
F = 5632
FT = F // P
EPS = 1e-6
SCALE1 = 128.0 ** -0.5
MLA_SCALE = 192.0 ** -0.5
NA_SCALE = 128.0 ** -0.5
NA_HEADS = 4
FN_GROUPS = 4
NEG = -1e30
RING = 4
CW = 1024
HW = 256
MOD_TILES = 6 * D // P
CTX_TILES = 2 * KT


DIRECT = ("out1", "dn1c")


class Layer:

    def __init__(self, name, its, halves, c, tiles=2, mod=0, ctx=False, loop=True, mod_at=None):
        self.name, self.its, self.halves, self.c, self.tiles = name, its, halves, c, tiles
        self.mod, self.ctx, self.loop = mod, ctx, loop and its > 1
        self.mtiles = 4 if ctx else 2
        if mod_at is not None:
            self.mod_at = mod_at
        elif ctx:
            self.mod_at = (0, 1, 3, 5, 7, 9, 11, 12)
        else:
            self.mod_at = (0, 1, 3, 4) if mod else ()
        self.cpi = halves * c
        self.tpi = halves * tiles


def ffn_layers(tag, mod):
    out = []
    for part, its in (("a", 8), ("b", 8), ("c", 6)):
        out.append(Layer("up" + tag + part, its, 2, 4, mod=2 * mod))
        if part == "c":
            out.append(Layer("dn" + tag + part, 2, 4, 3, loop=tag == "1"))
        else:
            out.append(Layer("dn" + tag + part, 4, 2, 4, mod=2 * mod))
    return out


LAYERS = ([Layer("kv1", 2, 4, 4, mod=2, ctx=True), Layer("f1", 1, 1, 2, tiles=1),
           Layer("q1", 1, 4, 4, mod=2, ctx=True),
           Layer("conv1", 3, 4, 4, mod=2, ctx=True), Layer("att1", 1, 0, 0, mod=2, ctx=True),
           Layer("out1", 1, 8, 4, mod=2, ctx=True, mod_at=(1, 4, 8, 12, 15, 18, 21, 24))]
          + ffn_layers("1", 1)
          + [Layer("joint", 2, 2, 4, mod=2), Layer("kr", 1, 1, 2, tiles=1), Layer("xonly", 3, 2, 4),
             Layer("vn", 1, 2, 4, tiles=4), Layer("uk", 1, 4, 1), Layer("uv", 1, 4, 1, tiles=4),
             Layer("uq", 1, 6, 1), Layer("out2", 4, 2, 4)]
          + ffn_layers("2", 0))
_c = _t = _g = _m = _mt = 0
for _l in LAYERS:
    _l.base, _l.tbase, _l.gbase, _l.mbase, _l.mtbase = _c, _t, _g, _m, _mt
    _c += _l.its * _l.cpi
    _t += _l.its * _l.tpi
    _g += _l.its if _l.mod else 0
    _m += _l.its * len(_l.mod_at)
    _mt += _l.its * _l.mtiles if _l.mod else 0
N_CHUNKS, MOD_GROUPS, MOD_CHUNKS = _c, _g, _m
assert _mt == MOD_TILES
LY = {_l.name: _l for _l in LAYERS}

COLS, _o = {}, 0
for _n, _w in (("norm_mix", 16), ("out_gain", 16), ("norm_ffn", 16), ("final_norm", 16), ("g_attn", 16),
               ("g_ffn", 16), ("g_final", 16), ("g_q", 4), ("g_kv", 4), ("c", 16), ("c_ctx", 16),
               ("b_mod", MOD_TILES), ("conv1", 24), ("conv2_w0", 88), ("conv2_w1", 88), ("conv2_w2", 88),
               ("conv2_b", 88), ("b_f", 1), ("eps", 1), ("one", 1), ("scratch", 1)):
    COLS[_n] = (_o, _w)
    _o += _w
N_COLS = _o
TABS, _o = {}, 0
for _n, _w in (("ident", P), ("mean", P), ("causal", 2 * N1), ("e31", 31)):
    TABS[_n] = (_o, _w)
    _o += _w
N_TABS1 = _o
_o = TABS["causal"][0]
for _n, _w in (("swap", P), ("cos", NX), ("sin", NX), ("dft_c", 2 * P), ("dft_l_cos", 2 * NX),
               ("dft_l_sin", 2 * NX), ("na_mask", 64)):
    TABS[_n] = (_o, _w)
    _o += _w
N_TABS = _o


def build(nc, tokens, ctx_tokens, cols_d, tables1_d, tables2_d, stream, mod_stream, na_bias_d, w_fnet_d, out):
    stack = ExitStack()
    with stack:
        def sem(name):
            return stack.enter_context(nc.semaphore(name))

        top = [nc.sbuf_base if isinstance(nc.sbuf_base, int) else 0]
        limit = nc.sbuf_usable_end if isinstance(nc.sbuf_usable_end, int) else 212863
        start = -(-top[0] // 64) * 64
        top[0] = start

        def at(name, shape, dt, offset):
            size = 4 * int(np.prod(shape[1:]))
            assert offset + size <= limit, (name, offset + size, limit)
            return nc.alloc_sbuf_tensor_at(name, shape, dt, offset=offset)

        def keep(name, shape, dt=F32):
            offset = top[0]
            top[0] += -(-4 * int(np.prod(shape[1:])) // 64) * 64
            return at(name, shape, dt, offset), offset

        raw, _ = keep("raw", [P, RING, CW])
        hi, _ = keep("hi", [P, RING, CW], F32R)
        lo, _ = keep("lo", [P, RING, CW], F32R)
        wm, o_wm = keep("wm", [P, 2, CW])
        acc, o_acc = keep("acc", [P, 2, 2 * HW])
        accf, o_accf = keep("accf", [P, 2, 2 * HW])
        h, _ = keep("h", [P, KT, N1])
        cols, _ = keep("cols", [P, N_COLS])
        tabs, _ = keep("tabs", [P, N_TABS])
        mod, _ = keep("mod", [P, MOD_TILES])
        modx, _ = keep("modx", [P, CTX_TILES])
        csilu, _ = keep("csilu", [P, 2 * KT])
        gm, _ = keep("gm", [P, 3, KT])
        att, _ = keep("att", [P, 3, 2 * HEADS])
        cq, _ = keep("cq", [P, 2, HEADS])
        std, _ = keep("std", [P, 2 * NX])
        rstd_q, tok = std[:, 0:NX], std[:, NX:2 * NX]
        rstd, o_rstd = keep("rstd", [P, 2 * NX])
        ssum = at("ssum", [P, 2, NX], F32, o_rstd)
        _, o_work = keep("work_slab", [P, 2, 4, N1])
        sq = at("sq", [P, 2, 4 * N1], F32, o_work)
        xn = at("xn", [P, 2, 4 * N1], F32, o_work)
        xnf = at("xnf", [P, 8 * N1], F32, o_work)
        tmp = at("tmp", [P, 4, HW], F32, o_work)
        sqb = at("sqb", [P, 2, 2, HW], F32, o_work + 4096)
        arena = top[0]
        xs1 = at("xs1", [P, KT, 2, N1], F32R, arena)
        ys1 = at("ys1", [P, KT, 2, NX], F32R, arena)
        o = arena + 4 * KT * 2 * N1
        z = at("z", [P, 48, N1], F32, o)
        o += 4 * 48 * N1
        vtok = at("vtok", [P, 3, 1024], F32, o)
        o += 4 * 3 * 1024
        fl = at("fl", [P, 3, N1], F32, o)
        p1 = at("p1", [P, 2, 2, N1], F32, o_work)
        pt1 = at("pt1", [P, 3, NX], F32, o_work + 4 * 4 * N1)
        o = arena
        hid = at("hid", [P, KT, 2, NX], F32R, o)
        o += 4 * KT * 2 * NX
        hs = at("hs", [P, KT, 2, NX], F32R, o)
        o += 4 * KT * 2 * NX
        o += 4 * KT * NX
        gt = at("gt", [P, 2, NX], F32, o)
        sg = at("sg", [P, 2, NX], F32, o + 2048)
        ut = at("ut", [P, 2, NX], F32, o + 4096)
        hv = at("hv", [P, 2, NX], F32, o + 6144)
        pad = at("pad", [P, 2, NX + 2], F32, o + 8192)
        cv = at("cv", [P, 2, 3, NX], F32, o + 8192 + 2112)
        csq = at("csq", [P, 2, NX], F32, o + 8192)
        csum = at("csum", [P, 2, NX], F32, o + 8192 + 4096)
        gsqb = at("gsqb", [P, 2, 2, NX], F32, o + 8192)
        gsum = at("gsum", [P, 2, NX], F32, o + 8192 + 4096)
        o = arena
        hs2 = at("hs2", [P, 2, KT, 2, NX], F32R, o)
        ysb = at("ysb", [P, 8, 2, NX], F32R, o)
        qn_m = at("qn_m", [P, HEADS, NX], F32, o + 16384)
        qr_m = at("qr_m", [P, 4, NX], F32, o + 24576)
        krm = at("krm", [P, 2, 2 * NX], F32, o + 28672)
        ckvs = at("ckvs", [P, 4, 2, 2 * NX], F32R, o + 16384)
        kn_m = at("kn_m", [P, HEADS, 2 * NX], F32, o + 32768)
        vt_m = at("vt_m", [P, 4, 1024], F32, o + 49152)
        o += 65536
        zj = at("zj", [P, 8, 2 * NX], F32, o)
        cx = at("cx", [P, KT, NX], F32, o)
        cqs = at("cqs", [P, 4, 2, NX], F32R, o + 8192)
        o += 16384
        kr = at("kr", [P, 2 * NX], F32, o)
        o += 2048
        zx = at("zx", [P, 12, NX], F32, o)
        ysa = at("ysa", [P, 8, 2, NX], F32R, o + 4096)
        rot = at("rot", [P, 2, 4, NX], F32, o + 4096)
        o += 12288
        vn = at("vn", [P, 4, 512], F32, o)
        kvsq = at("kvsq", [P, 4, 512], F32, o)
        na = at("na", [P, NA_HEADS, 2, NX], F32, o_wm)
        pt2 = at("pt2", [P, 4, NX], F32, o_acc)
        wfn = at("wfn", [P, FN_GROUPS, P], F32, o_accf)
        p2 = at("p2", [P, 2, 2, 2 * NX], F32, o_work)
        ab = at("ab", [P, 2, 2, 2 * P], F32, o_wm)
        sp = at("sp", [P, 2, NX], F32, o_wm + 4096)
        ps = stack.enter_context(nc.psum_tensor("ps", [P, 8, 512], F32))

        def col(name, i=0, n=1):
            return cols[:, COLS[name][0] + i:COLS[name][0] + i + n]

        def dcol(name, expr):
            return cols[:, bass.ds(expr + COLS[name][0], 1)]

        def tab(name):
            return tabs[:, TABS[name][0]:TABS[name][0] + TABS[name][1]]

        ident, mean = tab("ident"), tab("mean")
        causal = tab("causal").rearrange("p (a n) -> p a n", a=2)
        dft_lc = tab("dft_l_cos").rearrange("p (a n) -> p a n", a=2)
        dft_ls = tab("dft_l_sin").rearrange("p (a n) -> p a n", a=2)
        hx = h[:, :, NM:N1]

        tokens_in = [sem(f"tokens_in{b}") for b in range(4)]
        tables_in, ctx_in, late_in = sem("tables_in"), sem("ctx_in"), sem("late_in")
        silu_c_done = sem("silu_c_done")
        raw_full = [sem(f"raw_full{s}") for s in range(RING)]
        hi_done = sem("hi_done")
        lo_done = sem("lo_done")
        chunk_used = sem("chunk_used")
        tmp_ready = sem("tmp_ready")
        bank_free = sem("bank_free")
        res_done = sem("res_done")
        wm_full = [sem(f"wm_full{s}") for s in range(2)]
        wm_used = sem("wm_used")
        wm_op = sem("wm_op")
        accf_ready = sem("accf_ready")
        mod_sum = sem("mod_sum")
        mod_done = sem("mod_done")
        gm_done = sem("gm_done")
        sq_ready, sq_added = sem("sq_ready"), sem("sq_added")
        stat_ready, std_ready, inv_ready, rstd_ready = sem("stat_ready"), sem("std_ready"), sem("inv_ready"), sem("rstd_ready")
        sum_sq, sum_added = sem("sum_sq"), sem("sum_added")
        gsum_step, rstd_copied, qsq_ready, kvsq_ready = sem("gsum_step"), sem("rstd_copied"), sem("qsq_ready"), sem("kvsq_ready")
        csq_ready, csq_added = sem("csq_ready"), sem("csq_added")
        cxn_ready, cx_hi, cx_done = sem("cxn_ready"), sem("cx_hi"), sem("cx_done")
        xn_ready, xs_hi, xs_ready = sem("xn_ready"), sem("xs_hi"), sem("xs_ready")
        x_final = sem("x_final")
        f_act, f_dve, cq_psum, cq_ready = sem("f_act"), sem("f_dve"), sem("cq_psum"), sem("cq_ready")
        vt_ready, vtok_ready = sem("vt_ready"), sem("vtok_ready")
        s_ready, s_taken, max_ready, exp_ready = sem("s_ready"), sem("s_taken"), sem("max_ready"), sem("exp_ready")
        rsum_ready, p_ready = sem("rsum_ready"), sem("p_ready")
        pt_psum, pt_ready, o_ready, y_ready = sem("pt_psum"), sem("pt_ready"), sem("o_ready"), sem("y_ready")
        conv_u, conv_w0, conv_step, conv_ready = sem("conv_u"), sem("conv_w0"), sem("conv_step"), sem("conv_ready")
        gn_sq, gn_stat, gn_std, gn_r, gn_bc = sem("gn_sq"), sem("gn_stat"), sem("gn_std"), sem("gn_r"), sem("gn_bc")
        gn_y, gn_hi, gn_ready = sem("gn_y"), sem("gn_hi"), sem("gn_ready")
        sg_ready, hv_ready, hid_hi, hid_ready = sem("sg_ready"), sem("hv_ready"), sem("hid_hi"), sem("hid_ready")
        cv_step, pads_zero = sem("cv_step"), sem("pads_zero")
        na_bias_ready = sem("na_bias_ready")
        fn_a, fn_ab, fn_b, fn_sp, fn_c = sem("fn_a"), sem("fn_ab"), sem("fn_b"), sem("fn_sp"), sem("fn_c")
        y2_hi, y2_ready = sem("y2_hi"), sem("y2_ready")
        s2_ready, s2_half, max2_ready, nmax2_ready = sem("s2_ready"), sem("s2_half"), sem("max2_ready"), sem("nmax2_ready")
        s2_bias = sem("s2_bias")
        exp2_ready, rsum2_ready, p2_ready = sem("exp2_ready"), sem("rsum2_ready"), sem("p2_ready")
        pt2_psum, pt2_ready, o2_ready = sem("pt2_psum"), sem("pt2_ready"), sem("o2_ready")
        rot_psum, rot_step, rope_ready, krm_zero = sem("rot_psum"), sem("rot_step"), sem("rope_ready"), sem("krm_zero")
        out_done = sem("out_done")

        NORMS = {"mix": (N1, KT), "ffn1": (NX, KT), "ctx": (NX, KT), "final1": (NX, KT), "attn2": (NX, KT),
                 "kv": (2 * NX, 4), "q": (NX, 4), "ffn2": (NX, KT), "final2": (NX, KT)}
        NTH = {name: i for i, name in enumerate(NORMS)}
        STAT = {name: NTH[name] - (NTH[name] > NTH["final1"]) for name in NORMS}

        def token_tiles(name):
            n = NORMS[name][0]
            return [(th, min(P, n - th * P)) for th in range(-(-n // P))]

        def token_columns(name):
            whole, rest = divmod(NORMS[name][0], P)
            return [(P, 0, whole)] + ([(rest, whole, whole + 1)] if rest else [])

        def xn_slots(name):
            return 8 * N1 // NORMS[name][0]

        def xn_tile(name, k):
            n = NORMS[name][0]
            return xnf[:, k % xn_slots(name) * n:k % xn_slots(name) * n + n]

        def tok_std(name):
            return tok[:, 4 * NTH[name]:4 * NTH[name] + 4]

        def tok_inv(name):
            return tok[:, 64 + 4 * NTH[name]:64 + 4 * NTH[name] + 4]

        SPLIT, n_split = {}, 0
        for name in ("mix", "ffn1", "attn2", "kv", "q", "ffn2"):
            SPLIT[name] = n_split
            n_split += NORMS[name][1]
        SUMS, ADD0, n_sum = {}, {}, 0
        for name in ("out1", "dn1c", "out2", "dn2c"):
            SUMS[name], ADD0[name] = n_sum, n_sum + 4 * len(SUMS)
            n_sum += LY[name].its * LY[name].halves
        CONCAT, n_concat = {}, 0
        for ly in LAYERS:
            CONCAT[ly.name] = n_concat
            if ly.name != "dn1c" and ly.name[:2] in ("up", "dn") or ly.name in ("xonly", "uq", "out2"):
                n_concat += ly.its * ly.tpi
        RES, n_res = {}, 0
        for ly in LAYERS:
            RES[ly.name] = n_res
            if ly.name[:2] == "dn" and ly.name != "dn1c" or ly.name == "out2":
                n_res += ly.its * ly.tpi

        def tiles_added(ly, n):
            return (bank_free, ly.tbase + 4 + n) if ly.name in DIRECT else (res_done, RES[ly.name] + n)

        HID, n_hid = {}, 0
        for ly in LAYERS:
            HID[ly.name] = n_hid
            if ly.name[:2] == "up":
                n_hid += ly.its * 2

        def run(eng, ly, body):
            if ly.loop:
                with eng.Fori(0, ly.its) as it:
                    body(it)
            else:
                for it in range(ly.its):
                    body(it)

        def ahead(ly, it, hf, j):
            k = ly.base + RING + hf * ly.c + j
            if not ly.loop and k + it * ly.cpi >= N_CHUNKS:
                return None
            if ly.loop:
                return k + it * ly.cpi, k % RING, k // RING + it * (ly.cpi // RING)
            return k + it * ly.cpi, (k + it * ly.cpi) % RING, (k + it * ly.cpi) // RING

        def last_chunk(ly, it, hf):
            return ly.base + (hf + 1) * ly.c - 1 + it * ly.cpi

        def gsq(hd):
            return z[:, 8 + 2 * (hd % 2):10 + 2 * (hd % 2), 0:NX]

        def score_bank2(hd, qt, local):
            return (4 if hd % 2 == 0 or local else 2) + qt

        block = stack.enter_context(nc.Block())

        @block.sync
        def _(sp_):
            for b in range(4):
                sp_.dma_start(h[:, 4 * b:4 * b + 4, :], tokens[:, 4 * b:4 * b + 4, :]).then_inc(tokens_in[b], 16)
            sp_.dma_start(cols[:, :], cols_d).then_inc(tables_in, 16)
            sp_.dma_start(tabs[:, 0:N_TABS1], tables1_d).then_inc(tables_in, 16)

            def load(v, slot):
                sp_.wait_ge(lo_done, v + 1)
                sp_.dma_start(raw[:, slot, :], stream[bass.ds(v, 1)].rearrange("a p n -> p (a n)"))\
                   .then_inc(raw_full[slot], 16)

            def load_mod(m, slot):
                sp_.wait_ge(wm_used, m + 1)
                sp_.dma_start(wm[:, slot, :], mod_stream[bass.ds(m, 1)].rearrange("a p n -> p (a n)"))\
                   .then_inc(wm_full[slot], 16)

            for v in range(RING):
                load(v, v)
            for ly in LAYERS:
                def body(it, ly=ly):
                    for hf in range(ly.halves):
                        for j in range(ly.c):
                            a = ahead(ly, it, hf, j)
                            if a is not None:
                                load(a[0], a[1])
                            if hf * ly.c + j in ly.mod_at:
                                m = ly.mod_at.index(hf * ly.c + j)
                                load_mod(ly.mbase + m + it * len(ly.mod_at), m % 2)
                if ly.name == "att1":
                    for m in range(len(ly.mod_at)):
                        load_mod(ly.mbase + m, m % 2)
                    continue
                run(sp_, ly, body)
                if ly.name == "out1":
                    sp_.wait_ge(gn_ready, 4)
                    sp_.dma_start(cx[:, :, :], ctx_tokens).then_inc(ctx_in, 16)
                    sp_.dma_start(tabs[:, TABS["swap"][0]:N_TABS], tables2_d).then_inc(late_in, 16)
                if ly.name == "joint":
                    sp_.wait_ge(wm_used, MOD_CHUNKS + 2)
                    sp_.wait_ge(mod_sum, MOD_GROUPS + 1)
                    sp_.dma_start(na[:, :, :, :], na_bias_d).then_inc(late_in, 16)
                    sp_.dma_start(wfn[:, :, :], w_fnet_d).then_inc(late_in, 16)
            for b in range(4):
                sp_.wait_ge(x_final, KT + 4 * b + 4)
                sp_.dma_start(out[:, 4 * b:4 * b + 4, :], hx[:, 4 * b:4 * b + 4, :]).then_inc(out_done, 16)
            sp_.wait_ge(out_done, 64)

        @block.scalar
        def _(act):
            def split_hi(v, slot, turn):
                act.wait_ge(raw_full[slot], 16 * (turn + 1))
                act.wait_ge(chunk_used, v + 1)
                act.activation(hi[:, slot, :], raw[:, slot, :], ACT.Copy).then_inc(hi_done, 1)

            def mod_hand_over(ly, it):
                act.wait_ge(wm_used, ly.mbase + (it + 1) * 8 + 2)
                act.wait_ge(mod_sum, ly.gbase + it + 1)
                act.activation(accf[:, :, :], acc[:, :, :], ACT.Copy).then_inc(accf_ready, 1)

            def prepare(ly, it, hf, first=0, last=None):
                for j in range(first, ly.c if last is None else last):
                    a = ahead(ly, it, hf, j)
                    if a is not None:
                        split_hi(*a)
                    if ly.ctx and hf * ly.c + j == ly.mod_at[-1] + 1:
                        mod_hand_over(ly, it)

            def second_halves(ly, it, hf):
                act.wait_ge(chunk_used, last_chunk(ly, it, hf) + 5)
                for t in range(2):
                    bank = (2 * hf + t) % 4
                    act.activation(tmp[:, bank, :], ps[:, bank, NX:2 * NX], ACT.Copy).then_inc(tmp_ready, 1)

            def load_sqrt():
                act.activation(col("scratch"), col("one"), ACT.Sqrt)

            def token_std(name, bank=4):
                act.wait_ge(stat_ready, STAT[name] + 1)
                for rows, c0, c1 in token_columns(name):
                    ins = act.activation(tok_std(name)[0:rows, c0:c1], ps[0:rows, bank, c0:c1], ACT.Sqrt,
                                         bias=cols[0:rows, COLS["eps"][0]:COLS["eps"][0] + 1])
                ins.then_inc(std_ready, 1)

            def norm_hi(name, dst, shift=None, after=None):
                for k in range(NORMS[name][1]):
                    act.wait_ge(xn_ready, SPLIT[name] + k + 1)
                    if shift is None:
                        act.activation(dst(k), xn_tile(name, k), ACT.Copy).then_inc(xs_hi, 1)
                    else:
                        act.activation(dst(k), xn_tile(name, k), ACT.Identity, bias=shift(k)).then_inc(xs_hi, 1)
                    if after is not None:
                        after(k)

            for b in range(4):
                act.wait_ge(tokens_in[b], 16)
                act.activation(z[:, 4 * b:4 * b + 4, :], h[:, 4 * b:4 * b + 4, :], ACT.Square,
                               scale=KT ** -0.5).then_inc(sq_ready, 1)
            act.wait_ge(tables_in, 32)
            load_sqrt()
            split_hi(0, 0, 0)
            token_std("mix")
            split_hi(1, 1, 0)

            def between_tiles(k):
                if k in (3, 7):
                    split_hi(2 + k // 4, 2 + k // 4, 0)
                if k == 11:
                    act.activation(csilu[:, :], cols[:, COLS["c"][0]:COLS["c"][0] + 2 * KT], ACT.Silu).then_inc(silu_c_done, 1)

            norm_hi("mix", lambda k: xs1[:, k, 0, :], after=between_tiles)

            def to_z(name, z0, first_token, scale=1.0):
                ly = LY[name]

                def body(it):
                    for hf in range(ly.halves):
                        prepare(ly, it, hf)
                        act.wait_ge(chunk_used, last_chunk(ly, it, hf) + 5)
                        for t in range(2):
                            act.activation(z[:, bass.ds(it * ly.tpi + z0 + 2 * hf + t, 1), first_token:N1]
                                           .rearrange("p a n -> p (a n)"), ps[:, (2 * hf + t) % 4, 0:N1 - first_token],
                                           ACT.Copy, scale=scale).then_inc(bank_free, 1)
                run(act, ly, body)

            to_z("kv1", 0, 0)
            prepare(LY["f1"], 0, 0)
            for i in range(6):
                rows = P if i % 3 < 2 else N1 - 2 * P
                act.wait_ge(vt_ready, i + 1)
                act.activation(vtok[0:rows, i % 3, 512 * (i // 3):512 * (i // 3) + 512], ps[0:rows, 4 + i % 2, :],
                               ACT.Copy).then_inc(vtok_ready, 1)
            act.wait_ge(bank_free, LY["q1"].tbase + 4)
            act.activation(fl[0:HEADS, 1, :], fl[0:HEADS, 0, :], ACT.Abs).then_inc(f_act, 1)
            act.wait_ge(f_act, 1)
            act.activation(fl[0:HEADS, 2, :], fl[0:HEADS, 1, :], ACT.Exp, scale=-1.0).then_inc(f_act, 1)
            act.wait_ge(f_act, 2)
            act.activation(fl[0:HEADS, 1, :], fl[0:HEADS, 2, :], ACT.Ln, bias=1.0).then_inc(f_act, 1)
            to_z("q1", 16, NM - 2, SCALE1)

            def exps(hd):
                for qt in range(2):
                    u = 2 * hd + qt
                    act.wait_ge(max_ready, u + 1)
                    act.activation(p1[:, hd % 2, qt, :], p1[:, hd % 2, qt, :], ACT.Exp, bias=att[:, 0, u:u + 1],
                                   accum_out=att[:, 1, u:u + 1]).then_inc(exp_ready, 1)

            def normalised(hd):
                for qt in range(2):
                    u = 2 * hd + qt
                    act.wait_ge(rsum_ready, u + 1)
                    act.activation(p1[:, hd % 2, qt, :], p1[:, hd % 2, qt, :], ACT.Copy, scale=att[:, 2, u:u + 1])\
                       .then_inc(p_ready, 1)

            def take_pt(hd):
                act.wait_ge(pt_psum, hd + 1)
                if hd >= 1:
                    act.wait_ge(o_ready, hd)
                act.activation(pt1[:, 0:2, :], ps[:, 6, :].rearrange("p (k n) -> p k n", k=2), ACT.Copy)
                act.activation(pt1[0:NM, 2, :], ps[0:NM, 7, 0:NX], ACT.Copy).then_inc(pt_ready, 1)

            def take_y(hd):
                act.wait_ge(o_ready, hd + 1)
                act.activation(z[:, 16 + hd, NM:N1], ps[:, 0, 0:NX], ACT.Copy)
                if hd >= 2:
                    act.wait_ge(gn_stat, hd - 1)
                act.activation(gsq(hd)[:, 0, :], ps[:, 0, 0:NX], ACT.Square).then_inc(y_ready, 1)
                act.wait_ge(conv_ready, hd + 1)
                act.activation(gsq(hd)[:, 1, :], z[:, 24 + hd, NM:N1], ACT.Square).then_inc(gn_sq, 1)

            def conv_first(g):
                act.wait_ge(conv_u, g + 1)
                act.activation(z[:, 40 + g, 0:NX], z[:, 32 + g, NM - 2:N1 - 2], ACT.Copy, scale=col("conv1", g)).then_inc(conv_w0, 1)

            exps(0)
            normalised(0)
            to_z("conv1", 24, NM - 2)
            conv_first(0)
            for hd in range(HEADS):
                if hd + 1 < HEADS:
                    exps(hd + 1)
                if hd >= 1:
                    take_y(hd - 1)
                take_pt(hd)
                if hd + 1 < HEADS:
                    normalised(hd + 1)
                    conv_first(hd + 1)
            act.activation(col("scratch"), col("one"), ACT.Sqrt)
            take_y(HEADS - 1)
            act.wait_ge(gn_stat, HEADS)
            act.activation(std[0:16, 0:NX], ps[0:16, 1, 0:NX], ACT.Sqrt, bias=cols[0:16, COLS["eps"][0]:COLS["eps"][0] + 1])\
               .then_inc(gn_std, 1)
            mod_hand_over(LY["att1"], 0)
            for b in range(4):
                act.wait_ge(gn_y, 4 * b + 4)
                act.activation(ys1[:, 4 * b:4 * b + 4, 0, :], xn[:, b % 2, 0:4 * NX].rearrange("p (k n) -> p k n", k=4),
                               ACT.Copy).then_inc(gn_hi, 1)

            def residual(ly, sums=False, gain=None, after_first=None):
                def squares(it, hf):
                    n0 = it * ly.tpi + 2 * hf
                    act.wait_ge(*tiles_added(ly, n0 + 2))
                    if gain is not None:
                        for t in range(2):
                            act.activation(gsqb[:, hf % 2, t, :],
                                           hx[:, bass.ds(n0 + t, 1), :].rearrange("p a n -> p (a n)"),
                                           ACT.Square, scale=dcol(gain, n0 + t))
                    act.activation(sqb[:, hf % 2, :, :], hx[:, bass.ds(n0, 2), :], ACT.Square,
                                   scale=KT ** -0.5).then_inc(sum_sq, 1)

                def body(it):
                    for hf in range(ly.halves):
                        prepare(ly, it, hf, 0, 1)
                        if after_first is not None:
                            after_first(it, hf)
                        if sums and hf >= 1:
                            squares(it, hf - 1)
                        prepare(ly, it, hf, 1, ly.c - 1)
                        if ly.name not in DIRECT:
                            second_halves(ly, it, hf)
                        prepare(ly, it, hf, max(ly.c - 1, 1))
                    if sums:
                        squares(it, ly.halves - 1)
                run(act, ly, body)

            def gated(ly, gate_src, gate_step, after_first=None):
                def body(it):
                    prepare(ly, it, 0, 0, 3)
                    second_halves(ly, it, 0)
                    prepare(ly, it, 0, 3)
                    if after_first is not None:
                        after_first(it)
                    prepare(ly, it, 1, 0, 1)
                    for t in range(2):
                        act.wait_ge(*gate_step(it, t))
                        act.activation(sg[:, t, :], gate_src(t), ACT.Silu).then_inc(sg_ready, 1)
                    prepare(ly, it, 1, 1, 3)
                    second_halves(ly, it, 1)
                    prepare(ly, it, 1, 3)
                    for t in range(2):
                        n = HID[ly.name] + it * 2 + t
                        act.wait_ge(hv_ready, n + 1)
                        act.activation(hid[:, bass.ds(it * 2 + t, 1), 0, :].rearrange("p a n -> p (a n)"), hv[:, t, :],
                                       ACT.Copy).then_inc(hid_hi, 1)
                run(act, ly, body)

            residual(LY["out1"], sums=True)
            token_std("ffn1")
            norm_hi("ffn1", lambda k: hs[:, k, 0, :])

            def gated1(part, after_first=None):
                ly = LY["up1" + part]
                gated(ly, lambda t: gt[:, t, :], lambda it, t: (bank_free, ly.tbase + it * 4 + t + 5), after_first)

            def ctx_squares(it):
                act.wait_ge(csq_added, it + 1)
                act.activation(csq[:, :, :], cx[:, bass.ds(it * 2, 2), :], ACT.Square, scale=KT ** -0.5).then_inc(csq_ready, 1)

            act.wait_ge(ctx_in, 16)
            gated1("a", ctx_squares)
            load_sqrt()
            residual(LY["dn1a"])
            token_std("ctx")
            gated1("b")
            residual(LY["dn1b"])
            gated1("c")

            def ctx_hi(it, hf):
                n0 = it * LY["dn1c"].tpi + 2 * hf
                act.wait_ge(cxn_ready, it * LY["dn1c"].halves + hf + 1)
                for t in range(2):
                    ins = act.activation(hs2[:, 1, bass.ds(n0 + t, 1), 0, :].rearrange("p a n -> p (a n)"),
                                         cx[:, bass.ds(n0 + t, 1), :].rearrange("p a n -> p (a n)"), ACT.Identity,
                                         bias=modx[:, bass.ds(n0 + t, 1)])
                ins.then_inc(cx_hi, 1)

            act.wait_ge(mod_done, LY["joint"].gbase + 1)
            load_sqrt()
            residual(LY["dn1c"], sums=True, gain="final_norm", after_first=ctx_hi)
            token_std("final1")
            act.wait_ge(gsum_step, 2)
            act.activation(tok_std("attn2")[:, 0:2], tok[:, 130:132], ACT.Sqrt, bias=col("eps")).then_inc(std_ready, 1)
            norm_hi("attn2", lambda k: hs2[:, 0, k, 0, :], lambda k: mod[:, k:k + 1])

            def plain(ly):
                def body(it):
                    for hf in range(ly.halves):
                        prepare(ly, it, hf)
                run(act, ly, body)

            plain(LY["joint"])
            act.wait_ge(bank_free, LY["joint"].tbase + 4 + 4)
            act.activation(kvsq[:, :, :], zj[:, 0:4, :], ACT.Square, scale=0.5).then_inc(kvsq_ready, 1)
            plain(LY["kr"])
            residual(LY["xonly"])
            load_sqrt()
            token_std("kv")
            act.wait_ge(bank_free, LY["vn"].tbase + 4)
            act.activation(sq[:, 1, 0:4 * NX].rearrange("p (k n) -> p k n", k=4), zx[:, 0:4, :], ACT.Square, scale=0.5)\
               .then_inc(qsq_ready, 1)
            ly = LY["vn"]
            prepare(ly, 0, 0, 0, ly.c - 1)
            token_std("q", 7)
            act.wait_ge(rstd_ready, NTH["kv"] + 1)
            act.activation(rstd[:, :], ps[:, 6, :], ACT.Copy).then_inc(rstd_copied, 1)
            prepare(ly, 0, 0, ly.c - 1)
            prepare(ly, 0, 1)
            act.wait_ge(rstd_ready, NTH["q"] + 1)
            act.activation(rstd_q, ps[:, 0, 0:NX], ACT.Copy).then_inc(rstd_copied, 1)

            def attend(first, heads, scale, local, between=None):
                def exps2(hd):
                    for qt in range(2):
                        u = 2 * (first + hd) + qt
                        if local:
                            act.wait_ge(s2_ready, u + 1)
                            act.activation(p2[:, hd % 2, qt, NX:2 * NX], ps[:, score_bank2(hd, qt, local), NX:2 * NX], ACT.Copy,
                                           scale=scale).then_inc(s2_half, 1)
                    for qt in range(2):
                        u = 2 * (first + hd) + qt
                        act.wait_ge(nmax2_ready, u + 1)
                        src = p2[:, hd % 2, qt, :] if local else ps[:, score_bank2(hd, qt, local), :]
                        act.activation(p2[:, hd % 2, qt, :], src, ACT.Exp, bias=att[:, 0, u % 16:u % 16 + 1],
                                       scale=1.0 if local else scale,
                                       accum_out=att[:, 1, u % 16:u % 16 + 1]).then_inc(exp2_ready, 1)

                def take_pt2(hd):
                    n = first + hd
                    act.wait_ge(pt2_psum, n + 1)
                    if n >= 1:
                        act.wait_ge(o2_ready, n)
                    for qt in range(2):
                        ins = act.activation(pt2[:, :, qt * P:qt * P + P],
                                             ps[:, 6 + qt, :].rearrange("p (k n) -> p k n", k=4), ACT.Copy)
                    ins.then_inc(pt2_ready, 1)

                def take_y2(hd):
                    act.wait_ge(o2_ready, first + hd + 1)
                    y = ysb[:, hd, 0, :] if local else ysa[:, hd, 0, :]
                    act.activation(y, ps[:, hd % 2, 0:NX], ACT.Copy).then_inc(y2_hi, 1)

                exps2(0)
                for hd in range(heads):
                    if hd + 1 < heads and between is None:
                        exps2(hd + 1)
                    if hd >= 1 and between is not None:
                        exps2(hd)
                        take_y2(hd - 1)
                    if between is not None:
                        between(hd)
                    take_pt2(hd)
                    if hd >= 1 and between is None:
                        take_y2(hd - 1)
                take_y2(heads - 1)

            norm_hi("kv", lambda k: ckvs[:, k, 0, :])
            act.wait_ge(xs_ready, SPLIT["kv"] + 4)
            attend(0, NA_HEADS, NA_SCALE, True, lambda hd: prepare(LY["uk"], 0, hd))
            norm_hi("q", lambda k: cqs[:, k, 0, :])

            def fourier_y(g):
                act.wait_ge(fn_c, g + 1)
                act.activation(ysb[:, 4 + g, 0, :], ps[:, 7, 0:NX], ACT.Copy).then_inc(y2_hi, 1)

            for g in range(FN_GROUPS):
                act.wait_ge(fn_a, g + 1)
                act.activation(ab[:, g % 2, :, :], ps[:, 4:6, 0:2 * P], ACT.Copy).then_inc(fn_ab, 1)
                prepare(LY["uv"], 0, g)
                if g >= 1:
                    fourier_y(g - 1)
            for hf in range(LY["uq"].halves):
                prepare(LY["uq"], 0, hf)
                second_halves(LY["uq"], 0, hf)
                if hf == 0:
                    fourier_y(FN_GROUPS - 1)
            attend(NA_HEADS, HEADS, MLA_SCALE, False)

            load_sqrt()
            residual(LY["out2"], sums=True)
            token_std("ffn2")
            norm_hi("ffn2", lambda k: hs[:, k, 0, :], lambda k: mod[:, 48 + k:49 + k])
            for part in "abc":
                ly = LY["up2" + part]
                gated(ly, lambda t: cv[:, t, 2, :],
                      lambda it, t, ly=ly: (cv_step, (HID[ly.name] - HID["up2a"]) * 6 + it * 12 + 5 + t))
                if part == "c":
                    load_sqrt()
                residual(LY["dn2" + part], sums=part == "c")
            token_std("final2")

        @block.tensor
        def _(pe):
            def weights(ly, it, hf, j):
                k = ly.base + hf * ly.c + j
                pe.wait_ge(lo_done, k + 5 + it * ly.cpi)
                return k % RING if ly.loop else (k + it * ly.cpi) % RING

            def wide(ly, it, hf, xs, x_ready=None, width=HW):
                kk = CW // width
                last_k = ly.c * kk - 1
                for j in range(ly.c):
                    slot = weights(ly, it, hf, j)
                    for t in range(ly.tiles):
                        bank = (2 * hf + t) % 4
                        if j == 0:
                            pe.wait_ge(bank_free, ly.tbase + 2 * hf + t + 1 + it * ly.tpi)
                        both = ps[:, bank, :].rearrange("p (a n) -> p a n", a=2)
                        for k in range(kk):
                            kt = j * kk + k
                            if x_ready is not None and t == 0:
                                pe.wait_ge(*x_ready(kt))
                            w = slice(k * width + t * P, k * width + t * P + P)
                            pair, x_hi = xs(kt)
                            if kt == last_k:
                                pe.matmul(ps[:, bank, 0:NX], lo[:, slot, w], x_hi, start=False, stop=False)
                            ins = pe.matmul(both, hi[:, slot, w], pair, start=kt == 0, stop=kt == last_k)
                            if kt != last_k:
                                ins = pe.matmul(ps[:, bank, 0:NX], lo[:, slot, w], x_hi, start=False, stop=False)
                    ins.then_inc(chunk_used, 1)

            def triple(ly, it, hf, n, xs, x_ready=None, width=HW, first_bank=None):
                kk = CW // width
                last_k = ly.c * kk - 1
                for j in range(ly.c):
                    slot = weights(ly, it, hf, j)
                    for t in range(ly.tiles):
                        bank = (2 * hf + t) % 4 if first_bank is None else first_bank + t
                        if j == 0:
                            pe.wait_ge(bank_free, ly.tbase + 2 * hf + t + 1 + it * ly.tpi)
                        for k in range(kk):
                            kt = j * kk + k
                            if x_ready is not None and t == 0:
                                pe.wait_ge(*x_ready(kt))
                            w = slice(k * width + t * P, k * width + t * P + P)
                            x_hi, x_lo = xs(kt)
                            acc_ = ps[:, bank, 0:n]
                            if len(x_hi.shape) == 3:
                                acc_ = acc_.rearrange("p (a n) -> p a n", a=2)
                            pe.matmul(acc_, hi[:, slot, w], x_hi, start=kt == 0, stop=False)
                            pe.matmul(acc_, hi[:, slot, w], x_lo, start=False, stop=False)
                            ins = pe.matmul(acc_, lo[:, slot, w], x_hi, start=False, stop=kt == last_k)
                    ins.then_inc(chunk_used, 1)

            def by_token(ly, hf, xs, single=False, before_last=None):
                banks = range(4) if single else range(4 * (hf % 2), 4 * (hf % 2) + 4)
                if single:
                    pe.wait_ge(bank_free, ly.tbase + 4 * hf + 4)
                elif hf >= 2:
                    pe.wait_ge(bank_free, ly.tbase + 4 * (hf - 1) + 4)
                for j in range(ly.c):
                    if j == ly.c - 1 and before_last is not None:
                        before_last()
                    slot = weights(ly, 0, hf, j)
                    for t, bank in enumerate(banks):
                        for k in range(4):
                            kt = 4 * j + k
                            w = slice(k * HW, k * HW + HW)
                            x_hi, x_lo = xs(kt, t)
                            acc_ = ps[:, bank, 0:HW]
                            pe.matmul(acc_, x_hi, hi[:, slot, w], start=kt == 0, stop=False)
                            pe.matmul(acc_, x_lo, hi[:, slot, w], start=False, stop=False)
                            ins = pe.matmul(acc_, x_hi, lo[:, slot, w], start=False, stop=kt == 4 * ly.c - 1)
                    ins.then_inc(chunk_used, 1)

            def mod_group(ly, it):
                g = ly.gbase + it
                pe.wait_ge(accf_ready, g + 2)
                pe.wait_ge(mod_done, g + 1)
                for v in range(2 if ly.ctx else 1):
                    for t in range(ly.mtiles):
                        ins = pe.matmul(ps[:, 7, 4 * v + t:4 * v + t + 1], accf[:, v, t * P:t * P + P], col("one"),
                                        start=True, stop=True)
                ins.then_inc(mod_sum, 1)

            def token_stats(name, sums, bank=4, last=True):
                if NTH[name] >= 1:
                    pe.wait_ge(std_ready, NTH[name])
                for th, rows in token_tiles(name):
                    for i, x in enumerate(sums):
                        ins = pe.matmul(ps[0:rows, bank, th:th + 1], x[:, th * P:th * P + rows], mean[:, 0:1],
                                        start=i == 0, stop=i == len(sums) - 1)
                if last:
                    ins.then_inc(stat_ready, 1)

            def spread(name, bank, values=None):
                pe.wait_ge(inv_ready, NTH[name] + 1)
                for th, rows in token_tiles(name):
                    ins = pe.matmul(ps[:, bank, th * P:th * P + rows], (tok_inv(name) if values is None else values)[0:rows, th:th + 1].to_broadcast([rows, P]),
                                    ident[0:rows, 0:rows], start=True, stop=True)
                ins.then_inc(rstd_ready, 1)

            def residual_stats(ly, name, last=True):
                pe.wait_ge(sum_added, ADD0[ly] + LY[ly].its * LY[ly].halves + 4)
                token_stats(name, [ssum[:, 0, :]], last=last)

            pe.wait_ge(tables_in, 32)
            pe.wait_ge(sq_added, 4)
            token_stats("mix", [z[:, k, :] for k in range(2)])
            spread("mix", 5)

            def to_z(name, first_token, x_ready=None):
                ly = LY[name]

                def body(it):
                    for hf in range(ly.halves):
                        triple(ly, it, hf, N1 - first_token,
                               lambda kt: (xs1[:, kt, 0, first_token:N1], xs1[:, kt, 1, first_token:N1]),
                               x_ready if hf == 0 else None)
                    mod_group(ly, it)
                run(pe, ly, body)

            to_z("kv1", 0, lambda kt: (xs_ready, kt + 1))
            triple(LY["f1"], 0, 0, N1, lambda kt: (xs1[:, kt, 0, :], xs1[:, kt, 1, :]), width=P, first_bank=6)
            for g in range(2):
                pe.wait_ge(bank_free, 17 + 4 if g == 1 else 13 + 4)
                for kt in range(3):
                    rows = P if kt < 2 else N1 - 2 * P
                    bank = 4 + (3 * g + kt) % 2
                    if 3 * g + kt >= 2:
                        pe.wait_ge(vtok_ready, 3 * g + kt - 1)
                    for k in range(4):
                        ins = pe.transpose(ps[0:rows, bank, k * P:k * P + P],
                                           z[:, 8 + 4 * g + k, kt * P:kt * P + rows], ident)
                    ins.then_inc(vt_ready, 1)
            to_z("q1", NM - 2)

            pe.wait_ge(bank_free, LY["conv1"].tbase + 4)
            pe.wait_ge(vtok_ready, 6)
            pe.wait_ge(f_dve, 4)
            for qt in range(2):
                ins = pe.transpose(ps[:, 5, qt * HEADS:qt * HEADS + HEADS], fl[0:HEADS, 0, NM + qt * P:NM + qt * P + P],
                                   ident[0:HEADS, 0:HEADS])
            ins.then_inc(cq_psum, 1)

            def score_bank(hd, qt):
                return (4 if hd % 2 == 0 else 2) + qt

            def scores(hd):
                pick = ident[0:HEADS, hd:hd + 1]
                for qt in range(2):
                    q0 = NM + qt * P
                    if hd == 0:
                        pe.wait_ge(cq_ready, 1)
                    elif hd == 1:
                        pe.wait_ge(bank_free, LY["out1"].tbase + 4)
                    else:
                        pe.wait_ge(s_taken, 2 * (hd - 2) + qt + 1)
                    s = ps[:, score_bank(hd, qt), 0:N1]
                    pe.matmul(s, z[:, 16 + hd, q0:q0 + P], z[:, hd, :], start=True, stop=False)
                    pe.matmul(s, pick.to_broadcast([HEADS, P]), fl[0:HEADS, 2, :], start=False, stop=True)\
                      .then_inc(s_ready, 1)

            def transposed(hd):
                pe.wait_ge(p_ready, 2 * hd + 2)
                if hd == 0:
                    pe.wait_ge(mod_done, LY["att1"].gbase + 1)
                else:
                    pe.wait_ge(pt_ready, hd)
                for qt in range(2):
                    for kt in range(2):
                        pe.transpose(ps[:, 6, kt * NX + qt * P:kt * NX + qt * P + P],
                                     p1[:, hd % 2, qt, kt * P:kt * P + P], ident)
                    ins = pe.transpose(ps[0:NM, 7, qt * P:qt * P + P], p1[:, hd % 2, qt, 2 * P:N1], ident)
                ins.then_inc(pt_psum, 1)

            def mix(hd):
                pe.wait_ge(pt_ready, hd + 1)
                if hd >= 1:
                    pe.wait_ge(y_ready, hd)
                for kt in range(3):
                    rows = P if kt < 2 else N1 - 2 * P
                    ins = pe.matmul(ps[:, 0, 0:NX], vtok[0:rows, kt, hd * P:hd * P + P], pt1[0:rows, kt, :],
                                    start=kt == 0, stop=kt == 2)
                ins.then_inc(o_ready, 1)

            def group_stats(hd):
                pe.wait_ge(gn_sq, hd + 1)
                for a in range(2):
                    e0 = TABS["e31"][0] + 15 - (8 * a + hd)
                    ins = pe.matmul(ps[0:16, 1, 0:NX], tabs[:, e0:e0 + 16], gsq(hd)[:, a, :],
                                    start=hd == 0 and a == 0, stop=hd == HEADS - 1 and a == 1)
                ins.then_inc(gn_stat, 1)

            scores(0)
            to_z("conv1", NM - 2)
            scores(1)
            for hd in range(HEADS):
                transposed(hd)
                if hd + 2 < HEADS:
                    scores(hd + 2)
                mix(hd)
                if hd >= 1:
                    group_stats(hd - 1)
            group_stats(HEADS - 1)
            pe.wait_ge(gn_r, 1)
            pe.wait_ge(s_taken, 2 * HEADS)
            for g in range(16):
                if g >= 2:
                    pe.wait_ge(gn_y, g - 1)
                pe.matmul(ps[:, 2 + g % 2, 0:NX], ident[0:16, g:g + 1].to_broadcast([16, P]), rstd[0:16, 0:NX],
                          start=True, stop=True).then_inc(gn_bc, 1)

            def project(ly, xs, x_ready=None, mods=True):
                def body(it):
                    for hf in range(ly.halves):
                        wide(ly, it, hf, xs, x_ready if hf == 0 else None)
                    if ly.mod and mods:
                        mod_group(ly, it)
                run(pe, ly, body)

            def pair_of(x):
                return lambda kt: (x[:, kt, :, :], x[:, kt, 0, :])

            mod_group(LY["att1"], 0)
            pe.wait_ge(y_ready, HEADS)
            pe.wait_ge(gn_y, 16)
            ly = LY["out1"]

            def body(it, ly=ly):
                for hf in range(ly.halves):
                    triple(ly, it, hf, NX, lambda kt: (ys1[:, kt, 0, :], ys1[:, kt, 1, :]),
                           (lambda kt: (gn_ready, kt // 4 + 1)) if hf == 0 else None)
                mod_group(ly, it)
            run(pe, ly, body)
            residual_stats("out1", "ffn1")
            spread("ffn1", 5)

            def gated_part(tag, part, first_tile):
                project(LY["up" + tag + part], pair_of(hs), lambda kt: (xs_ready, first_tile + kt + 1))

            def down_part(tag, part):
                up = LY["up" + tag + part]
                if "dn" + tag + part in DIRECT:
                    ly = LY["dn" + tag + part]

                    def body(it):
                        for hf in range(ly.halves):
                            triple(ly, it, hf, NX, lambda kt: (hid[:, kt, 0, :], hid[:, kt, 1, :]),
                                   (lambda kt: (hid_ready, HID[up.name] + kt + 1)) if hf == 0 else None)
                    run(pe, ly, body)
                    return
                project(LY["dn" + tag + part], pair_of(hid), lambda kt: (hid_ready, HID[up.name] + kt + 1))

            for part in "abc":
                gated_part("1", part, SPLIT["ffn1"])
                if part == "b":
                    spread("ctx", 6)
                down_part("1", part)
                if part == "a":
                    pe.wait_ge(csq_added, 8 + 1)
                    token_stats("ctx", [csum[:, k, :] for k in range(2)])

            residual_stats("dn1c", "final1", last=False)
            for th in range(2):
                ins = pe.matmul(ps[:, 4, 2 + th:3 + th], gsum[:, 0, th * P:th * P + P], mean[:, 0:1], start=True, stop=True)
            ins.then_inc(stat_ready, 1)
            spread("final1", 5)
            pe.wait_ge(cxn_ready, 8)
            pe.wait_ge(gsum_step, 3)
            spread("attn2", 6, tok[:, 132:134])
            ly = LY["joint"]
            pe.wait_ge(bank_free, ly.tbase + 4)

            def both_of(kt):
                return hs2[:, :, kt, 0, :], hs2[:, :, kt, 1, :]

            def body(it, ly=ly):
                for hf in range(2):
                    triple(ly, it, hf, 2 * NX, both_of, lambda kt: (xs_ready, SPLIT["attn2"] + kt + 1))
                mod_group(ly, it)
            run(pe, ly, body)
            triple(LY["kr"], 0, 0, 2 * NX, both_of, width=P, first_bank=6)
            project(LY["xonly"], lambda kt: (hs2[:, 0, kt, :, :], hs2[:, 0, kt, 0, :]))
            pe.wait_ge(kvsq_ready, 1)
            token_stats("kv", [kvsq[:, k, :] for k in range(4)])
            pe.wait_ge(bank_free, LY["vn"].tbase + 4)

            def tokens_of(kt, t):
                x = hs2[:, t // 2, kt, :, (t % 2) * P:(t % 2) * P + P]
                return x[:, 0, :], x[:, 1, :]

            pe.wait_ge(mod_done, MOD_GROUPS + 1)

            def latent_norms():
                pe.wait_ge(qsq_ready, 1)
                token_stats("q", [sq[:, 1, k * NX:k * NX + NX] for k in range(4)], 7)
                spread("kv", 6)

            by_token(LY["vn"], 0, tokens_of, before_last=latent_norms)
            pe.wait_ge(std_ready, NTH["q"] + 1)
            pe.wait_ge(rstd_copied, 1)
            by_token(LY["vn"], 1, tokens_of)
            pe.wait_ge(bank_free, LY["vn"].tbase + 4 + 4)
            spread("q", 0)
            pe.wait_ge(late_in, 48)
            pe.wait_ge(bank_free, LY["uk"].tbase + 4)

            def attend(first, heads, score_terms, values, y0, between=None):
                local = between is not None

                def scores2(hd):
                    for qt in range(2):
                        u = 2 * (first + hd) + qt
                        if hd >= 2 or hd >= 1 and local:
                            pe.wait_ge(exp2_ready, u - 1 if local else u - 3)
                        terms = score_terms(hd, qt)
                        for i, (q, k) in enumerate(terms):
                            ins = pe.matmul(ps[:, score_bank2(hd, qt, local), :], q, k, start=i == 0, stop=i == len(terms) - 1)
                        ins.then_inc(s2_ready, 1)

                def transposed2(hd):
                    n = first + hd
                    pe.wait_ge(p2_ready, 2 * n + 2)
                    if n >= 1:
                        pe.wait_ge(pt2_ready, n)
                    for qt in range(2):
                        for kt in range(4):
                            ins = pe.transpose(ps[:, 6 + qt, kt * P:kt * P + P],
                                               p2[:, hd % 2, qt, kt * P:kt * P + P], ident)
                    ins.then_inc(pt2_psum, 1)

                def mix2(hd):
                    pe.wait_ge(pt2_ready, first + hd + 1)
                    if hd >= 2:
                        pe.wait_ge(y2_ready, y0 + hd - 1)
                    for kt in range(4):
                        ins = pe.matmul(ps[:, hd % 2, 0:NX], values[:, kt, hd * P:hd * P + P], pt2[:, kt, :],
                                        start=kt == 0, stop=kt == 3)
                    ins.then_inc(o2_ready, 1)

                scores2(0)
                if not local:
                    scores2(1)
                for hd in range(heads):
                    if local:
                        between(hd)
                    transposed2(hd)
                    ahead_by = 1 if local else 2
                    if hd + ahead_by < heads:
                        scores2(hd + ahead_by)
                    mix2(hd)

            def keys(hd):
                pe.wait_ge(bank_free, LY["uk"].tbase + 2 * hd + 4)
                triple(LY["uk"], 0, hd, 2 * NX, lambda kt: (ckvs[:, kt, 0, :], ckvs[:, kt, 1, :]),
                       lambda kt: (xs_ready, SPLIT["kv"] + kt + 1), first_bank=2)

            pe.wait_ge(rstd_copied, 2)
            attend(0, NA_HEADS, lambda hd, qt: [(zx[:, 4 + hd, qt * P:qt * P + P], zj[:, 4 + hd, :])], vn, 0, keys)

            def fourier_features(g):
                if g >= 1:
                    pe.wait_ge(fn_ab, g)
                for lt in range(2):
                    ins = pe.matmul(ps[:, 4 + lt, 0:2 * P], zx[:, 8 + g, lt * P:lt * P + P], tab("dft_c"),
                                    start=True, stop=True)
                ins.then_inc(fn_a, 1)

            def fourier_tokens(g):
                pe.wait_ge(fn_ab, g + 1)
                if g >= 1:
                    pe.wait_ge(fn_sp, g)
                n = 0
                for part, table in ((0, dft_lc), (1, dft_ls)):
                    for lt in range(2):
                        ins = pe.matmul(ps[:, 6, 0:NX], ab[:, g % 2, lt, part * P:part * P + P], table[:, lt, :],
                                        start=n == 0, stop=n == 3)
                        n += 1
                ins.then_inc(fn_b, 1)

            def fourier_out(g):
                pe.wait_ge(fn_sp, g + 1)
                if g >= 1:
                    pe.wait_ge(y2_ready, NA_HEADS + g)
                pe.matmul(ps[:, 7, 0:NX], wfn[:, g, :], sp[:, g % 2, :], start=True, stop=True).then_inc(fn_c, 1)

            fourier_features(0)
            for g in range(FN_GROUPS):
                if g == 0:
                    pe.wait_ge(y2_ready, NA_HEADS)
                by_token(LY["uv"], g, lambda kt, t: (ckvs[:, kt, 0, t * P:t * P + P], ckvs[:, kt, 1, t * P:t * P + P]),
                         single=True)
                if g >= 1:
                    fourier_out(g - 1)
                fourier_tokens(g)
                if g + 1 < FN_GROUPS:
                    fourier_features(g + 1)
            pe.wait_ge(bank_free, LY["uq"].tbase + 4)

            def queries(hf):
                wide(LY["uq"], 0, hf, pair_of(cqs), lambda kt: (xs_ready, SPLIT["q"] + kt + 1))

            queries(0)
            fourier_out(FN_GROUPS - 1)
            for hf in range(1, 3):
                queries(hf)
            pe.wait_ge(bank_free, LY["uq"].tbase + 4 + 4)
            pe.wait_ge(fn_sp, FN_GROUPS)
            for j in range(4):
                pe.matmul(ps[:, 4 + j // 2, (j % 2) * NX:(j % 2) * NX + NX], tab("swap"), qr_m[:, j, :],
                          start=True, stop=True)
            pe.matmul(ps[:, 6, 0:NX], tab("swap"), kr[:, 0:NX], start=True, stop=True).then_inc(rot_psum, 1)
            for hf in range(3, 6):
                queries(hf)
            pe.wait_ge(bank_free, LY["out2"].tbase + 4)
            pe.wait_ge(y2_ready, FN_GROUPS + NA_HEADS)
            pe.wait_ge(rope_ready, 6)
            attend(NA_HEADS, HEADS,
                   lambda hd, qt: [(qn_m[:, hd, qt * P:qt * P + P], kn_m[:, hd, :]),
                                   (qr_m[:, hd // 2, qt * P:qt * P + P], krm[:, hd % 2, :])],
                   vt_m, FN_GROUPS + NA_HEADS)
            pe.wait_ge(y2_ready, FN_GROUPS + NA_HEADS + HEADS)

            def mixed(kt):
                y = ysa[:, kt] if kt < 8 else ysb[:, kt - 8]
                return y[:, :, :], y[:, 0, :]

            project(LY["out2"], mixed)
            residual_stats("out2", "ffn2")
            spread("ffn2", 5)
            for part in "abc":
                gated_part("2", part, SPLIT["ffn2"])
                down_part("2", part)
            residual_stats("dn2c", "final2")
            spread("final2", 5)

        @block.vector
        def _(dve):
            def split_lo(v, slot):
                dve.wait_ge(hi_done, v + 1)
                dve.tensor_tensor(lo[:, slot, :], raw[:, slot, :], hi[:, slot, :].bitcast(F32), ALU.subtract)\
                   .then_inc(lo_done, 1)

            def mod_chunk(ly, it, m):
                n = ly.mbase + m + it * len(ly.mod_at)
                dve.wait_ge(wm_full[m % 2], 16 * ((ly.mbase + m) // 2 + 1 + it * (len(ly.mod_at) // 2)))
                width = 2 * HW if ly.ctx else HW
                for i in range(4):
                    k, v = (i // 2, i % 2) if ly.ctx else (i, 0)
                    kt = (2 if ly.ctx else 4) * m + k
                    w = wm[:, m % 2, k * width:k * width + width]
                    a = acc[:, i % 2, 0:width]
                    c = csilu[:, v * KT + kt:v * KT + kt + 1]
                    if m == 0 and i < 2:
                        dve.wait_ge(accf_ready, ly.gbase + 1 + it)
                        ins = dve.tensor_scalar(a, w, c, None, ALU.mult)
                    else:
                        if i == 1:
                            dve.wait_ge(wm_used, n + 2)
                        else:
                            dve.wait_ge(wm_op, 3 * n + (0 if i == 0 else i - 1))
                        ins = dve.scalar_tensor_tensor(a, w, c, a, ALU.mult, ALU.add)
                    ins.then_inc(wm_used if i == 3 else wm_op, 1)

            def mod_hand_over(ly, it):
                dve.wait_ge(mod_sum, ly.gbase + it + 1)
                dve.wait_ge(wm_used, ly.mbase + (it + 1) * 4 + 2)
                dve.tensor_tensor(accf[:, 0, 0:HW], acc[:, 0, 0:HW], acc[:, 1, 0:HW], ALU.add).then_inc(accf_ready, 1)

            def mod_take(ly, it):
                n, b0 = ly.mtiles, COLS["b_mod"][0]
                dve.wait_ge(mod_sum, ly.gbase + it + 2)
                bias = cols[:, bass.ds(it * n + ly.mtbase + b0, n)]
                if ly.ctx:
                    dve.tensor_tensor(modx[:, bass.ds(it * n + ly.mtbase, n)], ps[:, 7, 4:4 + n], bias, ALU.add)
                dve.tensor_tensor(mod[:, bass.ds(it * n + ly.mtbase, n)], ps[:, 7, 0:n], bias, ALU.add).then_inc(mod_done, 1)

            def prepare(ly, it, hf, first=0, last=None):
                for j in range(first, ly.c if last is None else last):
                    a = ahead(ly, it, hf, j)
                    if a is not None:
                        split_lo(a[0], a[1])
                    if hf * ly.c + j in ly.mod_at:
                        m = ly.mod_at.index(hf * ly.c + j)
                        mod_chunk(ly, it, m)
                        if m == 3 and not ly.ctx:
                            mod_hand_over(ly, it)

            def add_half(ly, it, hf, t, dst):
                bank = (2 * hf + t) % 4
                dve.wait_ge(tmp_ready, CONCAT[ly.name] + it * ly.tpi + 2 * hf + t + 1)
                dve.tensor_tensor(dst, ps[:, bank, 0:NX], tmp[:, bank, :], ALU.add).then_inc(bank_free, 1)

            def whole(ly, it, hf, t):
                return ly.tbase + it * ly.tpi + 2 * hf + t + 5

            def token_inv(name):
                dve.wait_ge(std_ready, NTH[name] + 1)
                for rows, c0, c1 in token_columns(name):
                    ins = dve.reciprocal(tok_inv(name)[0:rows, c0:c1], tok_std(name)[0:rows, c0:c1])
                ins.then_inc(inv_ready, 1)

            def norm_apply(name, rs, src, gain, dst_hi, dst_lo, shift=None, before=None, after=None):
                tiles, slots = NORMS[name][1], xn_slots(name)
                dve.wait_ge(rstd_ready, NTH[name] + 1)
                if SPLIT[name]:
                    dve.wait_ge(xs_ready, SPLIT[name])

                def rest(k):
                    dve.wait_ge(xs_hi, SPLIT[name] + k + 1)
                    if shift is None:
                        ins = dve.tensor_tensor(dst_lo(k), xn_tile(name, k), dst_hi(k).bitcast(F32), ALU.subtract)
                    else:
                        ins = dve.scalar_tensor_tensor(dst_lo(k), xn_tile(name, k), shift(k), dst_hi(k).bitcast(F32),
                                                       ALU.add, ALU.subtract)
                    ins.then_inc(xs_ready, 1)
                    if after is not None:
                        after(k)

                for k in range(tiles):
                    if before is not None:
                        before(k)
                    if k >= slots:
                        dve.wait_ge(xs_ready, SPLIT[name] + k - slots + 1)
                    dve.scalar_tensor_tensor(xn_tile(name, k), src(k), gain(k), rs, ALU.mult, ALU.mult).then_inc(xn_ready, 1)
                    if k >= 1:
                        rest(k - 1)
                rest(tiles - 1)

            dve.memset(att[:, 0, :], 0.0).then_inc(lo_done, RING)
            dve.memset(att[:, 1, :], 0.0).then_inc(chunk_used, RING)
            dve.memset(att[:, 2, :], 0.0).then_inc(bank_free, 4)
            dve.memset(mod[:, 0:1], 0.0).then_inc(wm_used, 2)
            dve.memset(mod[:, 1:2], 0.0).then_inc(mod_sum, 1)
            dve.memset(mod[:, 2:3], 0.0).then_inc(mod_done, 1)
            dve.memset(mod[:, 3:4], 0.0).then_inc(accf_ready, 1)
            dve.memset(mod[:, 4:5], 0.0).then_inc(sum_sq, 1)

            for b in range(1, 4):
                dve.wait_ge(sq_ready, b + 1)
                if b >= 2:
                    dve.wait_ge(sq_added, b - 1)
                dve.tensor_tensor(z[:, 0:4, :], z[:, 0:4, :], z[:, 4 * b:4 * b + 4, :], ALU.add).then_inc(sq_added, 1)
            dve.wait_ge(sq_added, 3)
            dve.tensor_tensor(z[:, 0:2, :], z[:, 0:2, :], z[:, 2:4, :], ALU.add).then_inc(sq_added, 1)
            split_lo(0, 0)
            token_inv("mix")
            split_lo(1, 1)
            dve.wait_ge(tables_in, 32)
            norm_apply("mix", ps[:, 5, 0:N1], lambda k: h[:, k, :], lambda k: col("norm_mix", k),
                       lambda k: xs1[:, k, 0, :], lambda k: xs1[:, k, 1, :],
                       after=lambda k: split_lo(2 + k // 4, 2 + k // 4) if k in (3, 7) else None)
            dve.wait_ge(silu_c_done, 1)

            def only_prepare(ly, after_second=None):
                def body(it):
                    for hf in range(ly.halves):
                        prepare(ly, it, hf)
                        if hf == 1 and after_second is not None:
                            after_second()
                    mod_take(ly, it)
                run(dve, ly, body)

            only_prepare(LY["kv1"])
            prepare(LY["f1"], 0, 0)
            dve.wait_ge(chunk_used, last_chunk(LY["f1"], 0, 0) + 5)
            dve.tensor_scalar(fl[0:HEADS, 0, :], ps[0:HEADS, 6, 0:N1],
                              cols[0:HEADS, COLS["b_f"][0]:COLS["b_f"][0] + 1], None, ALU.add).then_inc(bank_free, 1)
            def forget_gate():
                dve.wait_ge(f_act, 3)
                dve.wait_ge(bank_free, LY["q1"].tbase + 4)
                dve.scalar_tensor_tensor(fl[0:HEADS, 2, :], fl[0:HEADS, 0, :], 0.0, fl[0:HEADS, 1, :], ALU.min, ALU.subtract)\
                   .then_inc(f_dve, 1)
                dve.wait_ge(f_dve, 1)
                dve.memset(fl[0:HEADS, 1, :], 0.0).then_inc(f_dve, 1)
                dve.wait_ge(f_dve, 2)
                dve.tensor_tensor_scan(fl[0:HEADS, 0, :], fl[0:HEADS, 2, :], fl[0:HEADS, 1, :], 0.0, ALU.add, ALU.add)\
                   .then_inc(f_dve, 1)
                dve.wait_ge(f_dve, 3)
                dve.tensor_scalar(fl[0:HEADS, 2, :], fl[0:HEADS, 0, :], -1.0, None, ALU.mult).then_inc(f_dve, 1)

            only_prepare(LY["q1"], forget_gate)


            def conv_input(g):
                u = z[:, 32 + g, NM - 2:N1]
                dve.tensor_tensor(u, u, z[:, 40 + g, NM - 2:N1], ALU.mult).then_inc(conv_u, 1)

            def conv_group(g):
                dst = z[:, 40 + g, 0:NX]
                dve.wait_ge(conv_w0, g + 1)
                dve.scalar_tensor_tensor(dst, z[:, 32 + g, NM - 1:N1 - 1], col("conv1", 8 + g), dst, ALU.mult, ALU.add)\
                   .then_inc(conv_step, 1)
                if g + 1 < HEADS:
                    conv_input(g + 1)
                dve.wait_ge(conv_step, 2 * g + 1)
                dve.scalar_tensor_tensor(dst, z[:, 32 + g, NM:N1], col("conv1", 16 + g), dst, ALU.mult, ALU.add)\
                   .then_inc(conv_step, 1)
                dve.wait_ge(conv_step, 2 * g + 2)
                dve.tensor_tensor(z[:, 24 + g, NM:N1], dst, z[:, 24 + g, NM:N1], ALU.mult).then_inc(conv_ready, 1)

            dve.wait_ge(cq_psum, 1)
            dve.tensor_copy(cq[:, :, :], ps[:, 5, 0:2 * HEADS].rearrange("p (a n) -> p a n", a=2)).then_inc(cq_ready, 1)
            dve.wait_ge(cq_ready, 1)

            def masked(hd):
                for qt in range(2):
                    u = 2 * hd + qt
                    dve.wait_ge(s_ready, u + 1)
                    dve.scalar_tensor_tensor(p1[:, hd % 2, qt, :], ps[:, (4 if hd % 2 == 0 else 2) + qt, 0:N1],
                                             cq[:, qt, hd:hd + 1], causal[:, qt, :], ALU.add, ALU.add).then_inc(s_taken, 1)
                for qt in range(2):
                    u = 2 * hd + qt
                    dve.wait_ge(s_taken, u + 1)
                    dve.tensor_reduce(att[:, 0, u:u + 1], p1[:, hd % 2, qt, :], AX_X, ALU.max, negate=True)\
                       .then_inc(max_ready, 1)

            def inverse_sums(hd):
                for qt in range(2):
                    u = 2 * hd + qt
                    dve.wait_ge(exp_ready, u + 1)
                    dve.reciprocal(att[:, 2, u:u + 1], att[:, 1, u:u + 1]).then_inc(rsum_ready, 1)

            masked(0)
            inverse_sums(0)
            only_prepare(LY["conv1"])
            dve.wait_ge(bank_free, LY["out1"].tbase + 4)
            conv_input(0)
            for hd in range(HEADS):
                if hd + 1 < HEADS:
                    masked(hd + 1)
                conv_group(hd)
                if hd + 1 < HEADS:
                    inverse_sums(hd + 1)
                if 1 <= hd < HEADS - 1:
                    mod_chunk(LY["att1"], 0, hd - 1)
            for m in range(HEADS - 2, len(LY["att1"].mod_at)):
                mod_chunk(LY["att1"], 0, m)
            dve.wait_ge(gn_std, 1)
            dve.reciprocal(rstd[0:16, 0:NX], std[0:16, 0:NX]).then_inc(gn_r, 1)

            def gn_rest(b):
                dve.wait_ge(gn_hi, b + 1)
                dve.tensor_tensor(ys1[:, 4 * b:4 * b + 4, 1, :], xn[:, b % 2, 0:4 * NX].rearrange("p (k n) -> p k n", k=4),
                                  ys1[:, 4 * b:4 * b + 4, 0, :].bitcast(F32), ALU.subtract).then_inc(gn_ready, 1)

            for b in range(4):
                if b >= 2:
                    dve.wait_ge(gn_ready, b - 1)
                for k in range(4):
                    g = 4 * b + k
                    dve.wait_ge(gn_bc, g + 1)
                    dve.scalar_tensor_tensor(xn[:, b % 2, k * NX:k * NX + NX], z[:, 16 + g, NM:N1], col("out_gain", g),
                                             ps[:, 2 + g % 2, 0:NX], ALU.mult, ALU.mult).then_inc(gn_y, 1)
                    if b >= 1 and k == 1:
                        gn_rest(b - 1)
            gn_rest(3)
            mod_take(LY["att1"], 0)

            def residual(ly, gate=None, sums=False, gsums=False, before=None, after=None, finish=None, free=None):
                halves = ly.its * ly.halves

                def body(it):
                    for hf in range(ly.halves):
                        if before is not None:
                            before(it, hf)
                        prepare(ly, it, hf, 0, 1)
                        if after is not None:
                            after(it, hf)
                        if sums:
                            add_last(it * ly.halves + hf, (hf + 1) % 2)
                        prepare(ly, it, hf, 1, ly.c - 1)
                        if ly.name in DIRECT:
                            dve.wait_ge(chunk_used, last_chunk(ly, it, hf) + 5)
                            for t in range(2):
                                hk = h[:, bass.ds(it * ly.tpi + 2 * hf + t, 1), NM:N1].rearrange("p a n -> p (a n)")
                                dve.tensor_tensor(hk, ps[:, (2 * hf + t) % 4, 0:NX], hk, ALU.add).then_inc(bank_free, 1)
                            prepare(ly, it, hf, ly.c - 1)
                            continue
                        for t in range(2):
                            add_half(ly, it, hf, t, tmp[:, (2 * hf + t) % 4, :])
                        for t in range(2):
                            n = 2 * hf + t
                            hk = h[:, bass.ds(it * ly.tpi + n, 1), NM:N1].rearrange("p a n -> p (a n)")
                            dve.wait_ge(bank_free, whole(ly, it, hf, t))
                            if gate is None:
                                ins = dve.tensor_tensor(hk, tmp[:, n % 4, :], hk, ALU.add)
                            else:
                                ins = dve.scalar_tensor_tensor(hk, tmp[:, n % 4, :], mod[:, bass.ds(it * ly.tpi + gate + n, 1)],
                                                               hk, ALU.mult, ALU.add)
                            ins.then_inc(res_done, 1)
                        prepare(ly, it, hf, ly.c - 1)
                        if finish is not None:
                            finish(it, hf)
                    if ly.mod:
                        mod_take(ly, it)

                def add_last(n, slot):
                    dve.wait_ge(sum_sq, SUMS[ly.name] + n + 1)
                    dve.wait_ge(sum_added, ADD0[ly.name] + n + 1)
                    if gsums:
                        dve.tensor_tensor(gsum[:, :, :], gsum[:, :, :], gsqb[:, slot, :, :], ALU.add)
                    dve.tensor_tensor(ssum[:, :, :], ssum[:, :, :], sqb[:, slot, :, :], ALU.add).then_inc(sum_added, 1)

                if sums:
                    if free is not None:
                        dve.wait_ge(*free)
                    if gsums:
                        dve.memset(gsum[:, :, :], 0.0)
                        dve.memset(gsqb[:, 1, :, :], 0.0)
                    dve.memset(ssum[:, :, :], 0.0)
                    dve.memset(sqb[:, 1, :, :], 0.0).then_inc(sum_added, 1)
                run(dve, ly, body)
                if sums:
                    pairs = [(ssum, sqb)] + ([(gsum, gsqb)] if gsums else [])
                    for step in range(3):
                        dve.wait_ge(sum_added, ADD0[ly.name] + halves + 1 + step)
                        if step == 1:
                            dve.wait_ge(sum_sq, SUMS[ly.name] + halves + 1)
                        for total, part in pairs:
                            ins = dve.tensor_tensor(total[:, 0, :], total[:, 0, :],
                                                    total[:, 1, :] if step == 0 else part[:, 1, step - 1, :], ALU.add)
                        ins.then_inc(sum_added, 1)

            def hidden(ly, it, ready):
                for t in range(2):
                    s, v, value = ready(t)
                    dve.wait_ge(s, v)
                    dve.wait_ge(sg_ready, HID[ly.name] + it * 2 + t + 1)
                    dve.tensor_tensor(hv[:, t, :], value, sg[:, t, :], ALU.mult).then_inc(hv_ready, 1)

            def hidden_lo(ly, it):
                for t in range(2):
                    part = hid[:, bass.ds(it * 2 + t, 1), :, :].rearrange("p a b n -> p (a b) n")
                    dve.wait_ge(hid_hi, HID[ly.name] + it * 2 + t + 1)
                    dve.tensor_tensor(part[:, 1, :], hv[:, t, :], part[:, 0, :].bitcast(F32), ALU.subtract)\
                       .then_inc(hid_ready, 1)

            residual(LY["out1"], sums=True, free=(gn_ready, 4))
            token_inv("ffn1")
            norm_apply("ffn1", ps[:, 5, 0:NX], lambda k: hx[:, k, :], lambda k: col("norm_ffn", k),
                       lambda k: hs[:, k, 0, :], lambda k: hs[:, k, 1, :])

            def gated1(part, finish=None):
                ly = LY["up1" + part]

                def body(it):
                    prepare(ly, it, 0, 0, 3)
                    for t in range(2):
                        add_half(ly, it, 0, t, gt[:, t, :])
                    prepare(ly, it, 0, 3)
                    prepare(ly, it, 1, 0, 3)
                    for t in range(2):
                        add_half(ly, it, 1, t, ut[:, t, :])
                    hidden(ly, it, lambda t: (bank_free, whole(ly, it, 1, t), ut[:, t, :]))
                    prepare(ly, it, 1, 3)
                    hidden_lo(ly, it)
                    if finish is not None:
                        finish(it)
                    mod_take(ly, it)
                run(dve, ly, body)

            dve.memset(csum[:, :, :], 0.0).then_inc(csq_added, 1)

            def add_ctx(it):
                dve.wait_ge(csq_added, it + 1)
                dve.wait_ge(csq_ready, it + 1)
                dve.tensor_tensor(csum[:, :, :], csum[:, :, :], csq[:, :, :], ALU.add).then_inc(csq_added, 1)

            gated1("a", add_ctx)
            residual(LY["dn1a"])
            token_inv("ctx")
            gated1("b")
            dve.scalar_tensor_tensor(gm[:, 1, :], modx[:, KT:2 * KT], 1.0, col("g_attn", 0, KT), ALU.add, ALU.mult)\
               .then_inc(gm_done, 1)
            dve.scalar_tensor_tensor(gm[:, 0, :], mod[:, KT:2 * KT], 1.0, col("g_attn", 0, KT), ALU.add, ALU.mult)\
               .then_inc(gm_done, 1)
            dve.wait_ge(gm_done, 2)
            dve.tensor_tensor(gm[:, 0, :], gm[:, 0, :], col("final_norm", 0, KT), ALU.mult).then_inc(gm_done, 1)
            dve.wait_ge(rstd_ready, NTH["ctx"] + 1)

            def one(x, n):
                return x[:, bass.ds(n, 1), :].rearrange("p a n -> p (a n)")

            def ctx_scale(it, hf):
                for t in range(2):
                    n = it * LY["dn1b"].tpi + 2 * hf + t
                    ins = dve.scalar_tensor_tensor(one(cx, n), one(cx, n), gm[:, 1, bass.ds(n, 1)], ps[:, 6, 0:NX],
                                                   ALU.mult, ALU.mult)
                ins.then_inc(cxn_ready, 1)

            residual(LY["dn1b"], before=ctx_scale)
            gated1("c")
            dve.wait_ge(mod_done, LY["joint"].gbase + 1)
            dve.scalar_tensor_tensor(gm[:, 2, :], mod[:, 4 * KT:5 * KT], 1.0, col("g_ffn", 0, KT), ALU.add, ALU.mult)\
               .then_inc(gm_done, 1)

            def ctx_lo(it, hf):
                dve.wait_ge(cx_hi, it * LY["dn1c"].halves + hf + 1)
                for t in range(2):
                    n = it * LY["dn1c"].tpi + 2 * hf + t
                    part = hs2[:, 1, bass.ds(n, 1), :, :].rearrange("p a b n -> p (a b) n")
                    ins = dve.scalar_tensor_tensor(part[:, 1, :], one(cx, n), modx[:, bass.ds(n, 1)], part[:, 0, :].bitcast(F32),
                                                   ALU.add, ALU.subtract)
                ins.then_inc(cx_done, 1)

            residual(LY["dn1c"], sums=True, gsums=True, after=ctx_lo)
            token_inv("final1")
            dve.wait_ge(inv_ready, NTH["final1"] + 1)
            dve.scalar_tensor_tensor(tok[:, 128:130], ps[:, 4, 2:4], 1.0 / KT, tok_inv("final1")[:, 0:2], ALU.mult, ALU.mult)\
               .then_inc(gsum_step, 1)
            dve.wait_ge(gsum_step, 1)
            dve.tensor_tensor(tok[:, 130:132], tok[:, 128:130], tok_inv("final1")[:, 0:2], ALU.mult).then_inc(gsum_step, 1)
            token_inv("attn2")
            dve.wait_ge(inv_ready, NTH["attn2"] + 1)
            dve.tensor_tensor(tok[:, 132:134], tok_inv("final1")[:, 0:2], tok_inv("attn2")[:, 0:2], ALU.mult)\
               .then_inc(gsum_step, 1)
            dve.wait_ge(gm_done, 4)
            norm_apply("attn2", ps[:, 6, 0:NX], lambda k: hx[:, k, :], lambda k: gm[:, 0, k:k + 1],
                       lambda k: hs2[:, 0, k, 0, :], lambda k: hs2[:, 0, k, 1, :], shift=lambda k: mod[:, k:k + 1])
            for k in range(KT):
                dve.scalar_tensor_tensor(hx[:, k, :], hx[:, k, :], col("final_norm", k), ps[:, 5, 0:NX], ALU.mult, ALU.mult)\
                   .then_inc(x_final, 1)

            def straight(ly, dst, n):
                def body(it):
                    for hf in range(ly.halves):
                        prepare(ly, it, hf, 0, ly.c - 1)
                        dve.wait_ge(chunk_used, last_chunk(ly, it, hf) + 5)
                        for t in range(ly.tiles):
                            bank = 4 * (hf % 2) + t if ly.tiles == 4 else 6 if ly.name == "kr" else (2 * hf + t) % 4
                            dve.tensor_copy(dst(it, hf, t), ps[:, bank, 0:n]).then_inc(bank_free, 1)
                        prepare(ly, it, hf, ly.c - 1)
                        if ly.name == "vn" and hf == 0:
                            token_inv("q")
                    if ly.mod:
                        mod_take(ly, it)
                run(dve, ly, body)

            def summed(ly, dst):
                def body(it):
                    for hf in range(ly.halves):
                        prepare(ly, it, hf)
                        for t in range(2):
                            add_half(ly, it, hf, t, dst(it, hf, t))
                run(dve, ly, body)

            straight(LY["joint"], lambda it, hf, t: zj[:, bass.ds(it * 4 + 2 * hf + t, 1), :].rearrange("p a n -> p (a n)"),
                     2 * NX)
            straight(LY["kr"], lambda it, hf, t: kr[:, :], 2 * NX)
            summed(LY["xonly"], lambda it, hf, t: zx[:, bass.ds(it * 4 + 2 * hf + t, 1), :].rearrange("p a n -> p (a n)"))
            dve.wait_ge(late_in, 48)
            window = tab("na_mask").rearrange("p (a n) -> p a n", a=1).to_broadcast([P, 32, 64])
            flat = na[:, :, :, :].rearrange("p h q (a n) -> p (h q a) n", n=64)
            dve.tensor_tensor(flat, flat, window, ALU.add).then_inc(na_bias_ready, 1)
            token_inv("kv")
            straight(LY["vn"], lambda it, hf, t: vn[:, t, hf * HW:hf * HW + HW], HW)

            def attend(first, heads, scale, local, y0, between=None):
                def peaks(hd):
                    for qt in range(2):
                        u = 2 * (first + hd) + qt
                        dve.wait_ge(s2_ready, u + 1)
                        if local:
                            dve.wait_ge(s2_half, u + 1)
                            dve.scalar_tensor_tensor(p2[:, hd % 2, qt, 0:NX], ps[:, score_bank2(hd, qt, local), 0:NX], scale,
                                                     na[:, hd, qt, :], ALU.mult, ALU.add).then_inc(s2_bias, 1)
                        else:
                            dve.tensor_reduce(att[:, 2, u % 16:u % 16 + 1], ps[:, score_bank2(hd, qt, local), :], AX_X, ALU.max,
                                              negate=True).then_inc(max2_ready, 1)
                    for qt in range(2):
                        u = 2 * (first + hd) + qt
                        if local:
                            dve.wait_ge(s2_bias, u + 1)
                            dve.tensor_reduce(att[:, 0, u % 16:u % 16 + 1], p2[:, hd % 2, qt, :], AX_X, ALU.max, negate=True)\
                               .then_inc(nmax2_ready, 1)
                        else:
                            dve.wait_ge(max2_ready, 2 * hd + qt + 1)
                            dve.tensor_scalar(att[:, 0, u % 16:u % 16 + 1], att[:, 2, u % 16:u % 16 + 1], scale, None, ALU.mult)\
                               .then_inc(nmax2_ready, 1)

                def normalised2(hd):
                    for qt in range(2):
                        u = 2 * (first + hd) + qt
                        dve.wait_ge(exp2_ready, u + 1)
                        dve.reciprocal(att[:, 2, u % 16:u % 16 + 1], att[:, 1, u % 16:u % 16 + 1]).then_inc(rsum2_ready, 1)
                    for qt in range(2):
                        u = 2 * (first + hd) + qt
                        dve.wait_ge(rsum2_ready, u + 1)
                        dve.tensor_scalar(p2[:, hd % 2, qt, :], p2[:, hd % 2, qt, :], att[:, 2, u % 16:u % 16 + 1], None, ALU.mult)\
                           .then_inc(p2_ready, 1)

                def rest(hd):
                    y = ysb[:, hd] if local else ysa[:, hd]
                    dve.wait_ge(y2_hi, y0 + hd + 1)
                    dve.tensor_tensor(y[:, 1, :], ps[:, hd % 2, 0:NX], y[:, 0, :].bitcast(F32), ALU.subtract)\
                       .then_inc(y2_ready, 1)

                peaks(0)
                for hd in range(heads):
                    if hd + 1 < heads and between is None:
                        peaks(hd + 1)
                    if hd >= 1 and between is not None:
                        peaks(hd)
                    normalised2(hd)
                    if between is not None:
                        between(hd)
                    if hd >= 1:
                        rest(hd - 1)
                rest(heads - 1)

            dve.wait_ge(rstd_copied, 2)
            norm_apply("kv", rstd[:, :], lambda k: zj[:, k, :], lambda k: col("g_kv", k),
                       lambda k: ckvs[:, k, 0, :], lambda k: ckvs[:, k, 1, :])
            dve.wait_ge(na_bias_ready, 1)
            dve.wait_ge(xs_ready, SPLIT["kv"] + 4)

            def keys(hd):
                prepare(LY["uk"], 0, hd)
                dve.wait_ge(chunk_used, last_chunk(LY["uk"], 0, hd) + 5)
                for t in range(2):
                    dve.tensor_copy(kn_m[:, 2 * hd + t, :], ps[:, 2 + t, :]).then_inc(bank_free, 1)

            attend(0, NA_HEADS, NA_SCALE, True, 0, keys)
            dve.wait_ge(pt2_psum, NA_HEADS)
            norm_apply("q", rstd_q, lambda k: zx[:, k, :], lambda k: col("g_q", k),
                       lambda k: cqs[:, k, 0, :], lambda k: cqs[:, k, 1, :])

            def fourier_y(g):
                dve.wait_ge(y2_hi, NA_HEADS + g + 1)
                dve.tensor_tensor(ysb[:, 4 + g, 1, :], ps[:, 7, 0:NX], ysb[:, 4 + g, 0, :].bitcast(F32), ALU.subtract)\
                   .then_inc(y2_ready, 1)

            for g in range(FN_GROUPS):
                prepare(LY["uv"], 0, g)
                dve.wait_ge(chunk_used, last_chunk(LY["uv"], 0, g) + 5)
                for t in range(4):
                    dve.tensor_copy(vt_m[:, t, g * HW:g * HW + HW], ps[:, t, 0:HW]).then_inc(bank_free, 1)
                if g >= 1:
                    fourier_y(g - 1)
                dve.wait_ge(fn_b, g + 1)
                if g >= 2:
                    dve.wait_ge(fn_c, g - 1)
                dve.tensor_copy(sp[:, g % 2, :], ps[:, 6, 0:NX]).then_inc(fn_sp, 1)
            dve.wait_ge(bank_free, LY["uq"].tbase + 4)
            dve.memset(krm[:, :, :], 0.0).then_inc(krm_zero, 1)
            for hf in range(3):
                prepare(LY["uq"], 0, hf)
                for t in range(2):
                    add_half(LY["uq"], 0, hf, t, qr_m[:, 2 * hf + t, :] if hf < 2 else qn_m[:, 2 * hf - 4 + t, :])
                if hf == 0:
                    fourier_y(FN_GROUPS - 1)
            dve.wait_ge(rot_psum, 1)
            dve.wait_ge(bank_free, LY["uq"].tbase + 4 + 4)
            cos = tab("cos")
            sin = tab("sin")
            cos4 = cos.rearrange("p (a n) -> p a n", a=1).to_broadcast([P, 4, NX])
            sin2 = sin.rearrange("p (a n) -> p a n", a=1).to_broadcast([P, 2, NX])
            dve.tensor_tensor(rot[:, 0, :, :], qr_m[:, :, :], cos4, ALU.mult).then_inc(rot_step, 1)
            for j in range(2):
                dve.tensor_tensor(rot[:, 1, 2 * j:2 * j + 2, :], ps[:, 4 + j, :].rearrange("p (a n) -> p a n", a=2), sin2,
                                  ALU.mult).then_inc(rot_step, 1)
            dve.wait_ge(rot_step, 3)
            dve.tensor_tensor(qr_m[:, :, :], rot[:, 0, :, :], rot[:, 1, :, :], ALU.add).then_inc(rope_ready, 1)
            dve.wait_ge(rope_ready, 1)
            dve.tensor_tensor(rot[:, 0, 0, :], kr[:, 0:NX], cos, ALU.mult).then_inc(rot_step, 1)
            dve.tensor_tensor(rot[:, 1, 0, :], ps[:, 6, 0:NX], sin, ALU.mult).then_inc(rot_step, 1)
            dve.wait_ge(rot_step, 5)
            dve.wait_ge(krm_zero, 1)
            for half, rows in ((0, slice(0, 64)), (1, slice(64, 128))):
                dve.tensor_tensor(krm[rows, half, 0:NX], rot[rows, 0, 0, :], rot[rows, 1, 0, :], ALU.add).then_inc(rope_ready, 1)
                dve.tensor_copy(krm[rows, half, NX:2 * NX], kr[rows, NX:2 * NX]).then_inc(rope_ready, 1)
            dve.wait_ge(rope_ready, 5)
            dve.memset(att[:, 1, :], 0.0).then_inc(rope_ready, 1)
            for hf in range(3, 6):
                prepare(LY["uq"], 0, hf)
                for t in range(2):
                    add_half(LY["uq"], 0, hf, t, qn_m[:, 2 * hf - 4 + t, :])
            attend(NA_HEADS, HEADS, MLA_SCALE, False, FN_GROUPS + NA_HEADS)

            residual(LY["out2"], gate=2 * KT, sums=True, free=(y2_ready, FN_GROUPS + NA_HEADS + HEADS))
            dve.memset(pad[:, :, 0:1], 0.0).then_inc(pads_zero, 1)
            dve.memset(pad[:, :, NX + 1:NX + 2], 0.0).then_inc(pads_zero, 1)
            token_inv("ffn2")
            norm_apply("ffn2", ps[:, 5, 0:NX], lambda k: hx[:, k, :], lambda k: gm[:, 2, k:k + 1],
                       lambda k: hs[:, k, 0, :], lambda k: hs[:, k, 1, :],
                       shift=lambda k: mod[:, 3 * KT + k:3 * KT + k + 1])
            dve.wait_ge(pads_zero, 2)
            for part in "abc":
                ly = LY["up2" + part]

                def body(it, ly=ly):
                    tile0 = (HID[ly.name] - HID["up2a"])
                    step0 = tile0 * 6
                    for hf in range(2):
                        prepare(ly, it, hf, 0, 3)
                        for t in range(2):
                            add_half(ly, it, hf, t, pad[:, t, 1:NX + 1])
                        for step in range(3):
                            for t in range(2):
                                c = tile0 + hf * FT + t
                                n = step0 + it * 12 + hf * 6 + 2 * step + t
                                if step == 0:
                                    dve.wait_ge(bank_free, whole(ly, it, hf, t))
                                    ins = dve.tensor_scalar(cv[:, t, 0, :], pad[:, t, 1:NX + 1], dcol("conv2_w1", it * 2 + c),
                                                            dcol("conv2_b", it * 2 + c), ALU.mult, ALU.add)
                                elif step == 1:
                                    dve.wait_ge(cv_step, n - 1)
                                    ins = dve.scalar_tensor_tensor(cv[:, t, 1, :], pad[:, t, 0:NX], dcol("conv2_w0", it * 2 + c),
                                                                   cv[:, t, 0, :], ALU.mult, ALU.add)
                                else:
                                    dve.wait_ge(cv_step, n - 1)
                                    if hf == 1:
                                        dve.wait_ge(sg_ready, HID[ly.name] + it * 2 + t + 1)
                                    ins = dve.scalar_tensor_tensor(cv[:, t, 2, :], pad[:, t, 2:NX + 2], dcol("conv2_w2", it * 2 + c),
                                                                   cv[:, t, 1, :], ALU.mult, ALU.add)
                                ins.then_inc(cv_step, 1)
                        if hf == 1:
                            hidden(ly, it, lambda t: (cv_step, step0 + it * 12 + 6 + 4 + t + 1, cv[:, t, 2, :]))
                        prepare(ly, it, hf, 3)
                    hidden_lo(ly, it)
                run(dve, ly, body)
                residual(LY["dn2" + part], gate=5 * KT, sums=part == "c")
            token_inv("final2")
            dve.wait_ge(rstd_ready, NTH["final2"] + 1)
            for k in range(KT):
                dve.scalar_tensor_tensor(hx[:, k, :], hx[:, k, :], col("g_final", k), ps[:, 5, 0:NX], ALU.mult, ALU.mult)\
                   .then_inc(x_final, 1)


def tables():
    t = {"ident": np.eye(P), "mean": np.full((P, P), 1 / P)}
    key = np.arange(N1)[None, :]
    row = np.arange(P)[:, None]
    t["causal"] = np.concatenate([np.where(key <= NM + qt * P + row, 0.0, NEG) for qt in range(2)], 1)
    d = np.arange(P) % 64
    partner = np.arange(P) + np.where(d % 32 < 16, 16, -16)
    swap = np.zeros((P, P))
    swap[partner, np.arange(P)] = 1.0
    t["swap"] = swap
    freqs = np.float32(10000.0) ** (-np.arange(16, dtype=np.float32) / np.float32(16))
    pos = np.arange(NX)
    where = np.where(d[:, None] < 32, pos[None, :] // 64, pos[None, :] % 64).astype(np.float32)
    angle = (where * freqs[d % 16][:, None].astype(np.float32)).astype(np.float64)
    t["cos"] = np.cos(angle)
    t["sin"] = np.sin(angle) * np.where(d % 32 < 16, -1.0, 1.0)[:, None]
    ca = 2 * np.pi * (np.outer(np.arange(P), np.arange(P)) % P) / P
    t["dft_c"] = np.concatenate([np.cos(ca), np.sin(ca)], 1)
    la = 2 * np.pi * (np.outer(np.arange(NX), np.arange(NX)) % NX) / NX
    norm = (NX * P) ** -0.5
    for name, m in (("dft_l_cos", np.cos(la) * norm), ("dft_l_sin", -np.sin(la) * norm)):
        t[name] = m.reshape(2, P, NX).transpose(1, 0, 2).reshape(P, 2 * NX)
    w = (np.arange(P) % 64)[:, None]
    first = np.clip(w - 8, 0, 48)
    c = np.arange(64)[None, :]
    t["na_mask"] = np.where((c >= first) & (c < first + 16), 0.0, NEG)
    e = np.zeros((P, 31))
    e[:, 15] = 1 / P
    t["e31"] = e
    names = list(TABS)
    return tuple(np.concatenate([t[n] for n in part], 1).astype(np.float32) for part in (names[:4], names[4:]))


def kernel(**inputs):
    import concourse.bacc as bacc
    from concourse.bass_utils import run_bass_kernel_spmd

    a = {k: np.asarray(v) for k, v in inputs.items()}

    def chunks(w, per=4):
        k, n = w.shape
        width = CW // per
        w = w.reshape(k // (per * P), per, P, n // width, width)
        return w.transpose(3, 0, 2, 1, 4).reshape(-1, P, CW)

    def halves(first, second):
        f, s = chunks(first), chunks(second)
        per = first.shape[0] // (4 * P)
        f, s = f.reshape(-1, per, P, CW), s.reshape(-1, per, P, CW)
        return np.stack([f, s], 1).reshape(-1, P, CW)

    def feed_forward(gate, value, down):
        out = []
        for f0, f1 in ((0, 2048), (2048, 4096), (4096, F)):
            out += [halves(gate[:, f0:f1], value[:, f0:f1]), chunks(down[f0:f1])]
        return out

    w_in, w_in2 = a["w_in"][0], a["w_in_2"][0]
    o = np.cumsum([0, 512, 512, 64, 512, 512, 512, 512])
    cq, ckv, kr, qn, kn, vn, fn = (w_in2[:, o[i]:o[i + 1]] for i in range(7))
    uq = a["w_uq_2"][0].reshape(512, HEADS, 192)
    ukv = a["w_ukv_2"][0].reshape(512, HEADS, 2, P)
    up2 = a["w_up_2"][0]
    w_f = np.zeros((D, P), np.float32)
    w_f[:, :HEADS] = w_in[:, 6144:]
    stream = np.concatenate(
        [chunks(w_in[:, 1024:3072]), chunks(w_f, per=8), chunks(w_in[:, :1024]), chunks(w_in[:, 3072:6144]), chunks(a["w_out"][0])]
        + feed_forward(a["w_gate"][0], a["w_up"][0], a["w_down"][0])
        + [chunks(ckv), chunks(kn), chunks(np.concatenate([kr, kr], 1), per=8), chunks(cq), chunks(qn), chunks(fn),
           chunks(vn), chunks(ukv[:, :, 0].reshape(512, 1024)), chunks(ukv[:, :, 1].reshape(512, 1024)),
           chunks(uq[:, :, P:].reshape(512, 512)), chunks(uq[:, :, :P].reshape(512, 1024)), chunks(a["w_out_2"][0])]
        + feed_forward(up2[:, :F], up2[:, F:], a["w_down_2"][0]))
    assert len(stream) == N_CHUNKS

    def features(x):
        return x.T.reshape(-1, P, x.shape[0]).transpose(1, 0, 2)

    def columns(v):
        return v.reshape(-1, P).T

    conv_w2 = a["conv_w_2"][0]
    b_f = np.zeros((P, 1), np.float32)
    b_f[:HEADS, 0] = a["b_f"][0]
    vectors = {"norm_mix": a["norm_mix"], "out_gain": a["out_gain"], "norm_ffn": a["norm_ffn"],
               "final_norm": a["final_norm"], "g_attn": a["g_attn_2"], "g_ffn": a["g_ffn_2"], "g_final": a["g_final_2"],
               "g_q": a["g_q_2"], "g_kv": a["g_kv_2"], "c": a["c_2"], "c_ctx": a["c_ctx_2"], "b_mod": a["b_mod_2"],
               "conv1": a["conv_w"], "conv2_w0": conv_w2[0], "conv2_w1": conv_w2[1], "conv2_w2": conv_w2[2],
               "conv2_b": a["conv_b_2"]}
    packed = [columns(vectors[n]) if n in vectors else b_f if n == "b_f" else np.full((P, 1), {"eps": EPS, "one": 1.0, "scratch": 0.0}[n], np.float32)
              for n in COLS]
    rpb = a["na_rpb_2"][0]
    padded = np.zeros((NA_HEADS, 15, 127), np.float32)
    padded[:, :, 48:79] = rpb
    toeplitz = np.stack([padded[:, :, 63 - w:127 - w] for w in range(64)], 2)
    bias = np.stack([toeplitz[:, 7 - r:11 - r] for r in range(4)], 1)
    na_bias = bias.reshape(NA_HEADS, 2, 2, 4, 64, 64).transpose(2, 4, 0, 1, 3, 5).reshape(P, NA_HEADS, 2, NX)

    arrays = {
        "tokens": features(np.concatenate([a["meta"], a["x"][0]], 0)),
        "ctx_tokens": features(a["ctx_2"][0]),
        "cols": np.concatenate(packed, 1),
        "tables1": tables()[0],
        "tables2": tables()[1],
        "stream": stream,
        "mod_stream": np.concatenate([chunks(a["w_mod_2"][0][:, :CTX_TILES * P], per=2),
                                      chunks(a["w_mod_2"][0][:, CTX_TILES * P:])]),
        "na_bias": na_bias,
        "w_fnet": a["w_fnet_2"][0].transpose(1, 0, 2),
    }
    nc = bacc.Bacc("TRN2", target_bir_lowering=False, num_devices=1)
    args = []
    for name in arrays:
        arrays[name] = np.ascontiguousarray(arrays[name])
        args.append(nc.dram_tensor("in_" + name, arrays[name].shape, F32, kind="ExternalInput").ap())
    args.append(nc.dram_tensor("out_tokens", (P, KT, NX), F32, kind="ExternalOutput").ap())
    build(nc, *args)
    r = run_bass_kernel_spmd(nc, [{"in_" + k: v for k, v in arrays.items()}], core_ids=[0])
    got = r.results[0]["out_tokens"]
    return np.ascontiguousarray(got.transpose(2, 1, 0)).reshape(1, NX, D)
```
